# Optimizing a Trainium2 kernel written in Bass

```python
import math
import jax
import jax.numpy as jnp
from jax import lax
import numpy as np

D_MODEL = 1024
BATCH = 1
SEQ = 256
DEPTH = 1

CHUNK = 64
DN_HEADS = 4
DN_DK = 128
DN_DV = 128
CONV_K = 4
SB_HEADS = 8
SB_DH = 64
SB_BLOCK = 128
N_EXPERTS = 16
N_GROUPS = 4
EXPERTS_PER_GROUP = N_EXPERTS // N_GROUPS
TOP_K = 2
D_FF_EXPERT = 512

LN_EPS = 1e-5
RMS_EPS = 1e-6
DEEPNORM_ALPHA = (2 * DEPTH) ** 0.25
DEEPNORM_BETA = (8 * DEPTH) ** -0.25

DN_WIDTH = DN_HEADS * DN_DK
DN_VWIDTH = DN_HEADS * DN_DV
SB_WIDTH = SB_HEADS * SB_DH
IN_WIDTHS = (DN_WIDTH, DN_WIDTH, DN_VWIDTH, DN_VWIDTH, DN_HEADS, DN_HEADS,
             SB_WIDTH, SB_WIDTH, SB_WIDTH, D_MODEL, D_MODEL)
D_IN = sum(IN_WIDTHS)

kernel_name = 'hybrid_deltanet_stickbreaking_grouped_moe'

def layer_norm(x, g, b):
    xf = x.astype(jnp.float32)
    mu = jnp.mean(xf, axis=-1, keepdims=True)
    var = jnp.mean(jnp.square(xf - mu), axis=-1, keepdims=True)
    return ((xf - mu) * lax.rsqrt(var + LN_EPS) * g + b).astype(x.dtype)

def l2norm(x):
    return x * lax.rsqrt(jnp.sum(x * x, axis=-1, keepdims=True) + RMS_EPS)

def causal_depthwise_conv(x, w):
    s = x.shape[1]
    xp = jnp.pad(x, ((0, 0), (CONV_K - 1, 0), (0, 0)))
    return sum(xp[:, i:i + s] * w[i] for i in range(CONV_K))

def gated_delta_rule(q, k, v, beta, g):
    b_, s_, h_, dk = q.shape
    dv = v.shape[-1]
    n = s_ // CHUNK

    def chunks(t):
        return jnp.swapaxes(t.reshape(b_, n, CHUNK, h_, *t.shape[3:]), 2, 3)

    q, k, v, beta, g = chunks(q), chunks(k), chunks(v), chunks(beta), chunks(g)
    g = jnp.cumsum(g, axis=-1)
    tri = jnp.tril(jnp.ones((CHUNK, CHUNK), bool))
    strict = jnp.tril(jnp.ones((CHUNK, CHUNK), bool), -1)
    gdiff = g[..., :, None] - g[..., None, :]
    decay = jnp.where(tri, jnp.exp(jnp.where(tri, gdiff, 0.0)), 0.0)
    kb = k * beta[..., None]
    lmat = jnp.where(strict, jnp.einsum('bnhcd,bnhed->bnhce', kb, k) * decay, 0.0)
    eye = jnp.eye(CHUNK, dtype=jnp.float32)
    tinv = lax.linalg.triangular_solve(eye + lmat, jnp.broadcast_to(eye, lmat.shape),
                                       left_side=True, lower=True, unit_diagonal=True)
    w = jnp.einsum('bnhce,bnhed->bnhcd', tinv, kb * jnp.exp(g)[..., None])
    u = jnp.einsum('bnhce,bnhed->bnhcd', tinv, v * beta[..., None])
    qk = jnp.where(tri, jnp.einsum('bnhcd,bnhed->bnhce', q, k) * decay, 0.0)
    qg = q * jnp.exp(g)[..., None]
    g_last = g[..., -1]
    kdec = k * jnp.exp(g_last[..., None] - g)[..., None]

    def step(state, inp):
        w_i, u_i, qk_i, qg_i, kdec_i, gl_i = inp
        v_new = u_i - jnp.einsum('bhcd,bhde->bhce', w_i, state)
        o = jnp.einsum('bhcd,bhde->bhce', qg_i, state) + jnp.einsum('bhce,bhed->bhcd', qk_i, v_new)
        state = state * jnp.exp(gl_i)[..., None, None] + jnp.einsum('bhcd,bhce->bhde', kdec_i, v_new)
        return state, o

    xs = tuple(jnp.moveaxis(t, 1, 0) for t in (w, u, qk, qg, kdec, g_last))
    s0 = jnp.zeros((b_, h_, dk, dv), jnp.float32)
    _, o = lax.scan(step, s0, xs)
    return o.transpose(1, 0, 3, 2, 4).reshape(b_, s_, h_, dv)

def deltanet_branch(q, k, v, z, b, a, conv_w, a_log, dt_bias, norm_w):
    bsz, s_, _ = q.shape
    f32 = jnp.float32
    qkv = jax.nn.silu(causal_depthwise_conv(jnp.concatenate([q, k, v], axis=-1), conv_w))
    q, k, v = jnp.split(qkv.astype(f32), [DN_WIDTH, 2 * DN_WIDTH], axis=-1)
    q = l2norm(q.reshape(bsz, s_, DN_HEADS, DN_DK)) * (DN_DK ** -0.5)
    k = l2norm(k.reshape(bsz, s_, DN_HEADS, DN_DK))
    v = v.reshape(bsz, s_, DN_HEADS, DN_DV)
    beta = jax.nn.sigmoid(b.astype(f32))
    g = -jnp.exp(a_log.astype(f32)) * jax.nn.softplus(a.astype(f32) + dt_bias.astype(f32))
    o = gated_delta_rule(q, k, v, beta, g)
    o = o * lax.rsqrt(jnp.mean(o * o, axis=-1, keepdims=True) + RMS_EPS) * norm_w.astype(f32)
    o = o * jax.nn.silu(z.astype(f32).reshape(bsz, s_, DN_HEADS, DN_DV))
    return o.reshape(bsz, s_, DN_VWIDTH).astype(z.dtype)

def stick_breaking_attention(q, k, v):
    bsz, s_, _ = q.shape
    f32 = jnp.float32
    nb = s_ // SB_BLOCK
    qb = q.astype(f32).reshape(bsz, nb, SB_BLOCK, SB_HEADS, SB_DH).transpose(1, 0, 3, 2, 4) * (SB_DH ** -0.5)
    kh = k.astype(f32).reshape(bsz, s_, SB_HEADS, SB_DH).transpose(0, 2, 1, 3)
    vh = v.astype(f32).reshape(bsz, s_, SB_HEADS, SB_DH).transpose(0, 2, 1, 3)
    key_pos = jnp.arange(s_, dtype=jnp.int32)

    def block(args):
        qblk, q0 = args
        zs = jnp.einsum('bhqd,bhkd->bhqk', qblk, kh)
        strict = key_pos[None, :] < (q0 + jnp.arange(SB_BLOCK, dtype=jnp.int32))[:, None]
        log_keep = jnp.where(strict, jax.nn.log_sigmoid(-zs), 0.0)
        between = lax.cumsum(log_keep, axis=3, reverse=True) - log_keep
        att = jnp.where(strict, jnp.exp(jax.nn.log_sigmoid(zs) + between), 0.0)
        return jnp.einsum('bhqk,bhkd->bhqd', att, vh)

    starts = jnp.arange(nb, dtype=jnp.int32) * SB_BLOCK
    o = lax.map(block, (qb, starts))
    return o.transpose(1, 0, 3, 2, 4).reshape(bsz, s_, SB_WIDTH).astype(q.dtype)

def shared_grouped_router(x, w_router, router_bias):
    f32 = jnp.float32
    aff = jax.nn.sigmoid(jnp.einsum('bsd,de->bse', x, w_router).astype(f32))
    sel = aff + router_bias.astype(f32)
    bsz, s_, _ = aff.shape
    group_score = jnp.sum(lax.top_k(sel.reshape(bsz, s_, N_GROUPS, EXPERTS_PER_GROUP), TOP_K)[0], axis=-1)
    group = jnp.argmax(group_score, axis=-1)
    expert_group = jnp.arange(N_EXPERTS, dtype=jnp.int32) // EXPERTS_PER_GROUP
    masked = jnp.where(expert_group[None, None, :] == group[..., None], sel, -jnp.inf)
    _, idx = lax.top_k(masked, TOP_K)
    wsel = jnp.take_along_axis(aff, idx, axis=-1)
    wsel = wsel / jnp.sum(wsel, axis=-1, keepdims=True)
    return jnp.einsum('bsk,bske->bse', wsel, jax.nn.one_hot(idx, N_EXPERTS, dtype=f32))

def moe_ffn(x, combine, w_gate, w_up, w_down):
    h = jax.nn.silu(jnp.einsum('bsd,edf->bsef', x, w_gate)) * jnp.einsum('bsd,edf->bsef', x, w_up)
    h = h * combine[..., None].astype(h.dtype)
    return jnp.einsum('bsef,efd->bsd', h, w_down)

def setup_inputs(seed: int = 0) -> dict:
    key = jax.random.key(seed)
    ks = jax.random.split(key, 20)
    f32 = jnp.float32

    def nrm(k, shape, scale):
        return jax.random.normal(k, shape, f32) * scale

    conv_ch = 2 * DN_WIDTH + DN_VWIDTH
    dt = jnp.exp(jax.random.uniform(ks[4], (DEPTH, DN_HEADS), f32, math.log(1e-3), math.log(1e-1)))
    return {
        'x': nrm(ks[0], (BATCH, SEQ, D_MODEL), 1.0),
        'w_in': nrm(ks[1], (DEPTH, D_MODEL, D_IN), D_MODEL ** -0.5),
        'conv_w': nrm(ks[2], (DEPTH, CONV_K, conv_ch), CONV_K ** -0.5),
        'dn_a_log': jnp.log(jax.random.uniform(ks[3], (DEPTH, DN_HEADS), f32, 1.0, 16.0)),
        'dn_dt_bias': dt + jnp.log(-jnp.expm1(-dt)),
        'dn_norm_w': 1.0 + nrm(ks[5], (DEPTH, DN_DV), 0.02),
        'p_a': nrm(ks[6], (DEPTH, DN_VWIDTH, D_MODEL), DN_VWIDTH ** -0.5),
        'p_b': nrm(ks[7], (DEPTH, SB_WIDTH, D_MODEL), SB_WIDTH ** -0.5),
        'w_out': nrm(ks[8], (DEPTH, D_MODEL, D_MODEL), DEEPNORM_BETA * D_MODEL ** -0.5),
        'ln1_g': 1.0 + nrm(ks[9], (DEPTH, D_MODEL), 0.02),
        'ln1_b': nrm(ks[10], (DEPTH, D_MODEL), 0.02),
        'w_router': nrm(ks[11], (D_MODEL, N_EXPERTS), D_MODEL ** -0.5),
        'router_bias': nrm(ks[12], (N_EXPERTS,), 0.01),
        'w_gate': nrm(ks[13], (DEPTH, N_EXPERTS, D_MODEL, D_FF_EXPERT), D_MODEL ** -0.5),
        'w_up': nrm(ks[14], (DEPTH, N_EXPERTS, D_MODEL, D_FF_EXPERT), D_MODEL ** -0.5),
        'w_down': nrm(ks[15], (DEPTH, N_EXPERTS, D_FF_EXPERT, D_MODEL), DEEPNORM_BETA * D_FF_EXPERT ** -0.5),
        'ln2_g': 1.0 + nrm(ks[16], (DEPTH, D_MODEL), 0.02),
        'ln2_b': nrm(ks[17], (DEPTH, D_MODEL), 0.02),
    }

def reference(x, w_in, conv_w, dn_a_log, dn_dt_bias, dn_norm_w, p_a, p_b, w_out,
              ln1_g, ln1_b, w_router, router_bias, w_gate, w_up, w_down, ln2_g, ln2_b):
    split_points = np.cumsum(IN_WIDTHS)[:-1].tolist()
    for l in range(DEPTH):
        proj = jnp.einsum('bsd,de->bse', x, w_in[l])
        (dq, dk_, dv_, dz, db, da, sq, sk, sv, gate_a, gate_b) = jnp.split(proj, split_points, axis=-1)
        o_a = deltanet_branch(dq, dk_, dv_, dz, db, da, conv_w[l], dn_a_log[l], dn_dt_bias[l], dn_norm_w[l])
        o_b = stick_breaking_attention(sq, sk, sv)
        merged = (jax.nn.sigmoid(gate_a) * jnp.einsum('bsc,cd->bsd', o_a, p_a[l])
                  + jax.nn.sigmoid(gate_b) * jnp.einsum('bsc,cd->bsd', o_b, p_b[l]))
        mix = jnp.einsum('bsd,de->bse', merged, w_out[l])
        x = layer_norm(DEEPNORM_ALPHA * x + mix, ln1_g[l], ln1_b[l])
        combine = shared_grouped_router(x, w_router, router_bias)
        ffn = moe_ffn(x, combine, w_gate[l], w_up[l], w_down[l])
        x = layer_norm(DEEPNORM_ALPHA * x + ffn, ln2_g[l], ln2_b[l])
    return x


_drawn_inputs = setup_inputs


def setup_inputs(seed=0):
    import zlib

    import numpy as np

    out = dict(_drawn_inputs(seed))
    spreads = {}
    factors = {'dn_norm_w': 4.445, 'ln2_g': 2.859, 'ln2_b': 2.874}
    for name, (base, spread) in spreads.items():
        noise = np.random.default_rng([zlib.crc32(name.encode()), seed]).standard_normal(out[name].shape)
        drawn = base * np.exp(spread * noise) if base else spread * noise
        out[name] = jnp.asarray(drawn.astype(out[name].dtype))
    for name, factor in factors.items():
        out[name] = (out[name] * factor).astype(out[name].dtype)
    return out
```

```python
from contextlib import ExitStack

import concourse.bass as bass
from concourse import mybir
import numpy as np

F32 = mybir.dt.float32
I32 = mybir.dt.int32
ALU = mybir.AluOpType
ACT = mybir.ActivationFunctionType
AX_X = mybir.AxisListType.X

P = 128
D = 1024
KD = D // P
S = 256
TT = S // P
H = 4
U = TT * H
SH, DH = 8, 64
NE, NG, EPG = 16, 4, 4
F = 512
KF = F // P
CONV_K = 4
DELTA_W = H * P
LN_EPS, RMS_EPS = 1e-5, 1e-6
ALPHA = 2.0 ** 0.25
NPASS_MAX = NG + 1
MASKED = -1e30

SLOT = 4096
NSLOT = 6
PRE_LOADS = 15
PASS_LOADS = 3 * EPG
W_IN_BLOCKS = [0, 512, 1024, 2056, 2568, 3080, 1536, 3592, 4104, 4616, 5128]
BA_COL = 2048

C_IDENT, C_TRIU, C_TRIL, C_SUP, C_ONES, C_NEG, C_IOTA, C_LEV1 = (P * i for i in range(8))
C_LEV = C_LEV1 + P
C_JLT = C_LEV + 7 * P
C_SMALL = C_JLT + 16
NCONST = C_SMALL + 16


def constant_table():
    p = np.arange(P)[:, None]
    f = np.arange(P)[None, :]
    t = np.zeros((P, NCONST), np.float32)
    t[:, C_IDENT:C_IDENT + P] = p == f
    t[:, C_TRIU:C_TRIU + P] = p <= f
    t[:, C_TRIL:C_TRIL + P] = p >= f
    t[:, C_SUP:C_SUP + P] = p < f
    t[:, C_ONES:C_ONES + P] = 1.0
    t[:, C_NEG:C_NEG + P] = np.where(p < f, 0.0, MASKED)
    t[:, C_IOTA:C_IOTA + P] = f
    t[:, C_LEV1:C_LEV1 + P] = -((p // 2 == f // 2) & (p % 2 == 1) & (f % 2 == 0)).astype(np.float32)
    for n in range(7):
        s = 1 << n
        at = C_LEV + n * P
        m = (p // (2 * s) == f // (2 * s)) & ((f // s) % 2 == 1) & ((p // s) % 2 == 0)
        t[:, at:at + P] = -m.astype(np.float32) if n == 0 else m
    ij = np.arange(16)
    t[:, C_JLT:C_JLT + 16] = (ij % 4 < ij // 4)
    t[:, C_SMALL] = RMS_EPS
    t[:, C_SMALL + 1] = -0.5
    t[:, C_SMALL + 2] = -0.5
    t[:, C_SMALL + 3:C_SMALL + 16] = -0.5
    return t


class Steps:

    def __init__(self, eng, sem):
        self.eng, self.sem, self.n = eng, sem, 0

    def then(self, ins):
        self.n += 1
        ins.then_inc(self.sem, 1)
        self.eng.wait_ge(self.sem, self.n)


def hybrid_moe_block(nc, consts, x, w_in, conv_w, dn_a_log, dn_dt_bias, dn_norm_w, p_a, p_b, w_out,
                     ln1_g, ln1_b, w_router, router_bias, w_gate, w_up, w_down, ln2_g, ln2_b, out):
    ctx = ExitStack()
    with ctx:
        def sb(name, shape, dt=F32):
            return ctx.enter_context(nc.sbuf_tensor(name, shape, dt))

        def sem(name):
            return ctx.enter_context(nc.semaphore(name))

        ring = sb("ring", [P, NSLOT, SLOT])
        cst = sb("cst", [P, NCONST])
        xres = sb("xres", [P, TT, D])
        xT = sb("xT", [P, KD, S])
        qkvT = sb("qkvT", [P, 3 * H, S])
        raw = sb("raw", [P, 2, H, S + 4])
        zg = sb("zg", [P, TT, DELTA_W])
        sqT = sb("sqT", [P, 4, S])
        skT = sb("skT", [P, 4, S])
        sv = sb("sv", [P, TT, SH * DH])
        gates = sb("gates", [P, 2 * KD, S])
        buf_lt = sb("buf_lt", [P, U * P])
        buf_t = sb("buf_t", [P, U * P])
        buf_u = sb("buf_u", [P, U * P])
        buf_y = sb("buf_y", [P, U * P])
        buf_c = sb("buf_c", [P, U * P])
        buf_qk = sb("buf_qk", [P, U * P])
        stick = sb("stick", [P, 3, 2, 384])
        wba = sb("wba", [P, KD, 8])
        small = sb("small", [P, 512])
        small_i = sb("small_i", [P, 8], I32)

        def c(at, n=P):
            return cst[:, at:at + n]

        ident, triu, tril, sup, ones, neg, iota = (
            c(x_) for x_ in (C_IDENT, C_TRIU, C_TRIL, C_SUP, C_ONES, C_NEG, C_IOTA))

        def units(t):
            return t[:, :].rearrange("p (u c) -> p u c", c=P)

        raw_flat = raw[:, :, :, :].rearrange("p b h s -> p (b h s)")
        LT, T, UT, Y, CM, QKT = (units(b) for b in (buf_lt, buf_t, buf_u, buf_y, buf_c, buf_qk))
        L = raw_flat[:, 0:U * P].rearrange("p (u c) -> p u c", c=P)
        DEC = raw_flat[:, U * P:2 * U * P].rearrange("p (u c) -> p u c", c=P)
        VB = L
        KDEC = DEC[:, 0:H]
        U0 = DEC[:, H:U]
        S1 = T[:, 0:H]
        R1 = T[:, H:U]
        QS = Y[:, 0:H]
        VN = Y[:, H:U]
        O = CM
        ON = LT
        oaT = qkvT[:, 2 * H:3 * H, :]
        obT = sqT
        merged = gates[:, 0:KD, :]
        lnp = qkvT[:, 0:8, :].rearrange("p a s -> p (a s)").rearrange("p (w d) -> p w d", w=2)
        r2 = [buf_lt[:, :], buf_t[:, :]]
        xg = buf_u[:, :].rearrange("p (k s) -> p k s", s=P)
        silu_g = buf_qk[:, :].rearrange("p (b f) -> p b f", b=2)
        hid = buf_y[:, :].rearrange("p (b f) -> p b f", b=2)
        hidT = buf_c[:, :].rearrange("p (b k s) -> p b k s", b=2, s=P)
        ysb = raw_flat[:, 0:D]
        gflat = gates[:, :, :].rearrange("p a s -> p (a s)")
        SEL = gflat[:, 0:6 * S].rearrange("p (n t s) -> p n t s", n=6, t=TT)
        SELT = gflat[:, 6 * S:11 * S].rearrange("p (n s) -> p n s", n=5)
        selt_cur = gflat[:, 11 * S:12 * S]
        wr = gflat[:, 12 * S:12 * S + KD * NE].rearrange("p (k e) -> p k e", e=NE)

        at = [0]

        def cols(n):
            a = small[:, at[0]:at[0] + n]
            at[0] += n
            return a

        ba, gg, gb1, gb2, beta = cols(16), cols(U), cols(U), cols(U), cols(U)
        alog, dtb, nalog = cols(H), cols(H), cols(H)
        gcum, glast, expg, kdc, nbg = cols(U), cols(U), cols(U), cols(U), cols(U)
        ssq, rms = cols(U), cols(U)
        convw = cols(CONV_K * 3 * H)
        normw = cols(1)
        stats, mv, rstd = cols(4 * 6), cols(4), cols(2)
        aff, selv, top2 = cols(32), cols(32), cols(32)
        gscore, gsel, rank = cols(8), cols(8), cols(8)
        comb, wsum = cols(32), cols(2)
        sel5, rank5 = cols(TT * 5), cols(TT * 5)
        cg = cols(5 * EPG)
        comb5 = cols(TT * 5 * EPG)
        rbias = cols(NE)
        cnt, ovf = cols(4), cols(4)
        cgcur = cols(EPG)
        spare = buf_y[:, :]

        psum = ctx.enter_context(nc.psum_tensor("psum", [P, 8, 512], F32))
        bank = [psum[:, i, :] for i in range(8)]

        x_in, cst_in, small_in, late_in, ln2_in = (sem(n) for n in (
            "x_in", "cst_in", "small_in", "late_in", "ln2_in"))
        wr_in = sem("wr_in")
        slot_in = [sem(f"slot_in{i}") for i in range(NSLOT)]
        slot_free = [sem(f"slot_free{i}") for i in range(NSLOT)]
        xt_psum, xt_act, xt_dve = sem("xt_psum"), sem("xt_act"), sem("xt_dve")
        cw_psum, cw_sb, pads = sem("cw_psum"), sem("cw_sb"), sem("pads")
        proj_psum, proj_sb = sem("proj_psum"), sem("proj_sb")
        conv_done, silu_done, sq_done = sem("conv_done"), sem("silu_done"), sem("sq_done")
        ss_psum, rn_done, qk_norm = sem("ss_psum"), sem("rn_done"), sem("qk_norm")
        gb_pre, gb_exp, g_sb = sem("gb_pre"), sem("gb_exp"), sem("g_sb")
        gc_psum, gc_sb, dif_sb, dec_exp, eg_done = (sem(n) for n in (
            "gc_psum", "gc_sb", "dif_sb", "dec_exp", "eg_done"))
        kk_psum, lq_sb, lt_psum, lt_sb, qkt_sb = (sem(n) for n in (
            "kk_psum", "lq_sb", "lt_psum", "lt_sb", "qkt_sb"))
        lev_mask, lev_y, lev_ysb, lev_p, lev_tu = (sem(n) for n in (
            "lev_mask", "lev_y", "lev_ysb", "lev_p", "lev_tu"))
        vk_psum, vb_sb = sem("vk_psum"), sem("vb_sb")
        u0_psum, u0_sb, s1_psum, s1_sb, ks_psum, r1_sb, qs_sb = (sem(n) for n in (
            "u0_psum", "u0_sb", "s1_psum", "s1_sb", "ks_psum", "r1_sb", "qs_sb"))
        vn_psum, vn_sb, o_psum, o_sb, osq_sb, rms_in, rms_done, on_sb, z_sig = (sem(n) for n in (
            "vn_psum", "vn_sb", "o_psum", "o_sb", "osq_sb", "rms_in", "rms_done", "on_sb", "z_sig"))
        oat_psum, oat_sb = sem("oat_psum"), sem("oat_sb")
        sz_psum, sz_dve, sz_act, s_e, s_sp, cs_psum, s_t, s_att, av_psum, ob_sb = (sem(n) for n in (
            "sz_psum", "sz_dve", "sz_act", "s_e", "s_sp", "cs_psum", "s_t", "s_att", "av_psum", "ob_sb"))
        gate_sig, mg_psum, mg_sb, mix_psum, mix_sb = (sem(n) for n in (
            "gate_sig", "mg_psum", "mg_sb", "mix_psum", "mix_sb"))
        var1, rstd1, x1_sb, x1t_psum, x1t_sb = (sem(n) for n in (
            "var1", "rstd1", "x1_sb", "x1t_psum", "x1t_sb"))
        lg_psum, aff_sb, r2_init, gsel_sb, rank_psum, selv_sb = (sem(n) for n in (
            "lg_psum", "aff_sb", "r2_init", "gsel_sb", "rank_psum", "selv_sb"))
        npass_sb, sel_sb, selt_psum, selt_sb = (sem(n) for n in ("npass_sb", "sel_sb", "selt_psum", "selt_sb"))
        xg_psum, xg_sb, cur_sb, cg_sb = sem("xg_psum"), sem("xg_sb"), sem("cur_sb"), sem("cg_sb")
        gu_psum, silu_sb, hid_sb, ht_psum, ht_sb, y_psum, y_sb, sc_psum, sc_done = (sem(n) for n in (
            "gu_psum", "silu_sb", "hid_sb", "ht_psum", "ht_sb", "y_psum", "y_sb", "sc_psum", "sc_done"))
        var2, rstd2, out_sb, out_done = sem("var2"), sem("rstd2"), sem("out_sb"), sem("out_done")
        dve_steps, act_steps, pool_steps = sem("dve_steps"), sem("act_steps"), sem("pool_steps")

        x_d = x.rearrange("b (t p) d -> (b t) p d", p=P)
        out_d = out.rearrange("b (t p) d -> (b t) p d", p=P)
        win_d = w_in.rearrange("l (k p) n -> (l p) k n", p=P)
        pa_d = p_a.rearrange("l (k p) n -> (l p) k n", p=P)
        pb_d = p_b.rearrange("l (k p) n -> (l p) k n", p=P)
        wout_d = w_out.rearrange("l (k p) n -> (l p) k n", p=P)
        gate_d = w_gate.rearrange("l e (p k) f -> (l e) p (k f)", k=KD)
        up_d = w_up.rearrange("l e (p k) f -> (l e) p (k f)", k=KD)
        down_d = w_down.rearrange("l e (p k) d -> (l e) p (k d)", k=KF)

        def slot8(n):
            return ring[:, n % NSLOT, :].rearrange("p (k n) -> p k n", k=KD)

        def slot4(n):
            return ring[:, n % NSLOT, :].rearrange("p (k n) -> p k n", k=KF)

        def loads_of_slot(n):
            return n // NSLOT + 1

        UNITS = [(i // 2, "qkv", i) for i in range(6)] + [(None, "ba", 0)]
        UNITS += [(3, "sq", 0), (3, "sq", 1), (4, "sk", 0), (4, "sk", 1), (5, "sv", 0), (5, "sv", 1),
                  (6, "z", 0), (6, "z", 1)]
        UNITS += [(7 + i // 2, "gate", i) for i in range(8)]
        N_UNITS = len(UNITS)
        GATE0 = N_UNITS - 8
        MIX0 = N_UNITS

        block = ctx.enter_context(nc.Block())

        @block.sync
        def _(sp):
            for t in range(TT):
                sp.dma_start(xres[:, t, :], x_d[t]).then_inc(x_in, 16)

            def free(n):
                if n >= NSLOT:
                    sp.wait_ge(slot_free[n % NSLOT], loads_of_slot(n) - 1)

            for n in range(PRE_LOADS):
                free(n)
                if n < 11:
                    a = W_IN_BLOCKS[n]
                    dst, src = slot8(n), win_d[:, :, a:a + 512]
                elif n < 13:
                    dst, src = slot4(n), (pa_d if n == 11 else pb_d)
                else:
                    dst, src = slot4(n), wout_d[:, 4 * (n - 13):4 * (n - 13) + 4, :]
                sp.dma_start(dst, src).then_inc(slot_in[n % NSLOT], 16)

            def pass_loads(i, group):
                for j in range(EPG):
                    for w, src in enumerate((gate_d, up_d, down_d)):
                        n = PRE_LOADS + 3 * j + w
                        sp.wait_ge(slot_free[n % NSLOT], 2 * i + (loads_of_slot(n) - 1))
                        sp.dma_start(ring[:, n % NSLOT, :],
                                     src[bass.ds(group * EPG + j, 1)].rearrange("e p n -> (e p) n")
                                     ).then_inc(slot_in[n % NSLOT], 16)

            with sp.Fori(0, NG - 1) as i:
                pass_loads(i, i)
            sp.wait_ge(npass_sb, 1)
            npass = sp.value_load(small_i[0:1, 0:1], min_val=NG, max_val=NPASS_MAX)
            with sp.Fori(NG - 1, npass) as i:
                group = sp.value_load(small_i[0:1, bass.ds(i, 1)], min_val=0, max_val=NG - 1)
                pass_loads(i, group)
            for t in range(TT):
                sp.wait_ge(out_sb, t + 1)
                sp.dma_start(out_d[t], r2[t]).then_inc(out_done, 16)
            sp.wait_ge(out_done, 16 * TT)

        @block.tensor
        def _(pe):
            mm, tr = nc.tensor.matmul, nc.tensor.transpose

            def arrived(n):
                pe.wait_ge(slot_in[n % NSLOT], 16 * loads_of_slot(n))

            pe.wait_ge(cst_in, 16)
            pe.wait_ge(x_in, 16 * TT)
            for t in range(TT):
                for half in range(2):
                    for k in range(4):
                        kt = 4 * half + k
                        last = tr(bank[2 * t + half][:, k * P:(k + 1) * P], xres[:, t, kt * P:(kt + 1) * P], ident)
                    last.then_inc(xt_psum, 1)
            pe.wait_ge(small_in, 16 * 5)
            nrow = CONV_K * 3 * H
            tr(bank[4][:, 0:nrow], buf_y[0:nrow, 0:P], cst[0:nrow, C_IDENT:C_IDENT + nrow]).then_inc(cw_psum, 1)
            pe.wait_ge(xt_act, 2)
            pe.wait_ge(xt_dve, 2)

            def unit(u):
                n, kind, i = UNITS[u]
                b = bank[u % 4]
                if n is not None:
                    arrived(n)
                if u >= 4:
                    pe.wait_ge(proj_sb, u - 3)
                if kind in ("qkv", "sq", "sk", "gate"):
                    w = slot8(n)
                    for half in range(2):
                        a = ((2 * i + half) % 4) * P
                        for k in range(KD):
                            last = mm(b[:, half * S:(half + 1) * S], w[:, k, a:a + P], xT[:, k, :],
                                      start=(k == 0), stop=(k == KD - 1))
                elif kind == "ba":
                    for t in range(TT):
                        for k in range(KD):
                            last = mm(b[:, t * 8:t * 8 + 8], xT[:, k, t * P:(t + 1) * P], wba[:, k, :],
                                      start=(k == 0), stop=(k == KD - 1))
                else:
                    w = slot8(n)
                    for k in range(KD):
                        last = mm(b[:, :], xT[:, k, i * P:(i + 1) * P], w[:, k, :],
                                  start=(k == 0), stop=(k == KD - 1))
                last.then_inc(proj_psum, 1)
                if n is not None and (u + 1 == N_UNITS or UNITS[u + 1][0] != n):
                    pe.wait_ge(proj_psum, u + 1)
                    pe.sem_inc(slot_free[n % NSLOT], 1)

            for u in range(7):
                unit(u)
            for i in range(4):
                if i % 2 == 0:
                    pe.wait_ge(sq_done, i // 2 + 1)
                src = (buf_y if i < 2 else buf_c)[:, (i % 2) * 512:(i % 2) * 512 + 512]
                if i == 0:
                    pe.wait_ge(cw_sb, 1)
                mm(bank[4 + i][:, :], ones, src, start=True, stop=True).then_inc(ss_psum, 1)
            unit(7)
            unit(8)
            pe.wait_ge(g_sb, 1)
            pe.wait_ge(rn_done, 1)
            mm(bank[4][:, 0:U], triu, gg, start=True, stop=True)
            mm(bank[4][:, U:2 * U], ones, gg, start=True, stop=True).then_inc(gc_psum, 1)
            for u in range(U):
                last = mm(bank[5 + u // 4][:, (u % 4) * P:(u % 4 + 1) * P], LT[:, u, :], triu, start=True, stop=True)
            last.then_inc(gc_psum, 1)
            unit(9)
            unit(10)
            pe.wait_ge(qk_norm, 1)
            pe.wait_ge(gc_sb, 1)
            pe.wait_ge(dif_sb, 1)

            def head_tile(kind, u):
                t, h = u // H, u % H
                return qkvT[:, kind * H + h, t * P:(t + 1) * P]

            kkb, qkb = [bank[7], bank[4]], [bank[5], bank[6]]
            for u in range(U):
                last = mm(kkb[u // 4][:, (u % 4) * P:(u % 4 + 1) * P], head_tile(1, u), head_tile(1, u),
                          start=True, stop=True)
            last.then_inc(kk_psum, 1)
            for u in range(U):
                last = mm(qkb[u // 4][:, (u % 4) * P:(u % 4 + 1) * P], head_tile(0, u), head_tile(1, u),
                          start=True, stop=True)
            last.then_inc(kk_psum, 1)
            unit(11)
            unit(12)
            pe.wait_ge(lq_sb, 1)
            for u in range(U):
                last = tr(kkb[u // 4][:, (u % 4) * P:(u % 4 + 1) * P], L[:, u, :], ident)
            last.then_inc(lt_psum, 1)
            pe.wait_ge(lq_sb, 2)
            for u in range(U):
                last = tr(qkb[u // 4][:, (u % 4) * P:(u % 4 + 1) * P], QKT[:, u, :], ident)
            last.then_inc(lt_psum, 1)
            unit(13)
            unit(14)
            filler = [GATE0]

            def fill():
                if filler[0] < N_UNITS:
                    unit(filler[0])
                    filler[0] += 1

            for n in range(1, 7):
                for half in range(2):
                    a, b_ = bank[4 + 2 * half], bank[5 + 2 * half]
                    if n == 1 and half == 0:
                        pe.wait_ge(lt_sb, 1)
                        pe.wait_ge(qkt_sb, 1)
                    pe.wait_ge(lev_mask, n)
                    pe.wait_ge(lev_tu, 2 * (n - 1) + half + 1)
                    for j in range(4):
                        u = 4 * half + j
                        last = mm(a[:, j * P:(j + 1) * P], CM[:, u, :], T[:, u, :], start=True, stop=True)
                    last.then_inc(lev_y, 1)
                if n <= 6:
                    fill()
                for half in range(2):
                    a, b_ = bank[4 + 2 * half], bank[5 + 2 * half]
                    pe.wait_ge(lev_ysb, 2 * (n - 1) + half + 1)
                    for j in range(4):
                        u = 4 * half + j
                        last = mm(a[:, j * P:(j + 1) * P], Y[:, u, :], UT[:, u, :], start=True, stop=True)
                    if n < 6:
                        for j in range(4):
                            u = 4 * half + j
                            last = mm(b_[:, j * P:(j + 1) * P], UT[:, u, :], Y[:, u, :], start=True, stop=True)
                    last.then_inc(lev_p, 1)
            pe.wait_ge(lev_tu, 14)
            for u in range(U):
                t, h = u // H, u % H
                last = tr(bank[5 + 2 * t][:, h * P:(h + 1) * P], qkvT[:, 2 * H + h, t * P:(t + 1) * P], ident)
            for h in range(H):
                last = tr(bank[4][:, h * P:(h + 1) * P], head_tile(1, h), ident)
            last.then_inc(vk_psum, 1)
            fill()
            pe.wait_ge(vb_sb, 1)
            for h in range(H):
                last = mm(bank[6][:, h * P:(h + 1) * P], UT[:, h, :], VB[:, h, :], start=True, stop=True)
            last.then_inc(u0_psum, 1)
            fill()
            pe.wait_ge(u0_sb, 1)
            for h in range(H):
                last = mm(bank[4][:, h * P:(h + 1) * P], KDEC[:, h, :], U0[:, h, :], start=True, stop=True)
            last.then_inc(s1_psum, 1)
            for h in range(H):
                last = mm(bank[5][:, h * P:(h + 1) * P], QKT[:, h, :], U0[:, h, :], start=True, stop=True)
            last.then_inc(o_psum, 1)
            pe.wait_ge(s1_sb, 1)
            for h in range(H):
                last = mm(bank[6][:, h * P:(h + 1) * P], head_tile(1, H + h), S1[:, h, :], start=True, stop=True)
            last.then_inc(ks_psum, 1)
            for h in range(H):
                last = mm(bank[7][:, h * P:(h + 1) * P], head_tile(0, H + h), S1[:, h, :], start=True, stop=True)
            last.then_inc(ks_psum, 1)
            pe.wait_ge(r1_sb, 1)
            for h in range(H):
                last = mm(bank[4][:, h * P:(h + 1) * P], UT[:, H + h, :], R1[:, h, :], start=True, stop=True)
            last.then_inc(vn_psum, 1)
            pe.wait_ge(vn_sb, 1)
            for h in range(H):
                last = mm(bank[6][:, h * P:(h + 1) * P], QKT[:, H + h, :], VN[:, h, :], start=True, stop=True)
            last.then_inc(o_psum, 1)
            while filler[0] < N_UNITS:
                fill()

            pe.wait_ge(proj_sb, N_UNITS)
            for g in range(4):
                for e in range(2):
                    rows = slice(e * DH, (e + 1) * DH)
                    if g >= 1:
                        pe.wait_ge(sz_act, g)
                    mm(bank[e][:, 0:S], skT[rows, g, 0:P], sqT[rows, g, 0:S], start=True, stop=True)
                    last = mm(bank[e][:, S:S + P], skT[rows, g, P:S], sqT[rows, g, P:S], start=True, stop=True)
                last.then_inc(sz_psum, 1)
                pe.wait_ge(s_sp, g + 1)
                if g >= 1:
                    pe.wait_ge(s_t, g)
                for e in range(2):
                    spv = stick[:, 1, e, :]
                    mm(bank[2 + e][:, 0:S], tril, spv[:, 0:S], start=True, stop=False)
                    mm(bank[2 + e][:, P:S], ones, spv[:, S:S + P], start=False, stop=True)
                    last = mm(bank[2 + e][:, S:S + P], tril, spv[:, S:S + P], start=True, stop=True)
                last.then_inc(cs_psum, 1)
                pe.wait_ge(s_att, g + 1)
                if g == 0:
                    pe.wait_ge(o_sb, 2)
                else:
                    pe.wait_ge(ob_sb, g)
                for e in range(2):
                    h = 2 * g + e
                    att = stick[:, 2, e, :]
                    mm(bank[5][e * DH:(e + 1) * DH, 0:S], sv[:, 0, h * DH:(h + 1) * DH], att[:, 0:S],
                       start=True, stop=False)
                    last = mm(bank[5][e * DH:(e + 1) * DH, P:S], sv[:, 1, h * DH:(h + 1) * DH], att[:, S:S + P],
                              start=False, stop=True)
                last.then_inc(av_psum, 1)
            pe.wait_ge(on_sb, 1)
            for t in range(TT):
                for h in range(H):
                    last = tr(bank[6 + t][:, h * P:(h + 1) * P], ON[:, t * H + h, :], ident)
            last.then_inc(oat_psum, 1)

            pe.wait_ge(oat_sb, 1)
            pe.wait_ge(ob_sb, 4)
            arrived(11)
            arrived(12)
            for k in range(KD):
                if k >= 4:
                    pe.wait_ge(mg_sb, k - 3)
                for half, (n, src) in enumerate(((11, oaT), (12, obT))):
                    for j in range(4):
                        last = mm(bank[k % 4][:, half * S:(half + 1) * S], slot4(n)[:, j, k * P:(k + 1) * P],
                                  src[:, j, :], start=(j == 0), stop=(j == 3))
                last.then_inc(mg_psum, 1)
            pe.wait_ge(mg_psum, KD)
            pe.sem_inc(slot_free[11 % NSLOT], 1)
            pe.sem_inc(slot_free[12 % NSLOT], 1)
            arrived(13)
            arrived(14)
            pe.wait_ge(mg_sb, KD)
            for t in range(TT):
                for half in range(2):
                    for k in range(KD):
                        last = mm(bank[4 + 2 * t + half][:, :], merged[:, k, t * P:(t + 1) * P],
                                  slot4(13 + k // 4)[:, k % 4, half * 512:(half + 1) * 512],
                                  start=(k == 0), stop=(k == KD - 1))
                    last.then_inc(mix_psum, 1)
            pe.wait_ge(mix_psum, 4)
            pe.sem_inc(slot_free[13 % NSLOT], 1)
            pe.sem_inc(slot_free[14 % NSLOT], 1)

            for t in range(TT):
                pe.wait_ge(x1_sb, t + 1)
                x1k = xres[:, t, :].rearrange("s (p k) -> s k p", k=KD)
                for half in range(2):
                    for k in range(4):
                        last = tr(bank[2 * t + half][:, k * P:(k + 1) * P], x1k[:, 4 * half + k, :], ident)
                    last.then_inc(x1t_psum, 1)
            for t in range(TT):
                pe.wait_ge(x1t_sb, 2 * t + 2)
                for k in range(KD):
                    last = mm(bank[4][:, t * NE:(t + 1) * NE], xT[:, k, t * P:(t + 1) * P], wr[:, k, :],
                              start=(k == 0), stop=(k == KD - 1))
            last.then_inc(lg_psum, 1)
            pe.wait_ge(gsel_sb, 1)
            mm(bank[5][:, 0:4], sup, gsel[:, 0:4], start=True, stop=True)
            mm(bank[5][:, 4:8], ones, gsel[:, 0:4], start=True, stop=False)
            mm(bank[5][:, 4:8], sup, gsel[:, 4:8], start=False, stop=True)
            mm(bank[5][:, 8:12], ones, gsel[:, 0:4], start=True, stop=False)
            mm(bank[5][:, 8:12], ones, gsel[:, 4:8], start=False, stop=True).then_inc(rank_psum, 1)
            pe.wait_ge(sel_sb, 1)
            for n in range(5):
                for t in range(TT):
                    last = tr(bank[n // 2][:, (n % 2) * S + t * P:(n % 2) * S + (t + 1) * P], SEL[:, n, t, :], ident)
            last.then_inc(selt_psum, 1)
            for n in range(5):
                for t in range(TT):
                    last = mm(bank[6][:, n * EPG:(n + 1) * EPG], SEL[:, n, t, :],
                              comb5[:, (t * 5 + n) * EPG:(t * 5 + n + 1) * EPG], start=(t == 0), stop=(t == TT - 1))
            last.then_inc(selt_psum, 1)

            def gather(i):
                for half in range(2):
                    for k in range(4):
                        kt = 4 * half + k
                        for t in range(TT):
                            x1k = xres[:, t, :].rearrange("s (p k) -> s k p", k=KD)
                            last = mm(bank[7 - 3 * half][:, k * P:(k + 1) * P], x1k[:, kt, :],
                                      SEL[:, bass.ds(i, 1), t, :].rearrange("p n s -> p (n s)"),
                                      start=(t == 0), stop=(t == TT - 1))
                    last.then_inc(xg_psum, 1)

            pe.wait_ge(selt_sb, 1)
            pe.wait_ge(npass_sb, 1)
            npass = pe.value_load(small_i[0:1, 0:1], min_val=NG, max_val=NPASS_MAX)
            gather(0)
            with pe.Fori(0, npass) as i:
                def slot_wait(j, w):
                    n = PRE_LOADS + 3 * j + w
                    pe.wait_ge(slot_in[n % NSLOT], 32 * i + 16 * loads_of_slot(n))

                def slot_done(j, w):
                    pe.sem_inc(slot_free[(PRE_LOADS + 3 * j + w) % NSLOT], 1)

                def gate_up(j):
                    for w in range(2):
                        n = PRE_LOADS + 3 * j + w
                        slot_wait(j, w)
                        for k in range(KD):
                            last = mm(bank[2 * (j % 2) + w][:, :], xg[:, k, :], slot8(n)[:, k, :],
                                      start=(k == 0), stop=(k == KD - 1))
                        last.then_inc(gu_psum, 1)

                def transposes(j):
                    pe.wait_ge(hid_sb, i * 4 + (j + 1))
                    if j == 0:
                        pe.wait_ge(xg_sb, i + 1)
                    hk = hid[:, j % 2, :].rearrange("s (p k) -> s k p", k=KF)
                    for k in range(KF):
                        last = tr(bank[4][:, k * P:(k + 1) * P], hk[:, k, :], ident)
                    last.then_inc(ht_psum, 1)

                def down(j):
                    slot_wait(j, 2)
                    pe.wait_ge(ht_sb, i * 4 + (j + 1))
                    for half in range(2):
                        for k in range(KF):
                            last = mm(bank[5 + half][:, :], hidT[:, j % 2, k, :],
                                      slot4(PRE_LOADS + 3 * j + 2)[:, k, half * 512:(half + 1) * 512],
                                      start=(j == 0 and k == 0), stop=(j == EPG - 1 and k == KF - 1))
                    last.then_inc(y_psum, 1)

                pe.wait_ge(xg_sb, i + 1)
                gate_up(0)
                for j in range(1, EPG):
                    gate_up(j)
                    if j == 1:
                        pe.wait_ge(gu_psum, i * 8 + 2)
                    slot_done(j - 1, 0)
                    slot_done(j - 1, 1)
                    transposes(j - 1)
                    down(j - 1)
                    pe.wait_ge(gu_psum, i * 8 + 2 * (j + 1))
                    if j >= 2:
                        slot_done(j - 2, 2)
                pe.wait_ge(y_psum, i * 4 + 3)
                slot_done(2, 2)
                slot_done(3, 0)
                slot_done(3, 1)
                pe.wait_ge(ht_sb, i * 4 + 3)
                gather(i + 1)
                transposes_bank_free = 2 * (i + 1)
                pe.wait_ge(xg_sb, i + 2)
                pe.wait_ge(hid_sb, i * 4 + 4)
                hk = hid[:, 1, :].rearrange("s (p k) -> s k p", k=KF)
                for k in range(KF):
                    last = tr(bank[4][:, k * P:(k + 1) * P], hk[:, k, :], ident)
                last.then_inc(ht_psum, 1)
                down(3)
                pe.wait_ge(y_psum, i * 4 + 4)
                slot_done(3, 2)
                pe.wait_ge(y_sb, i + 1)
                pe.wait_ge(cur_sb, i + 1)
                for t in range(TT):
                    for half in range(2):
                        m = 2 * t + half
                        b = bank[7] if m % 2 == 0 else bank[4]
                        if m >= 2:
                            pe.wait_ge(sc_done, i * 4 + (m - 1))
                        mm(b[:, :], selt_cur[:, t * P:(t + 1) * P], ysb[:, half * 512:(half + 1) * 512],
                           start=True, stop=True).then_inc(sc_psum, 1)

        @block.scalar
        def _(act):
            steps = Steps(act, act_steps)
            a_ = nc.scalar.activation
            act.dma_start(cst[:, :], consts).then_inc(cst_in, 16)
            act.dma_start(wba[:, :, :], win_d[:, :, BA_COL:BA_COL + 8]).then_inc(small_in, 16)
            act.dma_start(buf_y[0:CONV_K * 3 * H, 0:P],
                          conv_w.rearrange("l k (j c) -> (l k j) c", c=P)).then_inc(small_in, 16)
            act.dma_start(alog, dn_a_log.partition_broadcast(P).rearrange("p a h -> p (a h)")).then_inc(small_in, 16)
            act.dma_start(dtb, dn_dt_bias.partition_broadcast(P).rearrange("p a h -> p (a h)")).then_inc(small_in, 16)
            act.dma_start(normw, dn_norm_w.rearrange("l (p o) -> (l p) o", o=1)).then_inc(small_in, 16)
            for t in range(TT):
                act.wait_ge(xt_psum, 2 * t + 1)
                nc.scalar.copy(xT[:, 0:4, t * P:(t + 1) * P],
                               bank[2 * t][:, :].rearrange("p (k s) -> p k s", s=P)).then_inc(xt_act, 1)

            def evacuate(u):
                _, kind, i = UNITS[u]
                b = bank[u % 4]
                b2 = b[:, :].rearrange("p (a s) -> p a s", a=2)
                act.wait_ge(proj_psum, u + 1)
                if kind == "qkv":
                    blk = i // 2
                    if blk == 0 and i == 0:
                        act.wait_ge(pads, 1)
                    if blk == 2:
                        act.wait_ge(conv_done, 1)
                    a = 2 * (i % 2)
                    ins = nc.scalar.copy(raw[:, blk % 2, a:a + 2, 3:3 + S], b2)
                elif kind == "ba":
                    ins = nc.scalar.copy(ba, b[:, 0:16])
                elif kind == "sq":
                    ins = nc.scalar.mul(sqT[:, 2 * i:2 * i + 2, :], b2, DH ** -0.5)
                elif kind == "sk":
                    ins = nc.scalar.copy(skT[:, 2 * i:2 * i + 2, :], b2)
                elif kind == "sv":
                    ins = nc.scalar.copy(sv[:, i, :], b[:, :])
                elif kind == "z":
                    ins = nc.scalar.copy(zg[:, i, :], b[:, :])
                else:
                    ins = nc.scalar.copy(gates[:, 2 * i:2 * i + 2, :], b2)
                ins.then_inc(proj_sb, 1)

            def silu_block(blk):
                act.wait_ge(conv_done, blk + 1)
                v = qkvT[:, 4 * blk:4 * blk + 4, :]
                a_(v, v, ACT.Silu).then_inc(silu_done, 1)
                if blk < 2:
                    act.wait_ge(silu_done, blk + 1)
                    dst = (buf_y if blk == 0 else buf_c)[:, :].rearrange("p (a s) -> p a s", a=4)
                    if blk == 0:
                        act.wait_ge(cw_psum, 1)
                    a_(dst, v, ACT.Square).then_inc(sq_done, 1)

            for u in range(4):
                evacuate(u)
            silu_block(0)
            evacuate(4)
            evacuate(5)
            silu_block(1)
            evacuate(6)
            silu_block(2)
            act.wait_ge(gb_pre, 1)
            a_(gb2, gb2, ACT.Exp)
            a_(nalog, alog, ACT.Exp)
            steps.then(a_(gb1, gg, ACT.Abs))
            steps.then(a_(gb1, gb1, ACT.Exp, scale=-1.0))
            a_(gb1, gb1, ACT.Ln, bias=1.0).then_inc(gb_exp, 1)
            rn = [buf_u[:, 0:512], buf_u[:, 512:1024], buf_t[:, 0:512], buf_t[:, 512:1024]]
            for i in range(4):
                act.wait_ge(ss_psum, i + 1)
                ins = a_(rn[i], bank[4 + i][:, :], ACT.Ln, bias=cst[:, C_SMALL:C_SMALL + 1])
            steps.then(ins)
            a_(buf_u[:, :], buf_u[:, :], ACT.Exp, scale=-0.5)
            a_(buf_t[:, :], buf_t[:, :], ACT.Exp, scale=-0.5).then_inc(rn_done, 1)
            evacuate(7)
            evacuate(8)
            act.wait_ge(dif_sb, 1)
            a_(DEC, DEC, ACT.Exp, scale=-1.0).then_inc(dec_exp, 1)
            a_(expg, gcum, ACT.Exp)
            a_(kdc, kdc, ACT.Exp).then_inc(eg_done, 1)
            evacuate(9)
            evacuate(10)
            evacuate(11)
            evacuate(12)
            act.wait_ge(lt_psum, 1)
            nc.scalar.copy(buf_lt[:, 0:512], bank[7][:, :])
            nc.scalar.copy(buf_lt[:, 512:1024], bank[4][:, :]).then_inc(lt_sb, 1)
            act.wait_ge(lt_psum, 2)
            nc.scalar.copy(buf_qk[:, 0:512], bank[5][:, :])
            nc.scalar.copy(buf_qk[:, 512:1024], bank[6][:, :]).then_inc(qkt_sb, 1)
            evacuate(13)
            evacuate(14)
            for n in range(1, 7):
                for half in range(2):
                    act.wait_ge(lev_y, 2 * (n - 1) + half + 1)
                    if n > 1:
                        act.wait_ge(lev_p, 2 * (n - 2) + half + 1)
                    nc.scalar.copy(buf_y[:, half * 512:(half + 1) * 512], bank[4 + 2 * half][:, :]).then_inc(lev_ysb, 1)
                evacuate(GATE0 + n - 1)
            evacuate(GATE0 + 6)
            act.wait_ge(vb_sb, 1)
            act.wait_ge(u0_psum, 1)
            nc.scalar.copy(U0, bank[6][:, :].rearrange("p (h c) -> p h c", c=P)).then_inc(u0_sb, 1)
            evacuate(GATE0 + 7)
            act.wait_ge(s1_psum, 1)
            nc.scalar.copy(S1, bank[4][:, :].rearrange("p (h c) -> p h c", c=P)).then_inc(s1_sb, 1)
            act.wait_ge(ks_psum, 2)
            for h in range(H):
                ins = nc.scalar.mul(QS[:, h, :], bank[7][:, h * P:(h + 1) * P], expg[:, H + h:H + h + 1])
            ins.then_inc(qs_sb, 1)
            act.wait_ge(vn_psum, 1)
            nc.scalar.copy(VN, bank[4][:, :].rearrange("p (h c) -> p h c", c=P)).then_inc(vn_sb, 1)
            act.wait_ge(o_sb, 2)
            a_(buf_y[:, :], buf_c[:, :], ACT.Square).then_inc(osq_sb, 1)

            for g in range(4):
                act.wait_ge(sz_psum, g + 1)
                if g >= 1:
                    act.wait_ge(s_t, g)
                nc.scalar.copy(stick[:, 0, :, :], psum[:, 0:2, 0:384]).then_inc(sz_act, 1)
                act.wait_ge(sz_dve, g + 1)
                if g >= 1:
                    act.wait_ge(av_psum, g)
                e_buf = stick[:, 2, :, :]
                steps.then(a_(e_buf, stick[:, 0, :, :], ACT.Abs))
                steps.then(a_(e_buf, e_buf, ACT.Exp, scale=-1.0))
                a_(e_buf, e_buf, ACT.Ln, bias=1.0).then_inc(s_e, 1)
                act.wait_ge(s_t, g + 1)
                a_(e_buf, e_buf, ACT.Exp).then_inc(s_att, 1)
            a_(buf_qk[:, :].rearrange("p (t n) -> p t n", t=TT), zg[:, :, :], ACT.Sigmoid).then_inc(z_sig, 1)
            a_(gates[:, 0:KD, :], gates[:, 0:KD, :], ACT.Sigmoid)
            a_(gates[:, KD:, :], gates[:, KD:, :], ACT.Sigmoid).then_inc(gate_sig, 1)
            act.wait_ge(o_psum, 2)
            act.wait_ge(on_sb, 1)
            act.dma_start(lnp[:, 0, :], ln1_g.partition_broadcast(P).rearrange("p a d -> p (a d)")).then_inc(late_in, 16)
            act.dma_start(lnp[:, 1, :], ln1_b.partition_broadcast(P).rearrange("p a d -> p (a d)")).then_inc(late_in, 16)
            act.dma_start(rbias, router_bias.partition_broadcast(P)).then_inc(late_in, 16)
            act.wait_ge(mg_sb, KD)
            act.dma_start(wr, w_router.rearrange("(p k) e -> p k e", k=KD)).then_inc(wr_in, 16)
            for t in range(TT):
                act.wait_ge(x1t_psum, 2 * t + 1)
                nc.scalar.copy(xT[:, 0:4, t * P:(t + 1) * P],
                               bank[2 * t][:, :].rearrange("p (k s) -> p k s", s=P)).then_inc(x1t_sb, 1)
                act.wait_ge(x1t_psum, 2 * t + 2)
                if t == 0:
                    act.wait_ge(wr_in, 16)
                nc.scalar.copy(xT[:, 4:8, t * P:(t + 1) * P],
                               bank[2 * t + 1][:, :].rearrange("p (k s) -> p k s", s=P)).then_inc(x1t_sb, 1)
            act.wait_ge(lg_psum, 1)
            a_(aff, bank[4][:, 0:TT * NE], ACT.Sigmoid).then_inc(aff_sb, 1)
            act.dma_start(lnp[:, 0, :], ln2_g.partition_broadcast(P).rearrange("p a d -> p (a d)")).then_inc(ln2_in, 16)
            act.dma_start(lnp[:, 1, :], ln2_b.partition_broadcast(P).rearrange("p a d -> p (a d)")).then_inc(ln2_in, 16)
            for t in range(TT):
                ins = nc.scalar.mul(r2[t], xres[:, t, :], ALPHA)
            ins.then_inc(r2_init, 1)
            act.wait_ge(selt_psum, 1)
            for n in range(0, 5, 2):
                m = min(2, 5 - n)
                nc.scalar.copy(SELT[:, n:n + m, :], bank[n // 2][:, 0:m * S].rearrange("p (n s) -> p n s", s=S))
            act.wait_ge(selt_psum, 2)
            nc.scalar.copy(cg, bank[6][:, 0:5 * EPG]).then_inc(selt_sb, 1)

            act.wait_ge(npass_sb, 1)
            npass = act.value_load(small_i[0:1, 0:1], min_val=NG, max_val=NPASS_MAX)
            act.wait_ge(xg_psum, 1)
            nc.scalar.copy(xg[:, 0:4, :], bank[7][:, :].rearrange("p (k s) -> p k s", s=P))
            act.wait_ge(xg_psum, 2)
            nc.scalar.copy(xg[:, 4:8, :], bank[4][:, :].rearrange("p (k s) -> p k s", s=P)).then_inc(xg_sb, 1)
            with act.Fori(0, npass) as i:
                def silu(j):
                    act.wait_ge(gu_psum, i * 8 + (2 * j + 1))
                    if j >= 2:
                        act.wait_ge(hid_sb, i * 4 + (j - 1))
                    a_(silu_g[:, j % 2, :], bank[2 * (j % 2)][:, :], ACT.Silu).then_inc(silu_sb, 1)

                def hid_t(j):
                    act.wait_ge(ht_psum, i * 4 + (j + 1))
                    nc.scalar.copy(hidT[:, j % 2, :, :],
                                   bank[4][:, :].rearrange("p (k s) -> p k s", s=P)).then_inc(ht_sb, 1)

                for j in range(EPG):
                    silu(j)
                    if j >= 1:
                        hid_t(j - 1)
                act.wait_ge(xg_psum, i * 2 + 3)
                nc.scalar.copy(xg[:, 0:4, :], bank[7][:, :].rearrange("p (k s) -> p k s", s=P))
                act.wait_ge(xg_psum, i * 2 + 4)
                nc.scalar.copy(xg[:, 4:8, :], bank[4][:, :].rearrange("p (k s) -> p k s", s=P)).then_inc(xg_sb, 1)
                hid_t(3)
                act.wait_ge(y_psum, i * 4 + 4)
                nc.scalar.copy(ysb[:, 0:512], bank[5][:, :])
                nc.scalar.copy(ysb[:, 512:1024], bank[6][:, :]).then_inc(y_sb, 1)

        @block.gpsimd
        def _(pool):
            nc.gpsimd.memset(raw[:, :, :, 0:3], 0.0).then_inc(pads, 1)
            pool.wait_ge(cst_in, 16)
            pool.wait_ge(lt_sb, 1)
            for n in range(1, 7):
                if n > 1:
                    pool.wait_ge(lev_y, 2 * (n - 1))
                m = c(C_LEV + n * P).unsqueeze(1).to_broadcast([P, U, P])
                nc.gpsimd.tensor_tensor(CM, LT, m, ALU.mult).then_inc(lev_mask, 1)
            pool.wait_ge(rms_in, 1)
            nc.gpsimd.tensor_tensor(rms, ssq, cst[:, C_SMALL + 1:C_SMALL + 1 + U], ALU.pow).then_inc(rms_done, 1)
            for n, (v, r) in enumerate(((var1, rstd1), (var2, rstd2))):
                if n == 1:
                    break
                pool.wait_ge(v, TT)
                nc.gpsimd.tensor_tensor(rstd, rstd, cst[:, C_SMALL + 1:C_SMALL + 3], ALU.pow).then_inc(r, 1)
            pool.wait_ge(npass_sb, 1)
            npass = pool.value_load(small_i[0:1, 0:1], min_val=NG, max_val=NPASS_MAX)
            pool.wait_ge(selt_sb, 1)
            with pool.Fori(0, npass) as i:
                pool.wait_ge(gu_psum, i * 8 + 1)
                nc.gpsimd.tensor_copy(selt_cur, SELT[:, bass.ds(i, 1), :].rearrange("p n s -> p (n s)")).then_inc(cur_sb, 1)
            pool.wait_ge(var2, TT)
            nc.gpsimd.tensor_tensor(rstd, rstd, cst[:, C_SMALL + 1:C_SMALL + 3], ALU.pow).then_inc(rstd2, 1)

        @block.vector
        def _(dve):
            v = nc.vector
            steps = Steps(dve, dve_steps)
            for t in range(TT):
                dve.wait_ge(xt_psum, 2 * t + 2)
                v.tensor_copy(xT[:, 4:8, t * P:(t + 1) * P],
                              bank[2 * t + 1][:, :].rearrange("p (k s) -> p k s", s=P)).then_inc(xt_dve, 1)
            dve.wait_ge(cw_psum, 1)
            v.tensor_copy(convw, bank[4][:, 0:CONV_K * 3 * H]).then_inc(cw_sb, 1)
            dve.wait_ge(cw_sb, 1)
            dve.wait_ge(pads, 1)

            def conv(blk):
                dve.wait_ge(proj_sb, 2 * blk + 2)
                for k in range(CONV_K):
                    for h in range(H):
                        j = 4 * blk + h
                        src, dst = raw[:, blk % 2, h, k:k + S], qkvT[:, j, :]
                        w = convw[:, k * 3 * H + j:k * 3 * H + j + 1]
                        if k == 0:
                            ins = v.tensor_scalar(dst, src, w, None, ALU.mult)
                        else:
                            ins = v.scalar_tensor_tensor(dst, src, w, dst, ALU.mult, ALU.add)
                    if k < CONV_K - 1:
                        steps.then(ins)
                ins.then_inc(conv_done, 1)

            conv(0)
            conv(1)
            conv(2)
            dve.wait_ge(proj_sb, 7)
            dve.wait_ge(small_in, 16 * 5)
            ba3 = ba.rearrange("p (t n) -> p t n", t=TT)
            g3, a3, b3, be3 = (z_.rearrange("p (t n) -> p t n", t=TT) for z_ in (gg, gb1, gb2, beta))
            steps.then(v.tensor_tensor(g3, ba3[:, :, H:2 * H], dtb.unsqueeze(1).to_broadcast([P, TT, H]), ALU.add))
            v.tensor_scalar(b3, ba3[:, :, 0:H], -1.0, None, ALU.mult).then_inc(gb_pre, 1)
            dve.wait_ge(gb_exp, 1)
            v.tensor_scalar_add(gb2, gb2, 1.0)
            steps.then(v.scalar_tensor_tensor(gg, gg, 0.0, gb1, ALU.max, ALU.add))
            v.reciprocal(beta, gb2)
            steps.then(v.scalar_tensor_tensor(g3, g3, -1.0, nalog.unsqueeze(1).to_broadcast([P, TT, H]), ALU.mult, ALU.mult))
            v.tensor_copy(LT, gg.unsqueeze(2).to_broadcast([P, U, P])).then_inc(g_sb, 1)
            dve.wait_ge(rn_done, 1)
            qv, kv = (qkvT[:, 4 * i:4 * i + 4, :].rearrange("p a s -> p (a s)") for i in range(2))
            v.scalar_tensor_tensor(qv, qv, P ** -0.5, buf_u[:, :], ALU.mult, ALU.mult)
            v.tensor_tensor(kv, kv, buf_t[:, :], ALU.mult).then_inc(qk_norm, 1)
            dve.wait_ge(gc_psum, 1)
            v.tensor_copy(gcum, bank[4][:, 0:U])
            v.tensor_copy(glast, bank[4][:, U:2 * U]).then_inc(gc_sb, 1)
            dve.wait_ge(gc_sb, 1)
            dve.wait_ge(gc_psum, 2)
            v.tensor_tensor(kdc, glast, gcum, ALU.subtract)
            for u in range(U):
                ins = v.tensor_scalar(DEC[:, u, :], bank[5 + u // 4][:, (u % 4) * P:(u % 4 + 1) * P],
                                      gcum[:, u:u + 1], 0.0, ALU.subtract, ALU.max)
            ins.then_inc(dif_sb, 1)
            dve.wait_ge(dec_exp, 1)
            dve.wait_ge(eg_done, 1)
            v.scalar_tensor_tensor(nbg, beta, -1.0, expg, ALU.mult, ALU.mult)
            steps.then(v.tensor_tensor(DEC, DEC, tril.unsqueeze(1).to_broadcast([P, U, P]), ALU.mult))
            dve.wait_ge(kk_psum, 1)
            kkb, qkb = [bank[7], bank[4]], [bank[5], bank[6]]
            for u in range(U):
                ins = v.scalar_tensor_tensor(L[:, u, :], kkb[u // 4][:, (u % 4) * P:(u % 4 + 1) * P],
                                             beta[:, u:u + 1], DEC[:, u, :], ALU.mult, ALU.mult)
            ins.then_inc(lq_sb, 1)
            dve.wait_ge(kk_psum, 2)
            for t in range(TT):
                ins = v.tensor_tensor(QKT[:, 4 * t:4 * t + 4, :], qkb[t][:, :].rearrange("p (u c) -> p u c", c=P),
                                      DEC[:, 4 * t:4 * t + 4, :], ALU.mult)
            ins.then_inc(lq_sb, 1)
            ident_b = ident.unsqueeze(1).to_broadcast([P, U, P])
            dve.wait_ge(lq_sb, 1)
            steps.then(v.tensor_tensor(T, L, c(C_LEV1).unsqueeze(1).to_broadcast([P, U, P]), ALU.mult))
            steps.then(v.tensor_tensor(T, T, ident_b, ALU.add))
            dve.wait_ge(lt_sb, 1)
            steps.then(v.tensor_tensor(UT, LT, c(C_LEV).unsqueeze(1).to_broadcast([P, U, P]), ALU.mult))
            v.tensor_tensor(UT, UT, ident_b, ALU.add).then_inc(lev_tu, 2)
            for n in range(1, 7):
                for half in range(2):
                    s = slice(half * 512, (half + 1) * 512)
                    dve.wait_ge(lev_p, 2 * (n - 1) + half + 1)
                    if n == 1 and half == 0:
                        dve.wait_ge(lev_tu, 2)
                    if n < 6:
                        v.tensor_tensor(buf_t[:, s], buf_t[:, s], bank[5 + 2 * half][:, :], ALU.subtract)
                    v.tensor_tensor(buf_u[:, s], buf_u[:, s], bank[4 + 2 * half][:, :], ALU.subtract).then_inc(lev_tu, 1)
            dve.wait_ge(vk_psum, 1)
            for u in range(U):
                t, h = u // H, u % H
                v.tensor_scalar(VB[:, u, :], bank[5 + 2 * t][:, h * P:(h + 1) * P], beta[:, u:u + 1], None, ALU.mult)
            for h in range(H):
                ins = v.tensor_scalar(KDEC[:, h, :], bank[4][:, h * P:(h + 1) * P], kdc[:, h:h + 1], None, ALU.mult)
            ins.then_inc(vb_sb, 1)
            dve.wait_ge(vb_sb, 1)
            dve.wait_ge(ks_psum, 1)
            for h in range(H):
                ins = v.scalar_tensor_tensor(R1[:, h, :], bank[6][:, h * P:(h + 1) * P], nbg[:, H + h:H + h + 1],
                                             VB[:, H + h, :], ALU.mult, ALU.add)
            ins.then_inc(r1_sb, 1)
            dve.wait_ge(o_psum, 1)
            v.tensor_copy(O[:, 0:H, :], bank[5][:, :].rearrange("p (h c) -> p h c", c=P)).then_inc(o_sb, 1)
            dve.wait_ge(o_psum, 2)
            dve.wait_ge(qs_sb, 1)
            v.tensor_tensor(O[:, H:U, :], QS, bank[6][:, :].rearrange("p (h c) -> p h c", c=P), ALU.add).then_inc(o_sb, 1)
            dve.wait_ge(osq_sb, 1)
            steps.then(v.tensor_reduce(ssq, Y, AX_X, ALU.add))
            v.tensor_scalar(ssq, ssq, 1.0 / P, RMS_EPS, ALU.mult, ALU.add).then_inc(rms_in, 1)

            for g in range(4):
                dve.wait_ge(sz_act, g + 1)
                diag = stick[:, 0, :, :].rearrange("p e (b s) -> p e b s", s=P)[:, :, 0:3:2, :]
                v.tensor_tensor(diag, diag, neg.unsqueeze(1).unsqueeze(1).to_broadcast([P, 2, 2, P]),
                                ALU.add).then_inc(sz_dve, 1)
                dve.wait_ge(sz_dve, g + 1)
                dve.wait_ge(s_e, g + 1)
                if g >= 1:
                    dve.wait_ge(cs_psum, g)
                v.scalar_tensor_tensor(stick[:, 1, :, :], stick[:, 0, :, :], 0.0, stick[:, 2, :, :],
                                       ALU.max, ALU.add).then_inc(s_sp, 1)
                dve.wait_ge(s_sp, g + 1)
                dve.wait_ge(cs_psum, g + 1)
                for e in range(2):
                    ins = v.tensor_tensor(stick[:, 2, e, :], stick[:, 0, e, :], bank[2 + e][:, 0:384], ALU.subtract)
                ins.then_inc(s_t, 1)
                dve.wait_ge(av_psum, g + 1)
                v.tensor_copy(obT[:, g, :], bank[5][:, 0:S]).then_inc(ob_sb, 1)
            dve.wait_ge(z_sig, 1)
            dve.wait_ge(rms_done, 1)
            zf = zg[:, :, :].rearrange("p t n -> p (t n)")
            steps.then(v.tensor_tensor(zf, zf, buf_qk[:, :], ALU.mult))
            for u in range(U):
                ins = v.scalar_tensor_tensor(ON[:, u, :], O[:, u, :], rms[:, u:u + 1],
                                             zf[:, u * P:(u + 1) * P], ALU.mult, ALU.mult)
            ins.then_inc(on_sb, 1)
            dve.wait_ge(oat_psum, 1)
            for t in range(TT):
                ins = v.tensor_scalar(oaT[:, :, t * P:(t + 1) * P],
                                      bank[6 + t][:, :].rearrange("p (h s) -> p h s", s=P), normw, None, ALU.mult)
            ins.then_inc(oat_sb, 1)
            dve.wait_ge(gate_sig, 1)
            for k in range(KD):
                dve.wait_ge(mg_psum, k + 1)
                gp = gates[:, k:k + KD + 1:KD, :]
                steps.then(v.tensor_tensor(gp, gp, bank[k % 4][:, :].rearrange("p (a s) -> p a s", a=2), ALU.mult))
                v.tensor_tensor(merged[:, k, :], gates[:, k, :], gates[:, KD + k, :], ALU.add).then_inc(mg_sb, 1)
            st = stats.rearrange("p (t h s) -> p t h s", t=TT, h=2)

            def norm_stats(src, sems):
                for t in range(TT):
                    for half in range(2):
                        ins = v.bn_stats(st[:, t, half, :], src(t)[:, half * 512:(half + 1) * 512])
                    steps.then(ins)
                    steps.then(v.bn_aggr(mv[:, 2 * t:2 * t + 2], st[:, t, :, :].rearrange("p h s -> p (h s)")))
                    v.tensor_scalar_add(rstd[:, t:t + 1], mv[:, 2 * t + 1:2 * t + 2], LN_EPS).then_inc(sems, 1)

            for t in range(TT):
                for half in range(2):
                    dve.wait_ge(mix_psum, 2 * t + half + 1)
                    xs = xres[:, t, half * 512:(half + 1) * 512]
                    ins = v.scalar_tensor_tensor(xs, xs, ALPHA, bank[4 + 2 * t + half][:, :], ALU.mult, ALU.add)
            steps.then(ins)
            norm_stats(lambda t: xres[:, t, :], var1)
            dve.wait_ge(rstd1, 1)
            dve.wait_ge(late_in, 48)
            for t in range(TT):
                xs = xres[:, t, :]
                steps.then(v.tensor_scalar(xs, xs, mv[:, 2 * t:2 * t + 1], rstd[:, t:t + 1], ALU.subtract, ALU.mult))
                steps.then(v.tensor_tensor(xs, xs, lnp[:, 0, :], ALU.mult))
                v.tensor_tensor(xs, xs, lnp[:, 1, :], ALU.add).then_inc(x1_sb, 1)

            dve.wait_ge(aff_sb, 1)
            sel3 = selv.rearrange("p (t e) -> p t e", t=TT)
            steps.then(v.tensor_tensor(sel3, aff.rearrange("p (t e) -> p t e", t=TT),
                                       rbias.unsqueeze(1).to_broadcast([P, TT, NE]), ALU.add))

            def rank_of_four(dst, src, n, limit):
                s4 = src.rearrange("p (m i) -> p m i", i=4)
                other = s4.unsqueeze(2).to_broadcast([P, n, 4, 4])
                own = s4.unsqueeze(3).to_broadcast([P, n, 4, 4])
                gt = spare[:, 0:16 * n]
                eq = spare[:, 256:256 + 16 * n]
                gt4 = gt.rearrange("p (m i j) -> p m i j", i=4, j=4)
                eq4 = eq.rearrange("p (m i j) -> p m i j", i=4, j=4)
                v.tensor_tensor(gt4, other, own, ALU.is_gt)
                steps.then(v.tensor_tensor(eq4, other, own, ALU.is_equal))
                eq3 = eq.rearrange("p (m q) -> p m q", q=16)
                steps.then(v.tensor_tensor(eq3, eq3, c(C_JLT, 16).unsqueeze(1).to_broadcast([P, n, 16]), ALU.mult))
                steps.then(v.tensor_tensor(gt, gt, eq, ALU.add))
                steps.then(v.tensor_reduce(dst, gt.rearrange("p (q j) -> p q j", j=4), AX_X, ALU.add))
                steps.then(v.tensor_single_scalar(dst, dst, limit, ALU.is_lt))

            rank_of_four(top2, selv, 2 * NG, 2.0)
            steps.then(v.tensor_tensor(selv, selv, top2, ALU.mult))
            steps.then(v.tensor_reduce(gscore, selv.rearrange("p (g i) -> p g i", i=EPG), AX_X, ALU.add))
            rank_of_four(gsel, gscore, TT, 1.0)
            v.sem_inc(gsel_sb, 1)
            gs3 = gsel.unsqueeze(2).to_broadcast([P, 2 * NG, EPG])
            t3 = top2.rearrange("p (g i) -> p g i", i=EPG)
            steps.then(v.tensor_tensor(t3, t3, gs3, ALU.mult))
            steps.then(v.tensor_tensor(comb, aff, top2, ALU.mult))
            steps.then(v.tensor_reduce(wsum, comb.rearrange("p (t e) -> p t e", t=TT), AX_X, ALU.add))
            steps.then(v.reciprocal(wsum, wsum))
            for t in range(TT):
                ins = v.tensor_scalar(comb[:, t * NE:(t + 1) * NE], comb[:, t * NE:(t + 1) * NE],
                                      wsum[:, t:t + 1], None, ALU.mult)
            steps.then(ins)
            c5 = comb5.rearrange("p (t n j) -> p t n j", t=TT, n=5)
            for t in range(TT):
                v.tensor_copy(c5[:, t, 0:NG, :], comb[:, t * NE:(t + 1) * NE].rearrange("p (g j) -> p g j", j=EPG))
                ins = v.tensor_reduce(c5[:, t, NG, :], comb[:, t * NE:(t + 1) * NE].rearrange("p (g j) -> p j g", j=EPG),
                                      AX_X, ALU.add)
            s5 = sel5.rearrange("p (t n) -> p t n", t=TT)
            r5 = rank5.rearrange("p (t n) -> p t n", t=TT)
            v.tensor_copy(s5[:, :, 0:NG], gsel.rearrange("p (t g) -> p t g", t=TT))
            v.memset(s5[:, :, NG:NG + 1], 1.0)
            v.memset(SEL[:, 5, :, :], 0.0)
            dve.wait_ge(rank_psum, 1)
            rk3 = rank.rearrange("p (t g) -> p t g", t=TT)
            v.tensor_copy(cnt, bank[5][:, 8:12])
            v.tensor_copy(r5[:, :, 0:NG], bank[5][:, 0:8].rearrange("p (t g) -> p t g", t=TT))
            steps.then(v.tensor_tensor(rank, gsel, bank[5][:, 0:8], ALU.mult))
            steps.then(v.tensor_reduce(wsum, rk3, AX_X, ALU.add))
            steps.then(v.tensor_scalar_add(r5[:, :, NG], wsum, -128.0))
            steps.then(v.tensor_single_scalar(ovf, cnt, 128.0, ALU.is_gt))
            steps.then(v.tensor_reduce(cnt[:, 0:1], ovf, AX_X, ALU.add))
            v.tensor_tensor(cnt[:, 1:4], ovf[:, 1:4], cst[:, C_IOTA + 1:C_IOTA + 4], ALU.mult)
            steps.then(v.tensor_scalar_add(small_i[:, 0:1], cnt[:, 0:1], float(NG)))
            v.memset(small_i[:, 3:4], NG - 1)
            steps.then(v.tensor_reduce(ovf[:, 0:1], cnt[:, 1:4], AX_X, ALU.add))
            steps.then(v.tensor_copy(small_i[:, 4:5], ovf[:, 0:1]))
            v.sem_inc(npass_sb, 1)
            for n in range(5):
                for t in range(TT):
                    ins = v.tensor_scalar(SEL[:, n, t, :], iota, rank5[:, t * 5 + n:t * 5 + n + 1],
                                          sel5[:, t * 5 + n:t * 5 + n + 1], ALU.is_equal, ALU.mult)
            ins.then_inc(sel_sb, 1)

            npass = dve.value_load(small_i[0:1, 0:1], min_val=NG, max_val=NPASS_MAX)
            dve.wait_ge(selt_sb, 1)
            dve.wait_ge(r2_init, 1)
            with dve.Fori(0, npass) as i:
                v.tensor_copy(cgcur, cg.rearrange("p (n j) -> p n j", j=EPG)[:, bass.ds(i, 1), :]
                              .rearrange("p n j -> p (n j)")).then_inc(cg_sb, 1)
                dve.wait_ge(cg_sb, i + 1)
                for j in range(EPG):
                    dve.wait_ge(gu_psum, i * 8 + (2 * j + 2))
                    dve.wait_ge(silu_sb, i * 4 + (j + 1))
                    if j >= 2:
                        dve.wait_ge(ht_psum, i * 4 + (j - 1))
                    v.scalar_tensor_tensor(hid[:, j % 2, :], silu_g[:, j % 2, :], cgcur[:, j:j + 1],
                                           bank[2 * (j % 2) + 1][:, :], ALU.mult, ALU.mult).then_inc(hid_sb, 1)
                for m in range(4):
                    t, half = m // 2, m % 2
                    dve.wait_ge(sc_psum, i * 4 + (m + 1))
                    rs = r2[t][:, half * 512:(half + 1) * 512]
                    v.tensor_tensor(rs, rs, (bank[7] if m % 2 == 0 else bank[4])[:, :], ALU.add).then_inc(sc_done, 1)
            dve.wait_ge(sc_done, npass * 4)
            norm_stats(lambda t: r2[t], var2)
            dve.wait_ge(rstd2, 1)
            dve.wait_ge(ln2_in, 32)
            for t in range(TT):
                steps.then(v.tensor_scalar(r2[t], r2[t], mv[:, 2 * t:2 * t + 1], rstd[:, t:t + 1], ALU.subtract, ALU.mult))
                steps.then(v.tensor_tensor(r2[t], r2[t], lnp[:, 0, :], ALU.mult))
                v.tensor_tensor(r2[t], r2[t], lnp[:, 1, :], ALU.add).then_inc(out_sb, 1)


_INS = ['x', 'w_in', 'conv_w', 'dn_a_log', 'dn_dt_bias', 'dn_norm_w', 'p_a', 'p_b', 'w_out', 'ln1_g', 'ln1_b',
        'w_router', 'router_bias', 'w_gate', 'w_up', 'w_down', 'ln2_g', 'ln2_b']


def kernel(**inputs):
    import numpy as _np
    import concourse.bacc as _bacc
    from concourse.bass_utils import run_bass_kernel_spmd as _run

    nc = _bacc.Bacc("TRN2", target_bir_lowering=False, num_devices=1)
    table = constant_table()
    arrays = {"consts_dram": table}
    args = [nc.dram_tensor("consts_dram", table.shape, F32, kind="ExternalInput").ap()]
    for name in _INS:
        a = _np.ascontiguousarray(inputs[name])
        arrays[f"in_{name}_dram"] = a
        args.append(nc.dram_tensor(f"in_{name}_dram", a.shape, mybir.dt.from_np(a.dtype), kind="ExternalInput").ap())
    args.append(nc.dram_tensor("out_dram", (1, S, D), F32, kind="ExternalOutput").ap())
    hybrid_moe_block(nc, *args)
    r = _run(nc, [arrays], core_ids=[0])
    return r.results[0]["out_dram"]
```

```python
from contextlib import ExitStack

import concourse.bass as bass
from concourse import mybir
import numpy as np

F32 = mybir.dt.float32
F32R = mybir.dt.float32r
I32 = mybir.dt.int32
ALU = mybir.AluOpType
ACT = mybir.ActivationFunctionType
AX_X = mybir.AxisListType.X

P = 128
D = 1024
KD = D // P
S = 256
TT = S // P
H = 4
U = TT * H
SH, DH = 8, 64
NE, NG, EPG = 16, 4, 4
F = 512
KF = F // P
CONV_K = 4
DELTA_W = H * P
LN_EPS, RMS_EPS = 1e-5, 1e-6
ALPHA = 2.0 ** 0.25
NPASS_MAX = NG + 1
MASKED = -1e30

HALF = 2048
NSLOT = 4
NRAW = 8
LO_CUT = 1536
BLOCKS = [(0, "qkv"), (512, "qkv"), (1024, "qkv"), (2056, "sq"), (2568, "sk"), (3080, "sv"), (1536, "z"),
          (3592, "gate"), (4104, "gate"), (4616, "gate"), (5128, "gate")]
NB = len(BLOCKS)
STICK_UNIT = 12
BA_COL = 2048
PB0, PA0, WO0 = 2 * NB, 2 * NB + 2, 2 * NB + 4
PRE = 2 * NB + 8
PASS = 2 * 3 * EPG
PASS_ORDER = [(0, 0), (0, 1), (1, 0), (1, 1), (0, 2), (2, 0), (2, 1), (1, 2), (3, 0), (3, 1), (2, 2), (3, 2)]

C_IDENT, C_TRIU, C_TRIL, C_ONES, C_NEG, C_LEV1 = (P * i for i in range(6))
C_LEV = C_LEV1 + P
C_SMALL = C_LEV + 7 * P
NCONST = C_SMALL + 16
C_SUP = NCONST
C_IOTA = C_SUP + P
C_JLT = C_IOTA + P
NTABLE = C_JLT + 16


def constant_table():
    p = np.arange(P)[:, None]
    f = np.arange(P)[None, :]
    t = np.zeros((P, NTABLE), np.float32)
    t[:, C_IDENT:C_IDENT + P] = p == f
    t[:, C_TRIU:C_TRIU + P] = p <= f
    t[:, C_TRIL:C_TRIL + P] = p >= f
    t[:, C_SUP:C_SUP + P] = p < f
    t[:, C_ONES:C_ONES + P] = 1.0
    t[:, C_NEG:C_NEG + P] = np.where(p < f, 0.0, MASKED)
    t[:, C_IOTA:C_IOTA + P] = f
    t[:, C_LEV1:C_LEV1 + P] = -((p // 2 == f // 2) & (p % 2 == 1) & (f % 2 == 0)).astype(np.float32)
    for n in range(7):
        s = 1 << n
        at = C_LEV + n * P
        m = (p // (2 * s) == f // (2 * s)) & ((f // s) % 2 == 1) & ((p // s) % 2 == 0)
        t[:, at:at + P] = -m.astype(np.float32) if n == 0 else m
    ij = np.arange(16)
    t[:, C_JLT:C_JLT + 16] = (ij % 4 < ij // 4)
    t[:, C_SMALL] = RMS_EPS
    t[:, C_SMALL + 1:C_SMALL + 16] = -0.5
    return t


class Steps:

    def __init__(self, eng, sem):
        self.eng, self.sem, self.n = eng, sem, 0

    def then(self, ins):
        self.n += 1
        ins.then_inc(self.sem, 1)
        self.eng.wait_ge(self.sem, self.n)


def hybrid_moe_block(nc, consts, x, w_in, conv_w, dn_a_log, dn_dt_bias, dn_norm_w, p_a, p_b, w_out,
                     ln1_g, ln1_b, w_router, router_bias, w_gate, w_up, w_down, ln2_g, ln2_b, out):
    ctx = ExitStack()
    with ctx:
        def sem(name):
            return ctx.enter_context(nc.semaphore(name))

        base = (nc.sbuf_base + 31) // 32 * 32
        top = [base]

        def region(nbytes):
            a = top[0]
            top[0] += nbytes
            return a

        def place(name, shape, offset, dt=F32):
            return nc.alloc_sbuf_tensor_at(name, shape, dt, offset=offset)

        KB = 1024
        R_RAW, R_HI, R_LO = (region(NSLOT * 4 * HALF) for _ in range(3))
        R_X, R_QKV, R_CONV, R_Z = region(16 * KB), region(12 * KB), region(2 * H * (S + 4) * 4), region(4 * KB)
        R_SQ, R_SK, R_SV, R_GATE = region(4 * KB), region(4 * KB), region(4 * KB), region(16 * KB)
        R_B = [region(4 * KB) for _ in range(6)]
        R_STICK, R_CST, R_SMALL = region(9 * KB), region(NCONST * 4), region(4 * 600 + 64)
        assert top[0] <= nc.sbuf_usable_end

        wraw = place("wraw", [P, NSLOT, HALF], R_RAW)
        extra = [place(f"wraw{i}", [P, HALF], a) for i, a in enumerate(
            (R_SQ, R_QKV + 8 * KB, R_QKV + 16 * KB, R_B[5]))]
        expert_raw = [t[:, :] for t in extra] + [wraw[:, (WO0 + i) % NSLOT, :] for i in range(NSLOT)]
        whi = place("whi", [P, NSLOT, HALF], R_HI, F32R)
        wlo = place("wlo", [P, NSLOT, HALF], R_LO, F32R)
        x0 = place("x0", [P, TT, D], R_GATE)
        xh = place("xh", [P, KD, S], R_X, F32R)
        xl = place("xl", [P, KD, S], R_X + 8 * KB, F32R)
        xres = place("xres", [P, TT, D], R_X)
        lgt = place("lgt", [P, S], R_STICK + 4 * KB)
        x1T = place("x1T", [P, KD, S], R_X + 8 * KB)
        qkvT = place("qkvT", [P, 3 * H, S], R_QKV)
        raw = place("raw", [P, 2, H, S + 4], R_CONV)
        L = place("L", [P, U, P], R_CONV)
        DEC = place("DEC", [P, U, P], R_CONV + 4 * KB)
        VB = place("VB", [P, U, P], R_CONV)
        KDEC = place("KDEC", [P, H, P], R_CONV + 4 * KB)
        U0 = place("U0", [P, H, P], R_CONV + 6 * KB)
        zg = place("zg", [P, TT * DELTA_W], R_Z)
        LT = place("LT", [P, U, P], R_B[0])
        GB = place("GB", [P, U, P], R_B[0])
        T = place("T", [P, U, P], R_B[1])
        UT = place("UT", [P, U, P], R_B[2])
        Y = place("Y", [P, U, P], R_B[3])
        CM = place("CM", [P, U, P], R_B[4])
        wbah = place("wbah", [P, KD, 8], R_B[5], F32R)
        wbal = place("wbal", [P, KD, 8], R_B[5] + 256, F32R)
        baT = place("baT", [P, S], R_B[5] + KB)
        QKT = place("QKT", [P, U, P], R_B[5])
        rn = place("rn", [P, 2 * U * P], R_B[1])
        sqq = place("sqq", [P, 2 * U * P], R_B[3])
        cwrow = place("cwrow", [P, P], R_B[3])
        S1 = place("S1", [P, H, P], R_B[1])
        R1 = place("R1", [P, H, P], R_B[1] + 2 * KB)
        QS = place("QS", [P, H, P], R_B[3])
        VN = place("VN", [P, H, P], R_B[3] + 2 * KB)
        O = place("O", [P, U, P], R_B[4])
        OSQ = place("OSQ", [P, U, P], R_STICK)
        ON = place("ON", [P, U, P], R_B[0])
        oah = place("oah", [P, H, S], R_QKV, F32R)
        oal = place("oal", [P, H, S], R_QKV + 4 * KB, F32R)
        sqT = place("sqT", [P, 4, S], R_SQ)
        skT = place("skT", [P, 4, S], R_SK)
        sv = place("sv", [P, TT, SH * DH], R_SV)
        obh = place("obh", [P, 4, S], R_SQ, F32R)
        obl = place("obl", [P, 4, S], R_SK, F32R)
        stick = place("stick", [P, 3, 2, 384], R_STICK)
        gates = place("gates", [P, 2 * KD, S], R_GATE)
        msum = place("msum", [P, 2, 2 * S], R_STICK + 4 * KB)
        mh = place("mh", [P, KD, S], R_GATE, F32R)
        ml = place("ml", [P, KD, S], R_GATE + 8 * KB, F32R)
        lnp = place("lnp", [P, 2, D], R_B[3])
        r2 = place("r2", [P, TT, D], R_B[0])
        SEL = place("SEL", [P, 5, TT, P], R_GATE)
        SELT = place("SELT", [P, 5, S], R_GATE + 5 * KB)
        selt_cur = place("selt_cur", [P, S], R_GATE + 10 * KB, F32R)
        spare = place("spare", [P, 512], R_SV)
        wr = place("wr", [P, KD, NE], R_SV + 2048)
        late = place("late", [P, NTABLE - NCONST], R_SV + 2560)
        xgh = place("xgh", [P, KD, P], R_QKV, F32R)
        xgl = place("xgl", [P, KD, P], R_QKV + 4 * KB, F32R)
        hid = place("hid", [P, F], R_B[2])
        silu_g = place("silu_g", [P, F], R_B[2] + 2 * KB)
        hth = place("hth", [P, KF, P], R_GATE + 11 * KB, F32R)
        htl = place("htl", [P, KF, P], R_GATE + 13 * KB, F32R)
        yh = place("yh", [P, D], R_X + 8 * KB, F32R)
        yl = place("yl", [P, D], R_X + 12 * KB, F32R)

        cst = place("cst", [P, NCONST], R_CST)
        small = place("small", [P, 592], R_SMALL)
        small_i = place("small_i", [P, 8], R_SMALL + 4 * 592, I32)

        def c(at, n=P):
            return cst[:, at:at + n]

        ident, triu, tril, ones, neg = (c(x_) for x_ in (C_IDENT, C_TRIU, C_TRIL, C_ONES, C_NEG))
        sup, iota, jlt = late[:, 0:P], late[:, P:2 * P], late[:, 2 * P:2 * P + 16]

        at = [0]

        def cols(n):
            a = small[:, at[0]:at[0] + n]
            at[0] += n
            return a

        wba = cols(KD * 8).rearrange("p (k n) -> p k n", k=KD)
        ba, gg, gb1, gb2, beta = cols(16), cols(U), cols(U), cols(U), cols(U)
        alog, dtb, nalog = cols(H), cols(H), cols(H)
        gcum, glast, expg, kdc, nbg = cols(U), cols(U), cols(U), cols(U), cols(U)
        ssq, rms = cols(U), cols(U)
        convw = cols(CONV_K * 3 * H)
        normw = cols(1)
        stats, mv, rstd = cols(4 * 6), cols(4), cols(2)
        aff, selv, top2 = cols(32), cols(32), cols(32)
        gscore, gsel, rank = cols(8), cols(8), cols(8)
        comb, wsum = cols(32), cols(2)
        sel5, rank5 = cols(TT * 5), cols(TT * 5)
        cg, comb5 = cols(5 * EPG), cols(TT * 5 * EPG)
        rbias, cnt, ovf, cgcur = cols(NE), cols(4), cols(4), cols(EPG)

        psum = ctx.enter_context(nc.psum_tensor("psum", [P, 8, 512], F32))
        bank = [psum[:, i, :] for i in range(8)]

        def quads(t):
            return t.rearrange("p (k s) -> p k s", s=P)

        def quad(t, j):
            return t[:, j * P:(j + 1) * P]

        (ident_in, x_in, cst_in, small_in, ln1_in, ln2_in, wr_in, late_in, xres_in) = (sem(n) for n in (
            "ident_in", "x_in", "cst_in", "small_in", "ln1_in", "ln2_in", "wr_in", "late_in", "xres_in"))
        raw_in = [sem(f"raw_in{i}") for i in range(NSLOT)]
        expert_in = [sem(f"expert_in{i}") for i in range(NRAW)]
        hi_done, lo_vector, lo_pool = sem("hi_done"), sem("lo_vector"), sem("lo_pool")
        halves_used = sem("halves_used")
        xt_psum, xh_sb, xl_sb = sem("xt_psum"), sem("xh_sb"), sem("xl_sb")
        cw_psum, cw_sb, pads = sem("cw_psum"), sem("cw_sb"), sem("pads")
        proj_a, proj_sb = sem("proj_a"), sem("proj_sb")
        ba_psum, ba_sb = sem("ba_psum"), sem("ba_sb")
        conv_done, silu_done, sq_done = sem("conv_done"), sem("silu_done"), sem("sq_done")
        ss_psum, rn_done, qk_norm = sem("ss_psum"), sem("rn_done"), sem("qk_norm")
        gb_pre, gb_exp, g_sb = sem("gb_pre"), sem("gb_exp"), sem("g_sb")
        gc_psum, gc_sb, dif_sb, dec_exp, eg_done = (sem(n) for n in (
            "gc_psum", "gc_sb", "dif_sb", "dec_exp", "eg_done"))
        kk_psum, lq_sb, lt_psum, lt_sb, qkt_sb = (sem(n) for n in (
            "kk_psum", "lq_sb", "lt_psum", "lt_sb", "qkt_sb"))
        lev_mask, lev_y, lev_ysb, lev_p, lev_u, lev_tt, lev_t = (sem(n) for n in (
            "lev_mask", "lev_y", "lev_ysb", "lev_p", "lev_u", "lev_tt", "lev_t"))
        vk_psum, vb_sb = sem("vk_psum"), sem("vb_sb")
        u0_psum, u0_sb, s1_psum, s1_sb, ks_psum, r1_sb, qs_sb = (sem(n) for n in (
            "u0_psum", "u0_sb", "s1_psum", "s1_sb", "ks_psum", "r1_sb", "qs_sb"))
        vn_psum, vn_sb, o_psum, o_sb, osq_sb, rms_in, rms_done, on_sb = (sem(n) for n in (
            "vn_psum", "vn_sb", "o_psum", "o_sb", "osq_sb", "rms_in", "rms_done", "on_sb"))
        oat_psum, oah_sb, oal_sb = sem("oat_psum"), sem("oah_sb"), sem("oal_sb")
        z_psum, z_sb, z_masked, s_ln, s_sp, cs_psum, s_t, s_att, av_psum, obh_sb, obl_sb = (sem(n) for n in (
            "z_psum", "z_sb", "z_masked", "s_ln", "s_sp", "cs_psum", "s_t", "s_att", "av_psum", "obh_sb", "obl_sb"))
        pa_psum, pa_sb, pb_psum, msum_sb, mh_sb, ml_sb = (sem(n) for n in (
            "pa_psum", "pa_sb", "pb_psum", "msum_sb", "mh_sb", "ml_sb"))
        mix_psum, var1, rstd1, x1_sb, x1t_psum, x1t_sb = (sem(n) for n in ("mix_psum", "var1", "rstd1", "x1_sb", "x1t_psum", "x1t_sb"))
        lg_psum, aff_sb, r2_init, gsel_sb, rank_psum = (sem(n) for n in (
            "lg_psum", "aff_sb", "r2_init", "gsel_sb", "rank_psum"))
        npass_sb, sel_sb, selt_psum, selt_sb = (sem(n) for n in ("npass_sb", "sel_sb", "selt_psum", "selt_sb"))
        xg_psum, xgh_sb, xgl_sb, cur_sb, cg_sb = (sem(n) for n in ("xg_psum", "xgh_sb", "xgl_sb", "cur_sb", "cg_sb"))
        silu_sb, hid_sb, ht_psum, hth_sb, htl_sb = (sem(n) for n in ("silu_sb", "hid_sb", "ht_psum", "hth_sb", "htl_sb"))
        y_psum, yh_sb, yl_sb, sc_psum, sc_done = (sem(n) for n in ("y_psum", "yh_sb", "yl_sb", "sc_psum", "sc_done"))
        var2, rstd2, out_sb, out_done = sem("var2"), sem("rstd2"), sem("out_sb"), sem("out_done")
        bn_sem = sem("bn_sem")
        dve_steps, act_steps, pool_steps = sem("dve_steps"), sem("act_steps"), sem("pool_steps")
        wbah_sb, wbal_sb, lgt_psum, lgt_sb = sem("wbah_sb"), sem("wbal_sb"), sem("lgt_psum"), sem("lgt_sb")
        zg_silu, gates_sb = sem("zg_silu"), sem("gates_sb")

        x_d = x.rearrange("b (t p) d -> (b t) p d", p=P)
        out_d = out.rearrange("b (t p) d -> (b t) p d", p=P)
        win_d, pa_d, pb_d, wout_d = (w.rearrange("l (k p) n -> (l p) k n", p=P) for w in (w_in, p_a, p_b, w_out))
        expert_d = [w_gate.rearrange("l e (p k) f -> (l e) p (k f)", k=KD),
                    w_up.rearrange("l e (p k) f -> (l e) p (k f)", k=KD),
                    w_down.rearrange("l e (p k) d -> (l e) p (k d)", k=KF)]

        def row(ap):
            return ap.partition_broadcast(P).rearrange("p a d -> p (a d)")

        def s4(t, n):
            return t[:, n % NSLOT, :].rearrange("p (k n) -> p k n", k=4)

        def s2(t, n):
            return t[:, n % NSLOT, :].rearrange("p (k n) -> p k n", k=2)

        def wait_split(eng, n, i=None):
            for lo_part in (lo_vector, lo_pool):
                eng.wait_ge(lo_part, (n + 1) + (0 if i is None else PASS * i))

        def raw_half(n):
            return wraw[:, n % NSLOT, :] if n < PRE else expert_raw[(n - PRE) % NRAW]

        def head_tile(kind, u):
            t, h = u // H, u % H
            return qkvT[:, kind * H + h, t * P:(t + 1) * P]

        def unit_bank(u):
            return u % 4 if u < STICK_UNIT else u % 2

        kkb, qkb = [bank[7], bank[4]], [bank[5], bank[6]]
        block = ctx.enter_context(nc.Block())

        @block.sync
        def _(sp):
            for t in range(TT):
                sp.dma_start(x0[:, t, :], x_d[t]).then_inc(x_in, 16)
            for n in range(PRE):
                if n >= NSLOT:
                    wait_split(sp, n - NSLOT)
                if n < PB0:
                    a, h = BLOCKS[n // 2][0], n % 2
                    src = win_d[:, 4 * h:4 * h + 4, a:a + 512]
                else:
                    w, m = [(pb_d, n - PB0), (pa_d, n - PA0), (wout_d, n - WO0)][min((n - PB0) // 2, 2)]
                    src = w[:, 2 * m:2 * m + 2, :]
                dst = s4(wraw, n) if n < PB0 else s2(wraw, n)
                sp.dma_start(dst, src).then_inc(raw_in[n % NSLOT], 16)
                if n == WO0:
                    sp.wait_ge(halves_used, 2 * NB)
                    for t in range(TT):
                        sp.dma_start(xres[:, t, :], x_d[t]).then_inc(xres_in, 16)

            def half_load(n, group):
                j, w = PASS_ORDER[(n - PRE) // 2]
                h = (n - PRE) % 2
                sp.dma_start(raw_half(n), expert_d[w][bass.ds(group * EPG + j, 1), :, h * HALF:(h + 1) * HALF]
                             .rearrange("e p n -> (e p) n")).then_inc(expert_in[(n - PRE) % NRAW], 16)

            def pass_loads(i, group):
                for n in range(PRE, PRE + PASS):
                    wait_split(sp, n - NRAW, i)
                    half_load(n, group)

            sp.wait_ge(halves_used, PB0 + 2)
            half_load(PRE, 0)
            sp.wait_ge(on_sb, 2)
            for n in range(PRE + 1, PRE + PASS):
                if n >= PRE + NRAW:
                    wait_split(sp, n - NRAW)
                elif n >= PRE + NSLOT:
                    wait_split(sp, WO0 + n - (PRE + NSLOT))
                half_load(n, 0)
            with sp.Fori(1, NG - 1) as i:
                pass_loads(i, i)
            sp.wait_ge(npass_sb, 1)
            npass = sp.value_load(small_i[0:1, 0:1], min_val=NG, max_val=NPASS_MAX)
            with sp.Fori(NG - 1, npass) as i:
                group = sp.value_load(small_i[0:1, bass.ds(i, 1)], min_val=0, max_val=NG - 1)
                pass_loads(i, group)
            for t in range(TT):
                sp.wait_ge(out_sb, t + 1)
                sp.dma_start(out_d[t], r2[:, t, :]).then_inc(out_done, 16)
            sp.wait_ge(out_done, 16 * TT)

        @block.tensor
        def _(pe):
            mm, tr = nc.tensor.matmul, nc.tensor.transpose

            def mm3(o, wh, wl, vh, vl, start, stop):
                mm(o, wh, vh, start=start, stop=False)
                mm(o, wh, vl, start=False, stop=False)
                return mm(o, wl, vh, start=False, stop=stop)

            pe.wait_ge(ident_in, 16)
            pe.wait_ge(x_in, 16 * TT)
            for t in range(TT):
                for half in range(2):
                    for k in range(4):
                        last = tr(quad(bank[2 * t + half], k), quad(x0[:, t, :], 4 * half + k), ident)
                    last.then_inc(xt_psum, 1)
            pe.wait_ge(xl_sb, 4)

            def project(b, part, only=None):
                u = 2 * b + part
                o = bank[unit_bank(u)]
                channel_major = BLOCKS[b][1] not in ("sv", "z")
                if only != 1:
                    if u < STICK_UNIT and u >= 4:
                        pe.wait_ge(proj_sb, u - 3)
                    elif u >= STICK_UNIT:
                        pe.wait_ge(proj_sb, u - 1)
                for sub in range(2 if channel_major else 1) if only is None else (only,):
                    a = (2 * part + sub) * P
                    for k in range(KD):
                        n = 2 * b + k // 4
                        if k % 4 == 0 and part == 0 and sub == 0:
                            wait_split(pe, n)
                        fl = dict(start=(k == 0), stop=(k == KD - 1))
                        if channel_major:
                            last = mm3(o[:, sub * S:(sub + 1) * S], s4(whi, n)[:, k % 4, a:a + P],
                                       s4(wlo, n)[:, k % 4, a:a + P], xh[:, k, :], xl[:, k, :], **fl)
                        else:
                            t = slice(part * P, (part + 1) * P)
                            last = mm3(o, xh[:, k, t], xl[:, k, t], s4(whi, n)[:, k % 4, :],
                                       s4(wlo, n)[:, k % 4, :], **fl)
                        final = sub == 1 or not channel_major
                        if final and part == 1 and k % 4 == 3:
                            last.then_inc(halves_used, 1)
                        elif final and part == 0 and k == KD - 1:
                            last.then_inc(proj_a, 1)

            def level_y(n):
                pe.wait_ge(lev_mask, n)
                for half in range(2):
                    pe.wait_ge(lev_t, 2 * (n - 1) + half + 1)
                    if n == 1:
                        pe.wait_ge(vb_sb, 1)
                    for j in range(4):
                        u = 4 * half + j
                        last = mm(quad(bank[4 + 2 * half], j), CM[:, u, :], T[:, u, :], start=True, stop=True)
                    last.then_inc(lev_y, 1)

            def level_p(n):
                for half in range(2):
                    pe.wait_ge(lev_ysb, 2 * (n - 1) + half + 1)
                    pe.wait_ge(lev_u, 2 * (n - 1) + half + 1)
                    for j in range(4):
                        u = 4 * half + j
                        last = mm(quad(bank[5 + 2 * half], j), Y[:, u, :], UT[:, u, :], start=True, stop=True)
                    last.then_inc(lev_p, 1)

            def level_t(n):
                for half in range(2):
                    pe.wait_ge(lev_u, 2 * n + half + 1)
                    for j in range(4):
                        u = 4 * half + j
                        last = tr(quad(bank[4 + 2 * half], j), UT[:, u, :], ident)
                    last.then_inc(lev_tt, 1)

            def scores(g):
                if g == 0:
                    pe.wait_ge(proj_sb, STICK_UNIT)
                else:
                    pe.wait_ge(obl_sb, g)
                for e in range(2):
                    rows = slice(e * DH, (e + 1) * DH)
                    mm(bank[2 + e][:, 0:S], skT[rows, g, 0:P], sqT[rows, g, 0:S], start=True, stop=True)
                    last = mm(bank[2 + e][:, S:S + P], skT[rows, g, P:S], sqT[rows, g, P:S], start=True, stop=True)
                last.then_inc(z_psum, 1)

            def key_sums(g):
                pe.wait_ge(s_sp, g + 1)
                for e in range(2):
                    spv = stick[:, 1, e, :]
                    mm(bank[2 + e][:, 0:S], tril, spv[:, 0:S], start=True, stop=False)
                    mm(bank[2 + e][:, P:S], ones, spv[:, S:S + P], start=False, stop=True)
                    last = mm(bank[2 + e][:, S:S + P], tril, spv[:, S:S + P], start=True, stop=True)
                last.then_inc(cs_psum, 1)

            def values(g):
                pe.wait_ge(s_att, g + 1)
                for e in range(2):
                    h = 2 * g + e
                    att = stick[:, 2, e, :]
                    o = bank[2][e * DH:(e + 1) * DH, :]
                    mm(o[:, 0:S], sv[:, 0, h * DH:(h + 1) * DH], att[:, 0:S], start=True, stop=False)
                    last = mm(o[:, P:S], sv[:, 1, h * DH:(h + 1) * DH], att[:, S:S + P], start=False, stop=True)
                last.then_inc(av_psum, 1)

            project(0, 0)
            pe.wait_ge(small_in, 16 * 5)
            nrow = CONV_K * 3 * H
            tr(bank[4][:, 0:nrow], cwrow[0:nrow, :], cst[0:nrow, C_IDENT:C_IDENT + nrow]).then_inc(cw_psum, 1)
            project(0, 1)
            project(1, 0)
            project(1, 1)
            pe.wait_ge(cw_sb, 1)
            pe.wait_ge(wbal_sb, 1)
            for k in range(KD):
                last = mm3(bank[4][0:8, 0:S], wbah[:, k, :], wbal[:, k, :], xh[:, k, :], xl[:, k, :],
                           start=(k == 0), stop=(k == KD - 1))
            last.then_inc(ba_psum, 1)
            project(2, 0)
            pe.wait_ge(ba_sb, 1)
            for t in range(TT):
                last = tr(bank[4][:, S + t * 8:S + t * 8 + 8], baT[0:8, t * P:(t + 1) * P], cst[0:8, C_IDENT:C_IDENT + 8])
            last.then_inc(ba_psum, 1)
            project(2, 1)
            project(3, 0)
            project(3, 1)
            pe.wait_ge(ba_sb, 2)
            pe.wait_ge(cst_in, 16)
            for i in range(4):
                pe.wait_ge(sq_done, i // 2 + 1)
                mm(bank[4 + i], ones, sqq[:, i * 512:(i + 1) * 512], start=True, stop=True).then_inc(ss_psum, 1)
            project(4, 0)
            project(4, 1)
            pe.wait_ge(g_sb, 1)
            pe.wait_ge(rn_done, 1)
            mm(bank[4][:, 0:U], triu, gg, start=True, stop=True)
            mm(bank[4][:, U:2 * U], ones, gg, start=True, stop=True).then_inc(gc_psum, 1)
            for u in range(U):
                last = mm(quad(bank[5 + u // 4], u % 4), GB[:, u, :], triu, start=True, stop=True)
            last.then_inc(gc_psum, 1)
            project(5, 0)
            project(5, 1)
            pe.wait_ge(qk_norm, 1)
            pe.wait_ge(dif_sb, 1)
            for u in range(U):
                last = mm(quad(kkb[u // 4], u % 4), head_tile(1, u), head_tile(1, u), start=True, stop=True)
            last.then_inc(kk_psum, 1)
            for u in range(U):
                last = mm(quad(qkb[u // 4], u % 4), head_tile(0, u), head_tile(1, u), start=True, stop=True)
            last.then_inc(kk_psum, 1)
            scores(0)
            project(6, 0)
            pe.wait_ge(lq_sb, 1)
            for u in range(U):
                last = tr(quad(kkb[u // 4], u % 4), L[:, u, :], ident)
            last.then_inc(lt_psum, 1)
            pe.wait_ge(lq_sb, 2)
            for u in range(U):
                last = tr(quad(qkb[u // 4], u % 4), QKT[:, u, :], ident)
            last.then_inc(lt_psum, 1)
            key_sums(0)
            project(6, 1)
            values(0)
            pe.wait_ge(lt_sb, 1)
            pe.wait_ge(qkt_sb, 1)
            for u in range(U):
                last = tr(quad(bank[5 + 2 * (u // H)], u % H), head_tile(2, u), ident)
            for h in range(H):
                last = tr(quad(bank[4], h), head_tile(1, h), ident)
            last.then_inc(vk_psum, 1)
            scores(1)
            project(7, 0)
            level_y(1)
            project(7, 1, 0)
            key_sums(1)
            level_p(1)
            project(7, 1, 1)
            values(1)
            level_y(2)
            scores(2)
            project(8, 0, 0)
            level_p(2)
            project(8, 0, 1)
            level_y(3)
            key_sums(2)
            project(8, 1, 0)
            level_p(3)
            values(2)
            project(8, 1, 1)
            level_y(4)
            scores(3)
            project(9, 0, 0)
            level_p(4)
            project(9, 0, 1)
            level_y(5)
            key_sums(3)
            project(9, 1, 0)
            level_p(5)
            values(3)
            project(9, 1, 1)
            level_t(5)
            level_y(6)
            project(10, 0, 0)
            level_p(6)
            project(10, 0, 1)

            def project_branch(n0, bh, bl, first_bank, pair, psum_sem):
                if pair == 0:
                    wait_split(pe, n0)
                    wait_split(pe, n0 + 1)
                for sub in range(2):
                    a = (2 * pair + sub) * P
                    for j in range(4):
                        n = n0 + j // 2
                        last = mm3(bank[first_bank + pair][:, sub * S:(sub + 1) * S],
                                   s2(whi, n)[:, j % 2, a:a + P], s2(wlo, n)[:, j % 2, a:a + P],
                                   bh[:, j, :], bl[:, j, :], start=(j == 0), stop=(j == 3))
                        if pair == 3 and sub == 1 and j % 2 == 1:
                            last.then_inc(halves_used, 1)
                if pair < 3:
                    last.then_inc(psum_sem, 1)

            def branch_b(pair):
                project_branch(PB0, obh, obl, 0, pair, pb_psum)

            pe.wait_ge(lev_u, 13)
            for h in range(H):
                last = mm(quad(bank[6], h), UT[:, h, :], VB[:, h, :], start=True, stop=True)
            last.then_inc(u0_psum, 1)
            project(10, 1, 0)
            pe.wait_ge(u0_sb, 1)
            for h in range(H):
                last = mm(quad(bank[4], h), KDEC[:, h, :], U0[:, h, :], start=True, stop=True)
            last.then_inc(s1_psum, 1)
            for h in range(H):
                last = mm(quad(bank[5], h), QKT[:, h, :], U0[:, h, :], start=True, stop=True)
            last.then_inc(o_psum, 1)
            project(10, 1, 1)
            pe.wait_ge(s1_sb, 1)
            pe.wait_ge(lev_u, 14)
            for h in range(H):
                last = mm(quad(bank[6], h), head_tile(1, H + h), S1[:, h, :], start=True, stop=True)
            last.then_inc(ks_psum, 1)
            for h in range(H):
                last = mm(quad(bank[7], h), head_tile(0, H + h), S1[:, h, :], start=True, stop=True)
            last.then_inc(ks_psum, 1)
            pe.wait_ge(obl_sb, 4)
            pe.wait_ge(proj_sb, 2 * NB)
            branch_b(0)
            pe.wait_ge(r1_sb, 1)
            for h in range(H):
                last = mm(quad(bank[4], h), UT[:, H + h, :], R1[:, h, :], start=True, stop=True)
            last.then_inc(vn_psum, 1)
            branch_b(1)
            pe.wait_ge(vn_sb, 1)
            for h in range(H):
                last = mm(quad(bank[6], h), QKT[:, H + h, :], VN[:, h, :], start=True, stop=True)
            last.then_inc(o_psum, 1)
            branch_b(2)

            def branch_a_t(t):
                pe.wait_ge(on_sb, t + 1)
                for h in range(H):
                    last = tr(quad(bank[5 + 2 * t], h), ON[:, t * H + h, :], ident)
                last.then_inc(oat_psum, 1)

            branch_a_t(0)
            branch_b(3)
            branch_a_t(1)
            pe.wait_ge(oal_sb, 2)
            for pair in range(4):
                project_branch(PA0, oah, oal, 4, pair, pa_psum)
            def mix(t, hs, half):
                for kk in range(2):
                    k = 2 * hs + kk
                    ts, cs_ = slice(t * P, (t + 1) * P), slice(half * 512, (half + 1) * 512)
                    last = mm3(bank[2 * t + half], mh[:, k, ts], ml[:, k, ts], s2(whi, WO0 + hs)[:, kk, cs_],
                               s2(wlo, WO0 + hs)[:, kk, cs_], start=(k == 0), stop=(k == KD - 1))
                return last

            for hs in range(4):
                wait_split(pe, WO0 + hs)
                pe.wait_ge(ml_sb, hs + 1)
                for half in range(2):
                    last = mix(0, hs, half)
            last.then_inc(mix_psum, 1)
            for hs in range(4):
                last = mix(1, hs, 0)
            last.then_inc(mix_psum, 1)

            def x1k(t):
                return xres[:, t, :].rearrange("s (p k) -> s k p", k=KD)

            def x1_transposed(t):
                pe.wait_ge(x1_sb, t + 1)
                for half in range(2):
                    for k in range(4):
                        last = tr(quad(bank[2 * t + half], k), x1k(t)[:, 4 * half + k, :], ident)
                    last.then_inc(x1t_psum, 1)

            def logits(t):
                pe.wait_ge(x1t_sb, 2 * t + 2)
                for k in range(KD):
                    last = mm(bank[4 + t][0:NE, 0:P], wr[:, k, :], x1T[:, k, t * P:(t + 1) * P],
                              start=(k == 0), stop=(k == KD - 1))
                last.then_inc(lgt_psum, 1)

            x1_transposed(0)
            for hs in range(4):
                mix(1, hs, 1).then_inc(halves_used, 1)
            logits(0)
            x1_transposed(1)
            logits(1)
            for t in range(TT):
                pe.wait_ge(lgt_sb, t + 1)
                last = tr(bank[6][:, t * NE:(t + 1) * NE], lgt[0:NE, t * P:(t + 1) * P], cst[0:NE, C_IDENT:C_IDENT + NE])
            last.then_inc(lg_psum, 1)
            pe.wait_ge(gsel_sb, 1)
            mm(bank[5][:, 0:4], sup, gsel[:, 0:4], start=True, stop=True)
            mm(bank[5][:, 4:8], ones, gsel[:, 0:4], start=True, stop=False)
            mm(bank[5][:, 4:8], sup, gsel[:, 4:8], start=False, stop=True)
            mm(bank[5][:, 8:12], ones, gsel[:, 0:4], start=True, stop=False)
            mm(bank[5][:, 8:12], ones, gsel[:, 4:8], start=False, stop=True).then_inc(rank_psum, 1)

            def gather(i):
                for half in range(2):
                    for k in range(4):
                        for t in range(TT):
                            last = mm(quad(bank[7 - 7 * half], k), x1k(t)[:, 4 * half + k, :],
                                      SEL[:, bass.ds(i, 1), t, :].rearrange("p n s -> p (n s)"),
                                      start=(t == 0), stop=(t == TT - 1))
                    last.then_inc(xg_psum, 1)

            pe.wait_ge(sel_sb, 1)
            gather(0)
            pe.wait_ge(sel_sb, 2)
            for n in range(5):
                for t in range(TT):
                    last = tr(bank[1 + n // 2][:, (n % 2) * S + t * P:(n % 2) * S + (t + 1) * P], SEL[:, n, t, :], ident)
            last.then_inc(selt_psum, 1)
            for n in range(5):
                for t in range(TT):
                    last = mm(bank[6][:, n * EPG:(n + 1) * EPG], SEL[:, n, t, :],
                              comb5[:, (t * 5 + n) * EPG:(t * 5 + n + 1) * EPG], start=(t == 0), stop=(t == TT - 1))
            last.then_inc(selt_psum, 1)
            pe.wait_ge(npass_sb, 1)
            before_last = pe.value_load(small_i[0:1, 1:2], min_val=NG - 1, max_val=NPASS_MAX - 1)

            def expert_pass(i, last_pass):
                def half_ready(n):
                    wait_split(pe, n, i)

                def gate_or_up(m):
                    j, w = PASS_ORDER[m]
                    for h in range(2):
                        n = PRE + 2 * m + h
                        half_ready(n)
                        for k in range(4):
                            kt = 4 * h + k
                            last = mm3(bank[2 * (j % 2) + w], xgh[:, kt, :], xgl[:, kt, :], s4(whi, n)[:, k, :],
                                       s4(wlo, n)[:, k, :], start=(kt == 0), stop=(kt == KD - 1))
                        last.then_inc(halves_used, 1)

                def transposes(j):
                    pe.wait_ge(hid_sb, i * 4 + (j + 1))
                    hk = hid[:, :].rearrange("s (p k) -> s k p", k=KF)
                    for k in range(KF):
                        last = tr(quad(bank[4], k), hk[:, k, :], ident)
                    last.then_inc(ht_psum, 1)

                def down(m):
                    j = PASS_ORDER[m][0]
                    pe.wait_ge(htl_sb, i * 4 + (j + 1))
                    for h in range(2):
                        n = PRE + 2 * m + h
                        half_ready(n)
                        for o in range(2):
                            for kk in range(2):
                                k = 2 * h + kk
                                last = mm3(bank[5 + o], hth[:, k, :], htl[:, k, :], s2(whi, n)[:, kk, o * 512:(o + 1) * 512],
                                           s2(wlo, n)[:, kk, o * 512:(o + 1) * 512], start=(j == 0 and k == 0), stop=False)
                        last.then_inc(halves_used, 1)

                def last_down(m):
                    pe.wait_ge(htl_sb, i * 4 + 4)
                    for h in range(2):
                        n = PRE + 2 * m + h
                        half_ready(n)
                        for o in range(2):
                            for kk in range(2):
                                k = 2 * h + kk
                                last = mm3(bank[5 + o], hth[:, k, :], htl[:, k, :], s2(whi, n)[:, kk, o * 512:(o + 1) * 512],
                                           s2(wlo, n)[:, kk, o * 512:(o + 1) * 512], start=False, stop=(k == KF - 1))
                            if h == 1 and o == 0:
                                last.then_inc(y_psum, 1)
                        last.then_inc(halves_used, 1)

                pe.wait_ge(xgl_sb, i * 2 + 2)
                gate_or_up(0)
                pe.wait_ge(selt_sb, 1)
                gate_or_up(1)
                gate_or_up(2)
                transposes(0)
                gate_or_up(3)
                down(4)
                gate_or_up(5)
                transposes(1)
                gate_or_up(6)
                down(7)
                gate_or_up(8)
                transposes(2)
                gate_or_up(9)
                down(10)
                transposes(3)
                if not last_pass:
                    gather(i + 1)
                last_down(11)
                pe.wait_ge(cur_sb, i + 1)
                if not last_pass:
                    pe.wait_ge(xgl_sb, i * 2 + 4)
                for o in range(2):
                    pe.wait_ge(yl_sb, i * 2 + (o + 1))
                    for t in range(TT):
                        b = bank[[7, 4, 5, 6][2 * o + t]]
                        ts, os_ = slice(t * P, (t + 1) * P), slice(o * 512, (o + 1) * 512)
                        mm(b, selt_cur[:, ts], yh[:, os_], start=True, stop=False)
                        mm(b, selt_cur[:, ts], yl[:, os_], start=False, stop=True).then_inc(sc_psum, 1)

            with pe.Fori(0, before_last) as i:
                expert_pass(i, False)
            expert_pass(before_last, True)

        @block.scalar
        def _(act):
            steps = Steps(act, act_steps)
            a_ = nc.scalar.activation
            act.dma_start(cst[:, 0:P], consts[:, 0:P]).then_inc(ident_in, 16)
            act.dma_start(cwrow[0:CONV_K * 3 * H, :], conv_w.rearrange("l k (j c) -> (l k j) c", c=P)).then_inc(small_in, 16)
            act.dma_start(wba, win_d[:, :, BA_COL:BA_COL + 8]).then_inc(small_in, 16)
            act.dma_start(alog, row(dn_a_log)).then_inc(small_in, 16)
            act.dma_start(dtb, row(dn_dt_bias)).then_inc(small_in, 16)
            act.dma_start(normw, dn_norm_w.rearrange("l (p o) -> (l p) o", o=1)).then_inc(small_in, 16)
            for t in range(TT):
                for half in range(2):
                    act.wait_ge(xt_psum, 2 * t + half + 1)
                    nc.scalar.copy(xh[:, 4 * half:4 * half + 4, t * P:(t + 1) * P],
                                   quads(bank[2 * t + half])).then_inc(xh_sb, 1)

            def to_hi(n, i=None):
                if n < PRE:
                    act.wait_ge(raw_in[n % NSLOT], 16 * (n // NSLOT + 1))
                else:
                    m = n - PRE
                    turns = 0 if i is None else (PASS // NRAW * 16) * i
                    act.wait_ge(expert_in[m % NRAW], turns + 16 * (m // NRAW + 1))
                if n >= NSLOT:
                    act.wait_ge(halves_used, (n - NSLOT + 1) + (0 if i is None else PASS * i))
                nc.scalar.copy(whi[:, n % NSLOT, :], raw_half(n)).then_inc(hi_done, 1)

            def block_hi(b):
                to_hi(2 * b)
                to_hi(2 * b + 1)

            def evacuate(b, part):
                kind = BLOCKS[b][1]
                u = 2 * b + part
                o = bank[unit_bank(u)]
                o2 = o.rearrange("p (a s) -> p a s", a=2)
                if part == 0:
                    act.wait_ge(proj_a, b + 1)
                else:
                    act.wait_ge(halves_used, 2 * b + 2)
                a = slice(2 * part, 2 * part + 2)
                if kind == "qkv":
                    if u == 0:
                        act.wait_ge(pads, 1)
                    if b == 2:
                        act.wait_ge(conv_done, 1)
                    ins = nc.scalar.copy(raw[:, b % 2, a, 3:3 + S], o2)
                elif kind == "sq":
                    ins = nc.scalar.mul(sqT[:, a, :], o2, DH ** -0.5)
                elif kind == "sk":
                    ins = nc.scalar.copy(skT[:, a, :], o2)
                elif kind == "sv":
                    ins = nc.scalar.copy(sv[:, part, :], o)
                elif kind == "z":
                    ins = nc.scalar.copy(zg[:, part * 512:(part + 1) * 512], o)
                else:
                    g = 4 * (b - 7) + 2 * part
                    ins = nc.scalar.copy(gates[:, g:g + 2, :], o2)
                ins.then_inc(proj_sb, 1)

            def silu_block(blk):
                act.wait_ge(conv_done, blk + 1)
                v = qkvT[:, 4 * blk:4 * blk + 4, :]
                a_(v, v, ACT.Silu).then_inc(silu_done, 1)
                if blk < 2:
                    act.wait_ge(silu_done, blk + 1)
                    if blk == 0:
                        act.wait_ge(cw_psum, 1)
                    dst = sqq[:, blk * D:(blk + 1) * D].rearrange("p (a s) -> p a s", a=4)
                    a_(dst, v, ACT.Square).then_inc(sq_done, 1)

            block_hi(0)
            block_hi(1)
            act.dma_start(cst[:, P:], consts[:, P:NCONST]).then_inc(cst_in, 16)
            act.wait_ge(small_in, 16 * 5)
            nc.scalar.copy(wbah[:, :, :], wba).then_inc(wbah_sb, 1)
            evacuate(0, 0)
            evacuate(0, 1)
            block_hi(2)
            evacuate(1, 0)
            evacuate(1, 1)
            block_hi(3)
            act.wait_ge(ba_psum, 1)
            nc.scalar.copy(baT[0:8, :], bank[4][0:8, 0:S]).then_inc(ba_sb, 1)
            silu_block(0)
            act.wait_ge(ba_psum, 2)
            nc.scalar.copy(ba, bank[4][:, S:S + 16]).then_inc(ba_sb, 1)
            evacuate(2, 0)
            evacuate(2, 1)
            block_hi(4)
            silu_block(1)
            evacuate(3, 0)
            silu_block(2)
            evacuate(3, 1)
            block_hi(5)
            act.wait_ge(gb_pre, 1)
            a_(gb2, gb2, ACT.Exp)
            a_(nalog, alog, ACT.Exp)
            steps.then(a_(gb1, gg, ACT.Abs))
            steps.then(a_(gb1, gb1, ACT.Exp, scale=-1.0))
            a_(gb1, gb1, ACT.Ln, bias=1.0).then_inc(gb_exp, 1)
            act.wait_ge(cst_in, 16)
            act.wait_ge(ss_psum, 4)
            steps.then(a_(rn[:, :].rearrange("p (b s) -> p b s", b=4), psum[:, 4:8, :], ACT.Ln,
                          bias=cst[:, C_SMALL:C_SMALL + 1]))
            a_(rn[:, :], rn[:, :], ACT.Exp, scale=-0.5).then_inc(rn_done, 1)
            evacuate(4, 0)
            evacuate(4, 1)
            block_hi(6)
            act.wait_ge(dif_sb, 1)
            a_(DEC[:, :, :], DEC[:, :, :], ACT.Exp, scale=-1.0).then_inc(dec_exp, 1)
            a_(expg, gcum, ACT.Exp)
            a_(kdc, kdc, ACT.Exp).then_inc(eg_done, 1)
            def y_sb(n):
                for half in range(2):
                    act.wait_ge(lev_y, 2 * (n - 1) + half + 1)
                    nc.scalar.copy(Y[:, 4 * half:4 * half + 4, :], quads(bank[4 + 2 * half])).then_inc(lev_ysb, 1)

            def t_sb():
                for half in range(2):
                    act.wait_ge(lev_tt, half + 1)
                    nc.scalar.copy(T[:, 4 * half:4 * half + 4, :], quads(bank[4 + 2 * half])).then_inc(lev_t, 1)

            def scores_sb(g):
                act.wait_ge(z_psum, g + 1)
                if g >= 1:
                    act.wait_ge(s_t, g)
                nc.scalar.copy(stick[:, 0, :, :], psum[:, 2:4, 0:384]).then_inc(z_sb, 1)

            def softplus(g):
                act.wait_ge(z_masked, g + 1)
                e_buf = stick[:, 1, :, :]
                steps.then(a_(e_buf, stick[:, 0, :, :], ACT.Abs))
                steps.then(a_(e_buf, e_buf, ACT.Exp, scale=-1.0))
                a_(e_buf, e_buf, ACT.Ln, bias=1.0).then_inc(s_ln, 1)

            def attention(g):
                act.wait_ge(s_t, g + 1)
                a_(stick[:, 2, :, :], stick[:, 2, :, :], ACT.Exp).then_inc(s_att, 1)

            def branch_b(g):
                act.wait_ge(av_psum, g + 1)
                nc.scalar.copy(obh[:, g, :], bank[2][:, 0:S]).then_inc(obh_sb, 1)

            evacuate(5, 0)
            evacuate(5, 1)
            scores_sb(0)
            to_hi(14)
            softplus(0)
            to_hi(15)
            evacuate(6, 0)
            act.wait_ge(lt_psum, 1)
            nc.scalar.copy(LT[:, 0:4, :], quads(bank[7]))
            nc.scalar.copy(LT[:, 4:8, :], quads(bank[4])).then_inc(lt_sb, 1)
            act.wait_ge(lt_psum, 2)
            nc.scalar.copy(QKT[:, :, :].rearrange("p (b j) c -> p b (j c)", b=2), psum[:, 5:7, :]).then_inc(qkt_sb, 1)
            attention(0)
            evacuate(6, 1)
            branch_b(0)
            to_hi(16)
            scores_sb(1)
            to_hi(17)
            softplus(1)
            evacuate(7, 0)
            y_sb(1)
            attention(1)
            evacuate(7, 1)
            branch_b(1)
            y_sb(2)
            scores_sb(2)
            to_hi(18)
            softplus(2)
            evacuate(8, 0)
            y_sb(3)
            attention(2)
            to_hi(19)
            branch_b(2)
            evacuate(8, 1)
            y_sb(4)
            scores_sb(3)
            to_hi(20)
            softplus(3)
            evacuate(9, 0)
            y_sb(5)
            attention(3)
            to_hi(21)
            branch_b(3)
            evacuate(9, 1)
            t_sb()
            y_sb(6)
            to_hi(PB0)
            evacuate(10, 0)
            to_hi(PB0 + 1)
            act.wait_ge(u0_psum, 1)
            nc.scalar.copy(U0[:, :, :], quads(bank[6])).then_inc(u0_sb, 1)
            act.wait_ge(proj_sb, 14)
            a_(zg[:, :], zg[:, :], ACT.Silu).then_inc(zg_silu, 1)
            act.wait_ge(s1_psum, 1)
            nc.scalar.copy(S1[:, :, :], quads(bank[4])).then_inc(s1_sb, 1)
            evacuate(10, 1)

            def output_squares(t):
                act.wait_ge(o_sb, t + 1)
                a_(OSQ[:, t * H:(t + 1) * H, :], O[:, t * H:(t + 1) * H, :], ACT.Square).then_inc(osq_sb, 1)

            output_squares(0)
            act.wait_ge(ks_psum, 2)
            for h in range(H):
                ins = nc.scalar.mul(QS[:, h, :], quad(bank[7], h), expg[:, H + h:H + h + 1])
            ins.then_inc(qs_sb, 1)
            to_hi(PA0)
            act.wait_ge(vn_psum, 1)
            nc.scalar.copy(VN[:, :, :], quads(bank[4])).then_inc(vn_sb, 1)
            act.wait_ge(proj_sb, 2 * NB)
            a_(gates[:, KD:2 * KD, :], gates[:, KD:2 * KD, :], ACT.Sigmoid).then_inc(gates_sb, 1)
            output_squares(1)

            def branch_a_hi(t):
                act.wait_ge(oat_psum, t + 1)
                nc.scalar.mul(oah[:, :, t * P:(t + 1) * P], quads(bank[5 + 2 * t]), normw).then_inc(oah_sb, 1)

            branch_a_hi(0)
            to_hi(PA0 + 1)
            a_(gates[:, 0:KD, :], gates[:, 0:KD, :], ACT.Sigmoid).then_inc(gates_sb, 1)
            branch_a_hi(1)
            act.dma_start(lnp[:, 0, :], row(ln1_g)).then_inc(ln1_in, 16)
            act.dma_start(lnp[:, 1, :], row(ln1_b)).then_inc(ln1_in, 16)
            act.dma_start(rbias, router_bias.partition_broadcast(P)).then_inc(late_in, 16)
            act.dma_start(late[:, :], consts[:, NCONST:NTABLE]).then_inc(late_in, 16)
            act.dma_start(wr[:, :, :], w_router.rearrange("(p k) e -> p k e", k=KD)).then_inc(wr_in, 16)
            to_hi(WO0)
            to_hi(WO0 + 1)
            for pair in range(4):
                act.wait_ge(msum_sb, pair + 1)
                nc.scalar.copy(mh[:, 2 * pair:2 * pair + 2, :],
                               msum[:, pair % 2, :].rearrange("p (a s) -> p a s", a=2)).then_inc(mh_sb, 1)
            to_hi(WO0 + 2)
            to_hi(WO0 + 3)
            act.wait_ge(wr_in, 16)
            for t in range(TT):
                for half in range(2):
                    act.wait_ge(x1t_psum, 2 * t + half + 1)
                    nc.scalar.copy(x1T[:, 4 * half:4 * half + 4, t * P:(t + 1) * P],
                                   quads(bank[2 * t + half])).then_inc(x1t_sb, 1)
                if t == 0:
                    for h in range(4):
                        to_hi(PRE + h)
                act.wait_ge(lgt_psum, t + 1)
                a_(lgt[0:NE, t * P:(t + 1) * P], bank[4 + t][0:NE, 0:P], ACT.Sigmoid).then_inc(lgt_sb, 1)
            act.wait_ge(x1_sb, 2)
            act.dma_start(lnp[:, 0, :], row(ln2_g)).then_inc(ln2_in, 16)
            act.dma_start(lnp[:, 1, :], row(ln2_b)).then_inc(ln2_in, 16)
            nc.scalar.mul(r2[:, :, :], xres[:, :, :], ALPHA).then_inc(r2_init, 1)

            def xg_hi(i):
                for half in range(2):
                    act.wait_ge(xg_psum, i * 2 + (half + 1))
                    nc.scalar.copy(xgh[:, 4 * half:4 * half + 4, :], quads(bank[7 - 7 * half])).then_inc(xgh_sb, 1)

            xg_hi(0)
            act.wait_ge(selt_psum, 1)
            for n in range(0, 5, 2):
                m = min(2, 5 - n)
                nc.scalar.copy(SELT[:, n:n + m, :], bank[1 + n // 2][:, 0:m * S].rearrange("p (n s) -> p n s", s=S))
            act.wait_ge(selt_psum, 2)
            nc.scalar.copy(cg, bank[6][:, 0:5 * EPG]).then_inc(selt_sb, 1)
            act.wait_ge(npass_sb, 1)
            before_last = act.value_load(small_i[0:1, 1:2], min_val=NG - 1, max_val=NPASS_MAX - 1)

            def expert_pass(i, last_pass):
                def matrix_hi(m):
                    for h in range(2):
                        to_hi(PRE + 2 * m + h, i)

                def silu(j):
                    m = PASS_ORDER.index((j, 0))
                    act.wait_ge(halves_used, PASS * i + (PRE + 2 * (m + 1)))
                    if j >= 1:
                        act.wait_ge(hid_sb, i * 4 + j)
                    a_(silu_g[:, :], bank[2 * (j % 2)], ACT.Silu).then_inc(silu_sb, 1)

                def hid_t(j):
                    act.wait_ge(ht_psum, i * 4 + (j + 1))
                    nc.scalar.copy(hth[:, :, :], quads(bank[4])).then_inc(hth_sb, 1)

                matrix_hi(2)
                silu(0)
                matrix_hi(3)
                hid_t(0)
                matrix_hi(4)
                silu(1)
                matrix_hi(5)
                matrix_hi(6)
                hid_t(1)
                matrix_hi(7)
                silu(2)
                matrix_hi(8)
                matrix_hi(9)
                hid_t(2)
                matrix_hi(10)
                silu(3)
                matrix_hi(11)
                hid_t(3)
                if not last_pass:
                    xg_hi(i + 1)
                    matrix_hi(12)
                for o in range(2):
                    if o == 0:
                        act.wait_ge(y_psum, i + 1)
                    else:
                        act.wait_ge(halves_used, PASS * i + (PRE + PASS))
                    nc.scalar.copy(yh[:, o * 512:(o + 1) * 512], bank[5 + o]).then_inc(yh_sb, 1)
                if not last_pass:
                    matrix_hi(13)

            with act.Fori(0, before_last) as i:
                expert_pass(i, False)
            expert_pass(before_last, True)

        @block.gpsimd
        def _(pool):
            nc.gpsimd.memset(raw[:, :, :, 0:3], 0.0).then_inc(pads, 1)
            steps = Steps(pool, pool_steps)

            def to_lo(n, i=None):
                pool.wait_ge(hi_done, (n + 1) + (0 if i is None else PASS * i))
                s = n % NSLOT
                nc.gpsimd.tensor_tensor(wlo[:, s, LO_CUT:], raw_half(n)[:, LO_CUT:], whi[:, s, LO_CUT:].bitcast(F32),
                                        ALU.subtract).then_inc(lo_pool, 1)

            def level_mask(n):
                if n > 1:
                    pool.wait_ge(lev_y, 2 * (n - 1))
                m = c(C_LEV + n * P).unsqueeze(1).to_broadcast([P, U, P])
                nc.gpsimd.tensor_tensor(CM[:, :, :], LT[:, :, :], m, ALU.mult).then_inc(lev_mask, 1)

            for n in range(15):
                to_lo(n)
            pool.wait_ge(cst_in, 16)
            pool.wait_ge(lt_sb, 1)
            level_mask(1)
            for n in (15, 16, 17):
                to_lo(n)
            level_mask(2)
            level_mask(3)
            to_lo(18)
            level_mask(4)
            to_lo(19)
            to_lo(20)
            level_mask(5)
            to_lo(21)
            level_mask(6)
            to_lo(PB0)
            to_lo(PB0 + 1)
            for t in range(TT):
                pool.wait_ge(rms_in, t + 1)
                hs_ = slice(t * H, (t + 1) * H)
                nc.gpsimd.tensor_tensor(rms[:, hs_], ssq[:, hs_], c(C_SMALL + 1, H), ALU.pow).then_inc(rms_done, 1)
                to_lo(PA0 + t)
            for n in range(WO0, WO0 + 4):
                to_lo(n)
            for t in range(TT):
                pool.wait_ge(var1, t + 1)
                nc.gpsimd.tensor_tensor(rstd[:, t:t + 1], rstd[:, t:t + 1], c(C_SMALL + 1, 1), ALU.pow).then_inc(rstd1, 1)
                for h in range(2):
                    to_lo(PRE + 2 * t + h)
            pool.wait_ge(npass_sb, 1)
            before_last = pool.value_load(small_i[0:1, 1:2], min_val=NG - 1, max_val=NPASS_MAX - 1)
            pool.wait_ge(selt_sb, 1)

            def expert_pass(i, last_pass):
                pool.wait_ge(halves_used, PASS * i + (PRE + 1))
                nc.gpsimd.tensor_copy(selt_cur[:, :], SELT[:, bass.ds(i, 1), :].rearrange("p n s -> p (n s)")).then_inc(cur_sb, 1)
                for n in range(PRE + NSLOT, PRE + PASS + (0 if last_pass else NSLOT)):
                    to_lo(n, i)

            with pool.Fori(0, before_last) as i:
                expert_pass(i, False)
            expert_pass(before_last, True)
            for t in range(TT):
                pool.wait_ge(var2, t + 1)
                nc.gpsimd.tensor_tensor(rstd[:, t:t + 1], rstd[:, t:t + 1], c(C_SMALL + 1, 1), ALU.pow).then_inc(rstd2, 1)

        @block.vector
        def _(dve):
            v = nc.vector
            steps = Steps(dve, dve_steps)

            def to_lo(n, i=None):
                dve.wait_ge(hi_done, (n + 1) + (0 if i is None else PASS * i))
                s = n % NSLOT
                v.tensor_tensor(wlo[:, s, 0:LO_CUT], raw_half(n)[:, 0:LO_CUT], whi[:, s, 0:LO_CUT].bitcast(F32), ALU.subtract).then_inc(lo_vector, 1)

            def block_lo(b):
                to_lo(2 * b)
                to_lo(2 * b + 1)

            def u_update(n):
                for half in range(2):
                    dve.wait_ge(lev_p, 2 * (n - 1) + half + 1)
                    us = UT[:, 4 * half:4 * half + 4, :]
                    v.tensor_tensor(us, us, quads(bank[5 + 2 * half]), ALU.subtract).then_inc(lev_u, 1)
                    if n <= 4:
                        dve.wait_ge(lev_u, 2 * n + half + 1)
                        hs_ = slice(4 * half, 4 * half + 4)
                        v.transpose(T[:, hs_, :].rearrange("p u c -> p (u c)"),
                                    UT[:, hs_, :].rearrange("p u c -> p (u c)")).then_inc(lev_t, 1)

            def mask_scores(g):
                dve.wait_ge(z_sb, g + 1)
                diag = stick[:, 0, :, :].rearrange("p e (b s) -> p e b s", s=P)[:, :, 0:3:2, :]
                v.tensor_tensor(diag, diag, neg.unsqueeze(1).unsqueeze(1).to_broadcast([P, 2, 2, P]),
                                ALU.add).then_inc(z_masked, 1)

            def softplus(g):
                dve.wait_ge(z_masked, g + 1)
                dve.wait_ge(s_ln, g + 1)
                v.scalar_tensor_tensor(stick[:, 1, :, :], stick[:, 0, :, :], 0.0, stick[:, 1, :, :],
                                       ALU.max, ALU.add).then_inc(s_sp, 1)

            def exponents(g):
                dve.wait_ge(cs_psum, g + 1)
                if g >= 1:
                    dve.wait_ge(av_psum, g)
                v.tensor_tensor(stick[:, 2, :, :], stick[:, 0, :, :], psum[:, 2:4, 0:384], ALU.subtract).then_inc(s_t, 1)

            def branch_b(g):
                dve.wait_ge(obh_sb, g + 1)
                v.tensor_tensor(obl[:, g, :], bank[2][:, 0:S], obh[:, g, :].bitcast(F32), ALU.subtract).then_inc(obl_sb, 1)

            for t in range(TT):
                for half in range(2):
                    dve.wait_ge(xh_sb, 2 * t + half + 1)
                    ks, ts = slice(4 * half, 4 * half + 4), slice(t * P, (t + 1) * P)
                    v.tensor_tensor(xl[:, ks, ts], quads(bank[2 * t + half]), xh[:, ks, ts].bitcast(F32),
                                    ALU.subtract).then_inc(xl_sb, 1)
            block_lo(0)
            block_lo(1)
            dve.wait_ge(small_in, 16 * 5)
            dve.wait_ge(wbah_sb, 1)
            v.tensor_tensor(wbal[:, :, :], wba, wbah[:, :, :].bitcast(F32), ALU.subtract).then_inc(wbal_sb, 1)
            dve.wait_ge(cw_psum, 1)
            v.tensor_copy(convw, bank[4][:, 0:CONV_K * 3 * H]).then_inc(cw_sb, 1)
            dve.wait_ge(cw_sb, 1)
            dve.wait_ge(pads, 1)

            def conv(blk):
                dve.wait_ge(proj_sb, 2 * blk + 2)
                for k in range(CONV_K):
                    for h in range(H):
                        j = 4 * blk + h
                        src, dst = raw[:, blk % 2, h, k:k + S], qkvT[:, j, :]
                        w = convw[:, k * 3 * H + j:k * 3 * H + j + 1]
                        if k == 0:
                            ins = v.tensor_scalar(dst, src, w, None, ALU.mult)
                        else:
                            ins = v.scalar_tensor_tensor(dst, src, w, dst, ALU.mult, ALU.add)
                    if k < CONV_K - 1:
                        steps.then(ins)
                ins.then_inc(conv_done, 1)

            block_lo(2)
            conv(0)
            block_lo(3)
            conv(1)
            dve.wait_ge(ba_sb, 2)
            dve.wait_ge(small_in, 16 * 5)
            ba3 = ba.rearrange("p (t n) -> p t n", t=TT)
            g3, b3 = (z_.rearrange("p (t n) -> p t n", t=TT) for z_ in (gg, gb2))
            steps.then(v.tensor_tensor(g3, ba3[:, :, H:2 * H], dtb.unsqueeze(1).to_broadcast([P, TT, H]), ALU.add))
            v.tensor_scalar(b3, ba3[:, :, 0:H], -1.0, None, ALU.mult).then_inc(gb_pre, 1)
            block_lo(4)
            conv(2)
            block_lo(5)
            dve.wait_ge(gb_exp, 1)
            v.tensor_scalar_add(gb2, gb2, 1.0)
            steps.then(v.scalar_tensor_tensor(gg, gg, 0.0, gb1, ALU.max, ALU.add))
            v.reciprocal(beta, gb2)
            steps.then(v.scalar_tensor_tensor(g3, g3, -1.0, nalog.unsqueeze(1).to_broadcast([P, TT, H]), ALU.mult, ALU.mult))
            v.tensor_copy(GB[:, :, :], gg.unsqueeze(2).to_broadcast([P, U, P])).then_inc(g_sb, 1)
            dve.wait_ge(rn_done, 1)
            qv, kv = (qkvT[:, 4 * i:4 * i + 4, :].rearrange("p a s -> p (a s)") for i in range(2))
            v.scalar_tensor_tensor(qv, qv, P ** -0.5, rn[:, 0:D], ALU.mult, ALU.mult)
            v.tensor_tensor(kv, kv, rn[:, D:2 * D], ALU.mult).then_inc(qk_norm, 1)
            block_lo(6)
            dve.wait_ge(gc_psum, 1)
            v.tensor_copy(gcum, bank[4][:, 0:U])
            v.tensor_copy(glast, bank[4][:, U:2 * U]).then_inc(gc_sb, 1)
            dve.wait_ge(gc_sb, 1)
            dve.wait_ge(gc_psum, 2)
            v.tensor_tensor(kdc, glast, gcum, ALU.subtract)
            for u in range(U):
                ins = v.tensor_scalar(DEC[:, u, :], quad(bank[5 + u // 4], u % 4),
                                      gcum[:, u:u + 1], 0.0, ALU.subtract, ALU.max)
            ins.then_inc(dif_sb, 1)
            dve.wait_ge(dec_exp, 1)
            dve.wait_ge(eg_done, 1)
            v.scalar_tensor_tensor(nbg, beta, -1.0, expg, ALU.mult, ALU.mult)
            dve.wait_ge(cst_in, 16)
            steps.then(v.tensor_tensor(DEC[:, :, :], DEC[:, :, :], tril.unsqueeze(1).to_broadcast([P, U, P]), ALU.mult))
            dve.wait_ge(kk_psum, 1)
            for u in range(U):
                ins = v.scalar_tensor_tensor(L[:, u, :], quad(kkb[u // 4], u % 4),
                                             beta[:, u:u + 1], DEC[:, u, :], ALU.mult, ALU.mult)
            ins.then_inc(lq_sb, 1)
            dve.wait_ge(kk_psum, 2)
            for t in range(TT):
                ins = v.tensor_tensor(QKT[:, 4 * t:4 * t + 4, :], quads(qkb[t]), DEC[:, 4 * t:4 * t + 4, :], ALU.mult)
            ins.then_inc(lq_sb, 1)
            mask_scores(0)
            to_lo(14)
            softplus(0)
            to_lo(15)
            ident_b = ident.unsqueeze(1).to_broadcast([P, U, P])
            dve.wait_ge(lq_sb, 1)
            steps.then(v.tensor_tensor(T[:, :, :], L[:, :, :], c(C_LEV1).unsqueeze(1).to_broadcast([P, U, P]), ALU.mult))
            v.tensor_tensor(T[:, :, :], T[:, :, :], ident_b, ALU.add)
            dve.wait_ge(lt_sb, 1)
            steps.then(v.tensor_tensor(UT[:, :, :], LT[:, :, :], c(C_LEV).unsqueeze(1).to_broadcast([P, U, P]), ALU.mult))
            steps.then(v.tensor_tensor(UT[:, :, :], UT[:, :, :], ident_b, ALU.add))
            v.sem_inc(lev_u, 2)
            v.sem_inc(lev_t, 2)
            exponents(0)
            branch_b(0)
            dve.wait_ge(vk_psum, 1)
            for u in range(U):
                v.tensor_scalar(VB[:, u, :], quad(bank[5 + 2 * (u // H)], u % H), beta[:, u:u + 1], None, ALU.mult)
            for h in range(H):
                ins = v.tensor_scalar(KDEC[:, h, :], quad(bank[4], h), kdc[:, h:h + 1], None, ALU.mult)
            ins.then_inc(vb_sb, 1)

            mask_scores(1)
            to_lo(16)
            to_lo(17)
            softplus(1)
            exponents(1)
            u_update(1)
            branch_b(1)
            mask_scores(2)
            u_update(2)
            to_lo(18)
            softplus(2)
            exponents(2)
            u_update(3)
            to_lo(19)
            branch_b(2)
            mask_scores(3)
            u_update(4)
            to_lo(20)
            softplus(3)
            exponents(3)
            u_update(5)
            to_lo(21)
            branch_b(3)
            to_lo(PB0)
            u_update(6)
            to_lo(PB0 + 1)

            def output_norm(t):
                hs_ = slice(t * H, (t + 1) * H)
                dve.wait_ge(osq_sb, t + 1)
                steps.then(v.tensor_reduce(ssq[:, hs_], OSQ[:, hs_, :], AX_X, ALU.add))
                v.tensor_scalar(ssq[:, hs_], ssq[:, hs_], 1.0 / P, RMS_EPS, ALU.mult, ALU.add).then_inc(rms_in, 1)

            def norm_gate(t):
                dve.wait_ge(rms_done, t + 1)
                dve.wait_ge(zg_silu, 1)
                dve.wait_ge(o_sb, t + 1)
                for u in range(t * H, (t + 1) * H):
                    ins = v.scalar_tensor_tensor(ON[:, u, :], O[:, u, :], rms[:, u:u + 1],
                                                 zg[:, u * P:(u + 1) * P], ALU.mult, ALU.mult)
                ins.then_inc(on_sb, 1)

            dve.wait_ge(o_psum, 1)
            v.tensor_copy(O[:, 0:H, :], quads(bank[5])).then_inc(o_sb, 1)
            output_norm(0)
            dve.wait_ge(vb_sb, 1)
            dve.wait_ge(ks_psum, 1)
            for h in range(H):
                ins = v.scalar_tensor_tensor(R1[:, h, :], quad(bank[6], h), nbg[:, H + h:H + h + 1],
                                             VB[:, H + h, :], ALU.mult, ALU.add)
            ins.then_inc(r1_sb, 1)
            norm_gate(0)
            dve.wait_ge(o_psum, 2)
            dve.wait_ge(qs_sb, 1)
            v.tensor_tensor(O[:, H:U, :], QS[:, :, :], quads(bank[6]), ALU.add).then_inc(o_sb, 1)
            output_norm(1)
            to_lo(PA0)

            def branch_a_lo(t):
                dve.wait_ge(oah_sb, t + 1)
                ts = slice(t * P, (t + 1) * P)
                v.scalar_tensor_tensor(oal[:, :, ts], quads(bank[5 + 2 * t]), normw, oah[:, :, ts].bitcast(F32),
                                       ALU.mult, ALU.subtract).then_inc(oal_sb, 1)

            norm_gate(1)
            branch_a_lo(0)
            to_lo(PA0 + 1)
            branch_a_lo(1)
            gp = [gates[:, 2 * q:2 * q + 2, :] for q in range(8)]

            def bank2(b):
                return bank[b].rearrange("p (a s) -> p a s", a=2)

            dve.wait_ge(gates_sb, 1)
            for pair in range(4):
                if pair < 3:
                    dve.wait_ge(pb_psum, pair + 1)
                else:
                    dve.wait_ge(halves_used, PB0 + 2)
                ins = v.tensor_tensor(gp[4 + pair], gp[4 + pair], bank2(pair), ALU.mult)
            steps.then(ins)
            dve.wait_ge(gates_sb, 2)
            to_lo(WO0)
            to_lo(WO0 + 1)
            for pair in range(4):
                if pair < 3:
                    dve.wait_ge(pa_psum, pair + 1)
                else:
                    dve.wait_ge(halves_used, PA0 + 2)
                m = msum[:, pair % 2, :].rearrange("p (a s) -> p a s", a=2)
                steps.then(v.tensor_tensor(gp[pair], gp[pair], bank2(4 + pair), ALU.mult))
                v.tensor_tensor(m, gp[pair], gp[4 + pair], ALU.add).then_inc(msum_sb, 1)
                dve.wait_ge(mh_sb, pair + 1)
                ps = slice(2 * pair, 2 * pair + 2)
                v.tensor_tensor(ml[:, ps, :], m, mh[:, ps, :].bitcast(F32), ALU.subtract).then_inc(ml_sb, 1)
            to_lo(WO0 + 2)
            to_lo(WO0 + 3)

            st = stats.rearrange("p (t h s) -> p t h s", t=TT, h=2)

            def half_stats(src, t, half):
                v.bn_stats(st[:, t, half, :], src[:, half * 512:(half + 1) * 512]).then_inc(bn_sem, 1)

            def norm_stats(t, count, done):
                dve.wait_ge(bn_sem, count)
                steps.then(v.bn_aggr(mv[:, 2 * t:2 * t + 2], st[:, t, :, :].rearrange("p h s -> p (h s)")))
                v.tensor_scalar_add(rstd[:, t:t + 1], mv[:, 2 * t + 1:2 * t + 2], LN_EPS).then_inc(done, 1)

            def normalise(dst, t, ready, done):
                steps.then(v.scalar_tensor_tensor(dst, dst, mv[:, 2 * t:2 * t + 1], lnp[:, 0, :], ALU.subtract, ALU.mult))
                dve.wait_ge(ready, t + 1)
                v.scalar_tensor_tensor(dst, dst, rstd[:, t:t + 1], lnp[:, 1, :], ALU.mult, ALU.add).then_inc(done, 1)

            dve.wait_ge(xres_in, 16 * TT)
            dve.wait_ge(ln1_in, 32)

            def mix_norm(t):
                for half in range(2):
                    if half == 0:
                        dve.wait_ge(mix_psum, t + 1)
                    elif t == 1:
                        dve.wait_ge(halves_used, PRE)
                    xs = xres[:, t, half * 512:(half + 1) * 512]
                    steps.then(v.scalar_tensor_tensor(xs, xs, ALPHA, bank[2 * t + half], ALU.mult, ALU.add))
                    half_stats(xres[:, t, :], t, half)
                norm_stats(t, 2 * t + 2, var1)
                normalise(xres[:, t, :], t, rstd1, x1_sb)

            mix_norm(0)
            mix_norm(1)
            for h in range(4):
                to_lo(PRE + h)

            dve.wait_ge(lg_psum, 1)
            dve.wait_ge(late_in, 32)
            v.tensor_copy(aff, bank[6][:, 0:TT * NE])
            sel3 = selv.rearrange("p (t e) -> p t e", t=TT)
            steps.then(v.tensor_tensor(sel3, bank[6][:, 0:TT * NE].rearrange("p (t e) -> p t e", t=TT),
                                       rbias.unsqueeze(1).to_broadcast([P, TT, NE]), ALU.add))

            def rank_of_four(dst, src, n, limit):
                s4_ = src.rearrange("p (m i) -> p m i", i=4)
                other = s4_.unsqueeze(2).to_broadcast([P, n, 4, 4])
                own = s4_.unsqueeze(3).to_broadcast([P, n, 4, 4])
                gt, eq = spare[:, 0:16 * n], spare[:, 256:256 + 16 * n]
                v.tensor_tensor(gt.rearrange("p (m i j) -> p m i j", i=4, j=4), other, own, ALU.is_gt)
                steps.then(v.tensor_tensor(eq.rearrange("p (m i j) -> p m i j", i=4, j=4), other, own, ALU.is_equal))
                eq3 = eq.rearrange("p (m q) -> p m q", q=16)
                steps.then(v.tensor_tensor(eq3, eq3, jlt.unsqueeze(1).to_broadcast([P, n, 16]), ALU.mult))
                steps.then(v.tensor_tensor(gt, gt, eq, ALU.add))
                steps.then(v.tensor_reduce(dst, gt.rearrange("p (q j) -> p q j", j=4), AX_X, ALU.add))
                steps.then(v.tensor_single_scalar(dst, dst, limit, ALU.is_lt))

            rank_of_four(top2, selv, 2 * NG, 2.0)
            steps.then(v.tensor_tensor(selv, selv, top2, ALU.mult))
            steps.then(v.tensor_reduce(gscore, selv.rearrange("p (g i) -> p g i", i=EPG), AX_X, ALU.add))
            rank_of_four(gsel, gscore, TT, 1.0)
            v.sem_inc(gsel_sb, 1)
            t3 = top2.rearrange("p (g i) -> p g i", i=EPG)
            s5 = sel5.rearrange("p (t n) -> p t n", t=TT)
            r5 = rank5.rearrange("p (t n) -> p t n", t=TT)
            c5 = comb5.rearrange("p (t n j) -> p t n j", t=TT, n=5)
            v.tensor_copy(s5[:, :, 0:NG], gsel.rearrange("p (t g) -> p t g", t=TT))
            v.memset(s5[:, :, NG:NG + 1], 1.0)
            steps.then(v.tensor_tensor(t3, t3, gsel.unsqueeze(2).to_broadcast([P, 2 * NG, EPG]), ALU.mult))
            dve.wait_ge(rank_psum, 1)
            rk3 = rank.rearrange("p (t g) -> p t g", t=TT)
            steps.then(v.tensor_copy(r5[:, :, 0:NG], bank[5][:, 0:8].rearrange("p (t g) -> p t g", t=TT)))

            def selection(n):
                for t in range(TT):
                    ins = v.tensor_scalar(SEL[:, n, t, :], iota, rank5[:, t * 5 + n:t * 5 + n + 1],
                                          sel5[:, t * 5 + n:t * 5 + n + 1], ALU.is_equal, ALU.mult)
                return ins

            selection(0).then_inc(sel_sb, 1)
            v.tensor_copy(cnt, bank[5][:, 8:12])
            steps.then(v.tensor_tensor(rank, gsel, bank[5][:, 0:8], ALU.mult))
            v.tensor_tensor(comb, aff, top2, ALU.mult)
            steps.then(v.tensor_reduce(wsum, rk3, AX_X, ALU.add))
            steps.then(v.tensor_scalar_add(r5[:, :, NG], wsum, -128.0))
            for n in range(1, 5):
                selection(n)
            steps.then(v.tensor_reduce(wsum, comb.rearrange("p (t e) -> p t e", t=TT), AX_X, ALU.add))
            steps.then(v.reciprocal(wsum, wsum))
            for t in range(TT):
                ins = v.tensor_scalar(comb[:, t * NE:(t + 1) * NE], comb[:, t * NE:(t + 1) * NE],
                                      wsum[:, t:t + 1], None, ALU.mult)
            steps.then(ins)
            for t in range(TT):
                v.tensor_copy(c5[:, t, 0:NG, :], comb[:, t * NE:(t + 1) * NE].rearrange("p (g j) -> p g j", j=EPG))
                ins = v.tensor_reduce(c5[:, t, NG, :], comb[:, t * NE:(t + 1) * NE].rearrange("p (g j) -> p j g", j=EPG),
                                      AX_X, ALU.add)
            ins.then_inc(sel_sb, 1)
            steps.then(v.tensor_single_scalar(ovf, cnt, 128.0, ALU.is_gt))
            steps.then(v.tensor_reduce(cnt[:, 0:1], ovf, AX_X, ALU.add))
            v.tensor_tensor(cnt[:, 1:4], ovf[:, 1:4], iota[:, 1:4], ALU.mult)
            steps.then(v.tensor_scalar_add(small_i[:, 0:1], cnt[:, 0:1], float(NG)))
            v.tensor_scalar_add(small_i[:, 1:2], cnt[:, 0:1], float(NG - 1))
            v.memset(small_i[:, 3:4], NG - 1)
            steps.then(v.tensor_reduce(ovf[:, 0:1], cnt[:, 1:4], AX_X, ALU.add))
            v.tensor_copy(small_i[:, 4:5], ovf[:, 0:1]).then_inc(npass_sb, 1)

            def xg_lo(i):
                for half in range(2):
                    dve.wait_ge(xgh_sb, i * 2 + (half + 1))
                    ks = slice(4 * half, 4 * half + 4)
                    v.tensor_tensor(xgl[:, ks, :], quads(bank[7 - 7 * half]), xgh[:, ks, :].bitcast(F32),
                                    ALU.subtract).then_inc(xgl_sb, 1)

            xg_lo(0)
            dve.wait_ge(npass_sb, 1)
            before_last = dve.value_load(small_i[0:1, 1:2], min_val=NG - 1, max_val=NPASS_MAX - 1)
            dve.wait_ge(selt_sb, 1)
            dve.wait_ge(r2_init, 1)

            def expert_pass(i, last_pass):
                def matrix_lo(m):
                    for h in range(2):
                        to_lo(PRE + 2 * m + h, i)

                def hidden(j):
                    m = PASS_ORDER.index((j, 1))
                    dve.wait_ge(halves_used, PASS * i + (PRE + 2 * (m + 1)))
                    dve.wait_ge(silu_sb, i * 4 + (j + 1))
                    if j >= 1:
                        dve.wait_ge(ht_psum, i * 4 + j)
                    v.scalar_tensor_tensor(hid[:, :], silu_g[:, :], cgcur[:, j:j + 1],
                                           bank[2 * (j % 2) + 1], ALU.mult, ALU.mult).then_inc(hid_sb, 1)

                def hid_t(j):
                    dve.wait_ge(hth_sb, i * 4 + (j + 1))
                    v.tensor_tensor(htl[:, :, :], quads(bank[4]), hth[:, :, :].bitcast(F32), ALU.subtract).then_inc(htl_sb, 1)

                v.tensor_copy(cgcur, cg.rearrange("p (n j) -> p n j", j=EPG)[:, bass.ds(i, 1), :]
                              .rearrange("p n j -> p (n j)")).then_inc(cg_sb, 1)
                matrix_lo(2)
                dve.wait_ge(cg_sb, i + 1)
                hidden(0)
                matrix_lo(3)
                hid_t(0)
                matrix_lo(4)
                hidden(1)
                matrix_lo(5)
                matrix_lo(6)
                hid_t(1)
                matrix_lo(7)
                hidden(2)
                matrix_lo(8)
                matrix_lo(9)
                hid_t(2)
                matrix_lo(10)
                hidden(3)
                matrix_lo(11)
                hid_t(3)
                if not last_pass:
                    xg_lo(i + 1)
                    matrix_lo(12)
                for o in range(2):
                    dve.wait_ge(yh_sb, i * 2 + (o + 1))
                    os_ = slice(o * 512, (o + 1) * 512)
                    v.tensor_tensor(yl[:, os_], bank[5 + o], yh[:, os_].bitcast(F32), ALU.subtract).then_inc(yl_sb, 1)
                if not last_pass:
                    matrix_lo(13)
                for o in range(2):
                    for t in range(TT):
                        m = 2 * o + t
                        dve.wait_ge(sc_psum, i * 4 + (m + 1))
                        rs = r2[:, t, o * 512:(o + 1) * 512]
                        v.tensor_tensor(rs, rs, bank[[7, 4, 5, 6][m]], ALU.add).then_inc(sc_done, 1)
                        if last_pass:
                            dve.wait_ge(sc_done, i * 4 + (m + 1))
                            half_stats(r2[:, t, :], t, o)
                            if o == 1 and t == 0:
                                norm_stats(0, 4 + 3, var2)

            with dve.Fori(0, before_last) as i:
                expert_pass(i, False)
            expert_pass(before_last, True)
            dve.wait_ge(ln2_in, 32)
            norm_stats(1, 4 + 4, var2)
            for t in range(TT):
                normalise(r2[:, t, :], t, rstd2, out_sb)


_INS = ['x', 'w_in', 'conv_w', 'dn_a_log', 'dn_dt_bias', 'dn_norm_w', 'p_a', 'p_b', 'w_out', 'ln1_g', 'ln1_b',
        'w_router', 'router_bias', 'w_gate', 'w_up', 'w_down', 'ln2_g', 'ln2_b']


def kernel(**inputs):
    import numpy as _np
    import concourse.bacc as _bacc
    from concourse.bass_utils import run_bass_kernel_spmd as _run

    nc = _bacc.Bacc("TRN2", target_bir_lowering=False, num_devices=1)
    table = constant_table()
    arrays = {"consts_dram": table}
    args = [nc.dram_tensor("consts_dram", table.shape, F32, kind="ExternalInput").ap()]
    for name in _INS:
        a = _np.ascontiguousarray(inputs[name])
        arrays[f"in_{name}_dram"] = a
        args.append(nc.dram_tensor(f"in_{name}_dram", a.shape, mybir.dt.from_np(a.dtype), kind="ExternalInput").ap())
    args.append(nc.dram_tensor("out_dram", (1, S, D), F32, kind="ExternalOutput").ap())
    hybrid_moe_block(nc, *args)
    r = _run(nc, [arrays], core_ids=[0])
    return r.results[0]["out_dram"]
```

```python
from contextlib import ExitStack

import concourse.bass as bass
from concourse import mybir
import numpy as np

F32 = mybir.dt.float32
F32R = mybir.dt.float32r
I32 = mybir.dt.int32
ALU = mybir.AluOpType
ACT = mybir.ActivationFunctionType
AX_X = mybir.AxisListType.X

P = 128
D = 1024
KD = D // P
S = 256
TT = S // P
H = 4
U = TT * H
SH, DH = 8, 64
NE, NG, EPG = 16, 4, 4
F = 512
KF = F // P
CONV_K = 4
DELTA_W = H * P
LN_EPS, RMS_EPS = 1e-5, 1e-6
ALPHA = 2.0 ** 0.25
NPASS_MAX = NG + 1
MASKED = -1e30

HALF = 2048
NSLOT = 4
NRAW = 8
LO_CUT = 1536
BLOCKS = [(0, "qkv"), (512, "qkv"), (1024, "qkv"), (2056, "sq"), (2568, "sk"), (3080, "sv"), (1536, "z"),
          (3592, "gate"), (4104, "gate"), (4616, "gate"), (5128, "gate")]
NB = len(BLOCKS)
STICK_UNIT = 12
BA_COL = 2048
PB0, PA0, WO0 = 2 * NB, 2 * NB + 2, 2 * NB + 4
PRE = 2 * NB + 8
PASS = 2 * 3 * EPG
PASS_ORDER = [(0, 0), (0, 1), (1, 0), (1, 1), (0, 2), (2, 0), (2, 1), (1, 2), (3, 0), (3, 1), (2, 2), (3, 2)]

C_IDENT, C_TRIU, C_TRIL, C_ONES, C_NEG, C_LEV1 = (P * i for i in range(6))
C_LEV = C_LEV1 + P
C_SMALL = C_LEV + 7 * P
NCONST = C_SMALL + 16
C_SUP = NCONST
C_IOTA = C_SUP + P
C_JLT = C_IOTA + P
NTABLE = C_JLT + 16


def constant_table():
    p = np.arange(P)[:, None]
    f = np.arange(P)[None, :]
    t = np.zeros((P, NTABLE), np.float32)
    t[:, C_IDENT:C_IDENT + P] = p == f
    t[:, C_TRIU:C_TRIU + P] = p <= f
    t[:, C_TRIL:C_TRIL + P] = p >= f
    t[:, C_SUP:C_SUP + P] = p < f
    t[:, C_ONES:C_ONES + P] = 1.0
    t[:, C_NEG:C_NEG + P] = np.where(p < f, 0.0, MASKED)
    t[:, C_IOTA:C_IOTA + P] = f
    t[:, C_LEV1:C_LEV1 + P] = -((p // 2 == f // 2) & (p % 2 == 1) & (f % 2 == 0)).astype(np.float32)
    for n in range(7):
        s = 1 << n
        at = C_LEV + n * P
        m = (p // (2 * s) == f // (2 * s)) & ((f // s) % 2 == 1) & ((p // s) % 2 == 0)
        t[:, at:at + P] = -m.astype(np.float32) if n == 0 else m
    ij = np.arange(16)
    t[:, C_JLT:C_JLT + 16] = (ij % 4 < ij // 4)
    t[:, C_SMALL] = RMS_EPS
    t[:, C_SMALL + 1:C_SMALL + 16] = -0.5
    return t


class Steps:

    def __init__(self, eng, sem):
        self.eng, self.sem, self.n = eng, sem, 0

    def then(self, ins):
        self.n += 1
        ins.then_inc(self.sem, 1)
        self.eng.wait_ge(self.sem, self.n)


def hybrid_moe_block(nc, consts, x, w_in, conv_w, dn_a_log, dn_dt_bias, dn_norm_w, p_a, p_b, w_out,
                     ln1_g, ln1_b, w_router, router_bias, w_gate, w_up, w_down, ln2_g, ln2_b, out):
    ctx = ExitStack()
    with ctx:
        def sem(name):
            return ctx.enter_context(nc.semaphore(name))

        base = (nc.sbuf_base + 31) // 32 * 32
        top = [base]

        def region(nbytes):
            a = top[0]
            top[0] += nbytes
            return a

        def place(name, shape, offset, dt=F32):
            return nc.alloc_sbuf_tensor_at(name, shape, dt, offset=offset)

        KB = 1024
        R_RAW, R_HI, R_LO = (region(NSLOT * 4 * HALF) for _ in range(3))
        R_X, R_QKV, R_CONV, R_Z = region(16 * KB), region(12 * KB), region(2 * H * (S + 4) * 4), region(4 * KB)
        R_SQ, R_SK, R_SV, R_GATE = region(4 * KB), region(4 * KB), region(4 * KB), region(16 * KB)
        R_B = [region(4 * KB) for _ in range(6)]
        R_STICK, R_CST, R_SMALL, R_SUMS = region(9 * KB), region(NCONST * 4), region(4 * 600 + 64), region(KB)
        assert top[0] <= nc.sbuf_usable_end

        wraw = place("wraw", [P, NSLOT, HALF], R_RAW)
        extra = [place(f"wraw{i}", [P, HALF], a) for i, a in enumerate(
            (R_SQ, R_QKV + 8 * KB, R_QKV + 16 * KB, R_B[5]))]
        expert_raw = [t[:, :] for t in extra] + [wraw[:, (WO0 + i) % NSLOT, :] for i in range(NSLOT)]
        whi = place("whi", [P, NSLOT, HALF], R_HI, F32R)
        wlo = place("wlo", [P, NSLOT, HALF], R_LO, F32R)
        x0 = place("x0", [P, TT, D], R_GATE)
        xh = place("xh", [P, KD, S], R_X, F32R)
        xl = place("xl", [P, KD, S], R_X + 8 * KB, F32R)
        xres = place("xres", [P, TT, D], R_X)
        lgt = place("lgt", [P, S], R_STICK + 4 * KB)
        x1T = place("x1T", [P, KD, S], R_X + 8 * KB)
        qkvT = place("qkvT", [P, 3 * H, S], R_QKV)
        raw = place("raw", [P, 2, H, S + 4], R_CONV)
        L = place("L", [P, U, P], R_CONV)
        DEC = place("DEC", [P, U, P], R_CONV + 4 * KB)
        VB = place("VB", [P, U, P], R_CONV)
        KDEC = place("KDEC", [P, H, P], R_CONV + 4 * KB)
        U0 = place("U0", [P, H, P], R_CONV + 6 * KB)
        zg = place("zg", [P, TT * DELTA_W], R_Z)
        LT = place("LT", [P, U, P], R_B[0])
        GB = place("GB", [P, U, P], R_B[0])
        T = place("T", [P, U, P], R_B[1])
        UT = place("UT", [P, U, P], R_B[2])
        Y = place("Y", [P, U, P], R_B[3])
        CM = place("CM", [P, U, P], R_B[4])
        idle = place("idle", [P, 512], R_B[4], mybir.dt.bfloat16)
        wbah = place("wbah", [P, KD, 8], R_B[5], F32R)
        wbal = place("wbal", [P, KD, 8], R_B[5] + 256, F32R)
        baT = place("baT", [P, S], R_B[5] + KB)
        QKT = place("QKT", [P, U, P], R_B[5])
        rn = place("rn", [P, 2 * U * P], R_B[1])
        sqq = place("sqq", [P, 2 * U * P], R_B[3])
        cwrow = place("cwrow", [P, P], R_B[3])
        S1 = place("S1", [P, H, P], R_B[1])
        R1 = place("R1", [P, H, P], R_B[1] + 2 * KB)
        QS = place("QS", [P, H, P], R_B[3])
        VN = place("VN", [P, H, P], R_B[3] + 2 * KB)
        O = place("O", [P, U, P], R_B[4])
        OSQ = place("OSQ", [P, U, P], R_STICK)
        ON = place("ON", [P, U, P], R_B[0])
        oah = place("oah", [P, H, S], R_QKV, F32R)
        oal = place("oal", [P, H, S], R_QKV + 4 * KB, F32R)
        sqT = place("sqT", [P, 4, S], R_SQ)
        skT = place("skT", [P, 4, S], R_SK)
        sv = place("sv", [P, TT, SH * DH], R_SV)
        obh = place("obh", [P, 4, S], R_SQ, F32R)
        obl = place("obl", [P, 4, S], R_SK, F32R)
        stick = place("stick", [P, 3, 2, 384], R_STICK)
        sph = place("sph", [P, 2, 384], R_STICK + 2 * 768 * 4, F32R)
        spl = place("spl", [P, 2, 384], R_STICK + 768 * 4, F32R)
        tril_r = place("tril_r", [P, P], R_SUMS, F32R)
        ones_r = place("ones_r", [P, P], R_SUMS + 512, F32R)
        gates = place("gates", [P, 2 * KD, S], R_GATE)
        msum = place("msum", [P, 2, 2 * S], R_STICK + 4 * KB)
        mh = place("mh", [P, KD, S], R_GATE, F32R)
        ml = place("ml", [P, KD, S], R_GATE + 8 * KB, F32R)
        lnp = place("lnp", [P, 2, D], R_B[3])
        r2 = place("r2", [P, TT, D], R_B[0])
        SEL = place("SEL", [P, 5, TT, P], R_GATE)
        SELT = place("SELT", [P, 5, S], R_GATE + 5 * KB)
        selt_cur = place("selt_cur", [P, S], R_GATE + 10 * KB, F32R)
        spare = place("spare", [P, 512], R_SV)
        wr = place("wr", [P, KD, NE], R_SV + 2048)
        late = place("late", [P, NTABLE - NCONST], R_SV + 2560)
        xgh = place("xgh", [P, KD, P], R_QKV, F32R)
        xgl = place("xgl", [P, KD, P], R_QKV + 4 * KB, F32R)
        hid = place("hid", [P, F], R_B[2])
        silu_g = place("silu_g", [P, F], R_B[2] + 2 * KB)
        hth = [place(f"hth{i}", [P, KF, P], (R_GATE + 11 * KB, R_STICK + 4 * KB)[i], F32R) for i in range(2)]
        htl = [place(f"htl{i}", [P, KF, P], (R_GATE + 13 * KB, R_STICK + 6 * KB)[i], F32R) for i in range(2)]
        yh = place("yh", [P, D], R_X + 8 * KB, F32R)
        yl = place("yl", [P, D], R_X + 12 * KB, F32R)
        y_last = place("y_last", [P, D], R_X + 8 * KB)

        cst = place("cst", [P, NCONST], R_CST)
        small = place("small", [P, 592], R_SMALL)
        small_i = place("small_i", [P, 8], R_SMALL + 4 * 592, I32)

        def c(at, n=P):
            return cst[:, at:at + n]

        ident, triu, tril, ones, neg = (c(x_) for x_ in (C_IDENT, C_TRIU, C_TRIL, C_ONES, C_NEG))
        sup, iota, jlt = late[:, 0:P], late[:, P:2 * P], late[:, 2 * P:2 * P + 16]

        at = [0]

        def cols(n):
            a = small[:, at[0]:at[0] + n]
            at[0] += n
            return a

        wba = cols(KD * 8).rearrange("p (k n) -> p k n", k=KD)
        ba, gg, gb1, gb2, beta = cols(16), cols(U), cols(U), cols(U), cols(U)
        alog, dtb, nalog = cols(H), cols(H), cols(H)
        gcum, glast, expg, kdc, nbg = cols(U), cols(U), cols(U), cols(U), cols(U)
        ssq, rms = cols(U), cols(U)
        convw = cols(CONV_K * 3 * H)
        normw = cols(1)
        stats, mv, rstd = cols(4 * 6), cols(4), cols(2)
        aff, selv, top2 = cols(32), cols(32), cols(32)
        gscore, gsel, rank = cols(8), cols(8), cols(8)
        comb, wsum = cols(32), cols(2)
        sel5, rank5 = cols(TT * 5), cols(TT * 5)
        cg, comb5 = cols(5 * EPG), cols(TT * 5 * EPG)
        rbias, cnt, ovf, cgcur = cols(NE), cols(4), cols(4), cols(EPG)

        psum = ctx.enter_context(nc.psum_tensor("psum", [P, 8, 512], F32))
        bank = [psum[:, i, :] for i in range(8)]

        def quads(t):
            return t.rearrange("p (k s) -> p k s", s=P)

        def quad(t, j):
            return t[:, j * P:(j + 1) * P]

        x_in = [sem(f"x_in{t}") for t in range(TT)]
        (ident_in, cst_in, small_in, ln1_in, ln2_in, wr_in, late_in, xres_in) = (sem(n) for n in (
            "ident_in", "cst_in", "small_in", "ln1_in", "ln2_in", "wr_in", "late_in", "xres_in"))
        raw_in = [sem(f"raw_in{i}") for i in range(NSLOT)]
        expert_in = [sem(f"expert_in{i}") for i in range(NRAW)]
        hi_done, lo_vector, lo_pool = sem("hi_done"), sem("lo_vector"), sem("lo_pool")
        halves_used = sem("halves_used")
        xt_psum, xh_sb, xl_sb = sem("xt_psum"), sem("xh_sb"), sem("xl_sb")
        cw_psum, cw_sb, pads = sem("cw_psum"), sem("cw_sb"), sem("pads")
        proj_a, proj_sb = sem("proj_a"), sem("proj_sb")
        ba_psum, ba_sb = sem("ba_psum"), sem("ba_sb")
        conv_done, silu_done, sq_done = sem("conv_done"), sem("silu_done"), sem("sq_done")
        ss_psum, rn_done, qk_norm = sem("ss_psum"), sem("rn_done"), sem("qk_norm")
        gb_pre, gb_exp, g_sb = sem("gb_pre"), sem("gb_exp"), sem("g_sb")
        gc_psum, gc_sb, dif_sb, dec_exp, eg_done = (sem(n) for n in (
            "gc_psum", "gc_sb", "dif_sb", "dec_exp", "eg_done"))
        kk_psum, lq_sb, lt_psum, lt_sb, qkt_sb = (sem(n) for n in (
            "kk_psum", "lq_sb", "lt_psum", "lt_sb", "qkt_sb"))
        lev_mask, lev_y, lev_ysb, lev_p, lev_u, lev_tt, lev_t = (sem(n) for n in (
            "lev_mask", "lev_y", "lev_ysb", "lev_p", "lev_u", "lev_tt", "lev_t"))
        vk_psum, vb_sb = sem("vk_psum"), sem("vb_sb")
        u0_psum, u0_sb, s1_psum, s1_sb, ks_psum, r1_sb, qs_sb = (sem(n) for n in (
            "u0_psum", "u0_sb", "s1_psum", "s1_sb", "ks_psum", "r1_sb", "qs_sb"))
        vn_psum, vn_sb, o_psum, o_sb, osq_sb, rms_in, rms_done, on_sb = (sem(n) for n in (
            "vn_psum", "vn_sb", "o_psum", "o_sb", "osq_sb", "rms_in", "rms_done", "on_sb"))
        oat_psum, oah_sb, oal_sb = sem("oat_psum"), sem("oah_sb"), sem("oal_sb")
        z_psum, z_sb, z_masked, s_ln, s_sp, cs_psum, s_t, s_att, av_psum, obh_sb, obl_sb = (sem(n) for n in (
            "z_psum", "z_sb", "z_masked", "s_ln", "s_sp", "cs_psum", "s_t", "s_att", "av_psum", "obh_sb", "obl_sb"))
        pa_psum, pb_psum, msum_sb, mh_sb, ml_sb = (sem(n) for n in (
            "pa_psum", "pb_psum", "msum_sb", "mh_sb", "ml_sb"))
        mix_psum, var1, rstd1, x1_sb, x1t_psum, x1t_sb = (sem(n) for n in (
            "mix_psum", "var1", "rstd1", "x1_sb", "x1t_psum", "x1t_sb"))
        lgt_psum, lgt_sb, lg_psum, r2_init, gsel_sb, rank_psum = (sem(n) for n in (
            "lgt_psum", "lgt_sb", "lg_psum", "r2_init", "gsel_sb", "rank_psum"))
        npass_sb, sel_sb, selt_psum, selt_sb = (sem(n) for n in ("npass_sb", "sel_sb", "selt_psum", "selt_sb"))
        xg_psum, xgh_sb, xgl_sb, cur_sb, cg_sb = (sem(n) for n in ("xg_psum", "xgh_sb", "xgl_sb", "cur_sb", "cg_sb"))
        silu_sb, hid_sb, ht_psum, hth_sb, htl_sb = (sem(n) for n in ("silu_sb", "hid_sb", "ht_psum", "hth_sb", "htl_sb"))
        y_psum, yh_sb, yl_sb, sc_psum, sc_done = (sem(n) for n in ("y_psum", "yh_sb", "yl_sb", "sc_psum", "sc_done"))
        var2, rstd2, out_sb, out_done = sem("var2"), sem("rstd2"), sem("out_sb"), sem("out_done")
        bn_sem = sem("bn_sem")
        dve_steps, act_steps, pool_steps = sem("dve_steps"), sem("act_steps"), sem("pool_steps")
        wbah_sb, wbal_sb = sem("wbah_sb"), sem("wbal_sb")
        table_in, idle_set = sem("table_in"), sem("idle_set")
        rn_ln = sem("rn_ln")
        hi_first, lo_first = sem("hi_first"), sem("lo_first")
        zg_silu, gates_sb = sem("zg_silu"), sem("gates_sb")

        x_d = x.rearrange("b (t p) d -> (b t) p d", p=P)
        out_d = out.rearrange("b (t p) d -> (b t) p d", p=P)
        win_d, pa_d, pb_d, wout_d = (w.rearrange("l (k p) n -> (l p) k n", p=P) for w in (w_in, p_a, p_b, w_out))
        expert_d = [w_gate.rearrange("l e (p k) f -> (l e) p (k f)", k=KD),
                    w_up.rearrange("l e (p k) f -> (l e) p (k f)", k=KD),
                    w_down.rearrange("l e (p k) d -> (l e) p (k d)", k=KF)]

        def row(ap):
            return ap.partition_broadcast(P).rearrange("p a d -> p (a d)")

        def s4(t, n):
            return t[:, n % NSLOT, :].rearrange("p (k n) -> p k n", k=4)

        def s2(t, n):
            return t[:, n % NSLOT, :].rearrange("p (k n) -> p k n", k=2)

        def wait_split(eng, n, i=None):
            for lo_part in (lo_vector, lo_pool):
                eng.wait_ge(lo_part, (n + 1) + (0 if i is None else PASS * i))

        def raw_half(n):
            return wraw[:, n % NSLOT, :] if n < PRE else expert_raw[(n - PRE) % NRAW]

        def head_tile(kind, u):
            t, h = u // H, u % H
            return qkvT[:, kind * H + h, t * P:(t + 1) * P]

        def unit_bank(u):
            return u % 4 if u < STICK_UNIT else u % 2

        kkb, qkb = [bank[7], bank[4]], [bank[5], bank[6]]
        block = ctx.enter_context(nc.Block())

        @block.sync
        def _(sp):
            for t in range(TT):
                sp.dma_start(x0[:, t, :], x_d[t]).then_inc(x_in[t], 16)
            for n in range(PRE):
                if n >= NSLOT:
                    wait_split(sp, n - NSLOT)
                if n < PB0:
                    a, h = BLOCKS[n // 2][0], n % 2
                    src = win_d[:, 4 * h:4 * h + 4, a:a + 512]
                else:
                    w, m = [(pb_d, n - PB0), (pa_d, n - PA0), (wout_d, n - WO0)][min((n - PB0) // 2, 2)]
                    src = w[:, 2 * m:2 * m + 2, :]
                dst = s4(wraw, n) if n < PB0 else s2(wraw, n)
                sp.dma_start(dst, src).then_inc(raw_in[n % NSLOT], 16)
                if n == WO0:
                    sp.wait_ge(halves_used, 2 * NB)
                    for t in range(TT):
                        sp.dma_start(xres[:, t, :], x_d[t]).then_inc(xres_in, 16)

            def half_load(n, group):
                j, w = PASS_ORDER[(n - PRE) // 2]
                h = (n - PRE) % 2
                sp.dma_start(raw_half(n), expert_d[w][bass.ds(group * EPG + j, 1), :, h * HALF:(h + 1) * HALF]
                             .rearrange("e p n -> (e p) n")).then_inc(expert_in[(n - PRE) % NRAW], 16)

            def pass_loads(i, group):
                for n in range(PRE, PRE + PASS):
                    wait_split(sp, n - NRAW, i)
                    half_load(n, group)

            sp.wait_ge(halves_used, PB0 + 2)
            half_load(PRE, 0)
            sp.wait_ge(on_sb, 2)
            for n in range(PRE + 1, PRE + PASS):
                if n >= PRE + NRAW:
                    wait_split(sp, n - NRAW)
                elif n >= PRE + NSLOT:
                    wait_split(sp, WO0 + n - (PRE + NSLOT))
                half_load(n, 0)
            with sp.Fori(1, NG - 1) as i:
                pass_loads(i, i)
            sp.wait_ge(npass_sb, 1)
            npass = sp.value_load(small_i[0:1, 0:1], min_val=NG, max_val=NPASS_MAX)
            with sp.Fori(NG - 1, npass) as i:
                group = sp.value_load(small_i[0:1, bass.ds(i, 1)], min_val=0, max_val=NG - 1)
                pass_loads(i, group)
            for t, half in [(t, half) for t in range(TT) for half in range(2)]:
                sp.wait_ge(out_sb, 2 * t + half + 1)
                hs_ = slice(half * 512, (half + 1) * 512)
                sp.dma_start(out_d[t, :, hs_], r2[:, t, hs_]).then_inc(out_done, 16)
            sp.wait_ge(out_done, 16 * 2 * TT)

        @block.tensor
        def _(pe):
            mm, tr = nc.tensor.matmul, nc.tensor.transpose

            def mm3(o, wh, wl, vh, vl, start, stop):
                mm(o, wh, vh, start=start, stop=False)
                mm(o, wh, vl, start=False, stop=False)
                return mm(o, wl, vh, start=False, stop=stop)

            def keep_clock(n, weights, moving, b):
                for _ in range(n):
                    mm(b[:, 0:moving.free_size()], weights, moving, start=True, stop=True)

            pe.wait_ge(idle_set, 1)
            keep_clock(9, idle[:, 0:P], idle[:, :], bank[7])
            pe.wait_ge(ident_in, 16)
            for t in range(TT):
                pe.wait_ge(x_in[t], 16)
                for half in range(2):
                    for k in range(4):
                        last = tr(quad(bank[2 * t + half], k), quad(x0[:, t, :], 4 * half + k), ident)
                    last.then_inc(xt_psum, 1)
            keep_clock(20, idle[:, 0:P], idle[:, :], bank[7])
            pe.wait_ge(xl_sb, 4)

            def project(b, part, only=None, ks=range(KD)):
                u = 2 * b + part
                channel_major = BLOCKS[b][1] not in ("sv", "z")
                if only != 1:
                    if u in (2, 3):
                        pe.wait_ge(proj_sb, u - 1)
                    elif u < STICK_UNIT and u >= 4:
                        pe.wait_ge(proj_sb, u - 3)
                    elif u >= STICK_UNIT:
                        pe.wait_ge(proj_sb, u - 1)
                for sub in range(2 if channel_major else 1) if only is None else (only,):
                    a = (2 * part + sub) * P
                    o, at_ = (bank[2 * sub + part], 0) if b == 0 else (bank[unit_bank(u)], sub * S)
                    for k in ks:
                        n = 2 * b + k // 4
                        if part == 0 and sub == 0:
                            if k == 0 and b == 0:
                                pe.wait_ge(lo_first, 1)
                            elif k % 4 == 0 or (k == 2 and b == 0):
                                wait_split(pe, n)
                        fl = dict(start=(k == 0), stop=(k == KD - 1))
                        if channel_major:
                            last = mm3(o[:, at_:at_ + S], s4(whi, n)[:, k % 4, a:a + P],
                                       s4(wlo, n)[:, k % 4, a:a + P], xh[:, k, :], xl[:, k, :], **fl)
                        else:
                            t = slice(part * P, (part + 1) * P)
                            last = mm3(o, xh[:, k, t], xl[:, k, t], s4(whi, n)[:, k % 4, :],
                                       s4(wlo, n)[:, k % 4, :], **fl)
                        final = sub == 1 or not channel_major
                        if final and part == 1 and k % 4 == 3:
                            last.then_inc(halves_used, 1)
                        elif final and part == 0 and k == KD - 1:
                            last.then_inc(proj_a, 1)

            def level_y(n):
                pe.wait_ge(lev_mask, n)
                for half in range(2):
                    pe.wait_ge(lev_t, 2 * (n - 1) + half + 1)
                    if n == 1:
                        pe.wait_ge(vb_sb, 1)
                    for j in range(4):
                        u = 4 * half + j
                        last = mm(quad(bank[4 + 2 * half], j), CM[:, u, :], T[:, u, :], start=True, stop=True)
                    last.then_inc(lev_y, 1)

            def level_p(n):
                for half in range(2):
                    pe.wait_ge(lev_ysb, 2 * (n - 1) + half + 1)
                    pe.wait_ge(lev_u, 2 * (n - 1) + half + 1)
                    for j in range(4):
                        u = 4 * half + j
                        last = mm(quad(bank[5 + 2 * half], j), Y[:, u, :], UT[:, u, :], start=True, stop=True)
                    last.then_inc(lev_p, 1)

            def level_t(n):
                for half in range(2):
                    pe.wait_ge(lev_u, 2 * n + half + 1)
                    for j in range(4):
                        u = 4 * half + j
                        last = tr(quad(bank[4 + 2 * half], j), UT[:, u, :], ident)
                    last.then_inc(lev_tt, 1)

            def scores(g):
                if g == 0:
                    pe.wait_ge(proj_sb, STICK_UNIT)
                else:
                    pe.wait_ge(obl_sb, g)
                for e in range(2):
                    rows = slice(e * DH, (e + 1) * DH)
                    mm(bank[2 + e][:, 0:S], skT[rows, g, 0:P], sqT[rows, g, 0:S], start=True, stop=True)
                    last = mm(bank[2 + e][:, S:S + P], skT[rows, g, P:S], sqT[rows, g, P:S], start=True, stop=True)
                last.then_inc(z_psum, 1)

            def key_sums(g):
                pe.wait_ge(s_sp, g + 1)
                first = bank[2].rearrange("p (e s) -> p e s", e=2)
                second = bank[3][:, 0:2 * P].rearrange("p (e s) -> p e s", e=2)
                for sp_, start in ((sph, True), (spl, False)):
                    mm(first, tril_r[:, :], sp_[:, :, 0:S], start=start, stop=False)
                    mm(first[:, :, P:S], ones_r[:, :], sp_[:, :, S:S + P], start=False, stop=not start)
                    last = mm(second, tril_r[:, :], sp_[:, :, S:S + P], start=start, stop=not start)
                last.then_inc(cs_psum, 1)

            def values(g):
                pe.wait_ge(s_att, g + 1)
                for e in range(2):
                    h = 2 * g + e
                    att = stick[:, 2, e, :]
                    o = bank[2][e * DH:(e + 1) * DH, :]
                    mm(o[:, 0:S], sv[:, 0, h * DH:(h + 1) * DH], att[:, 0:S], start=True, stop=False)
                    last = mm(o[:, P:S], sv[:, 1, h * DH:(h + 1) * DH], att[:, S:S + P], start=False, stop=True)
                last.then_inc(av_psum, 1)

            for ks in (range(2), range(2, 4)):
                for part in range(2):
                    for sub in range(2):
                        project(0, part, sub, ks)
            project(0, 0, 0, range(4, KD))
            project(0, 0, 1, range(4, KD))
            pe.wait_ge(small_in, 16 * 5)
            nrow = CONV_K * 3 * H
            tr(bank[4][:, 0:nrow], cwrow[0:nrow, :], cst[0:nrow, C_IDENT:C_IDENT + nrow]).then_inc(cw_psum, 1)
            project(0, 1, 0, range(4, KD))
            project(0, 1, 1, range(4, KD))
            project(1, 0)
            project(1, 1)
            pe.wait_ge(cw_sb, 1)
            pe.wait_ge(wbal_sb, 1)
            for k in range(KD):
                last = mm3(bank[4][0:8, 0:S], wbah[:, k, :], wbal[:, k, :], xh[:, k, :], xl[:, k, :],
                           start=(k == 0), stop=(k == KD - 1))
            last.then_inc(ba_psum, 1)
            project(2, 0)
            pe.wait_ge(ba_sb, 1)
            for t in range(TT):
                last = tr(bank[4][:, S + t * 8:S + t * 8 + 8], baT[0:8, t * P:(t + 1) * P], cst[0:8, C_IDENT:C_IDENT + 8])
            last.then_inc(ba_psum, 1)
            project(2, 1)
            project(3, 0)
            project(3, 1)
            pe.wait_ge(ba_sb, 2)
            pe.wait_ge(cst_in, 16)
            for i in range(4):
                pe.wait_ge(sq_done, i // 2 + 1)
                mm(bank[4 + i], ones, sqq[:, i * 512:(i + 1) * 512], start=True, stop=True).then_inc(ss_psum, 1)
            project(4, 0)
            project(4, 1)
            pe.wait_ge(g_sb, 1)
            pe.wait_ge(rn_ln, 1)
            mm(bank[4][:, 0:U], triu, gg, start=True, stop=True)
            mm(bank[4][:, U:2 * U], ones, gg, start=True, stop=True).then_inc(gc_psum, 1)
            for u in range(U):
                last = mm(quad(bank[5 + u // 4], u % 4), GB[:, u, :], triu, start=True, stop=True)
            last.then_inc(gc_psum, 1)
            project(5, 0)
            project(5, 1)
            pe.wait_ge(qk_norm, 1)
            pe.wait_ge(dif_sb, 1)
            for u in range(U):
                last = mm(quad(kkb[u // 4], u % 4), head_tile(1, u), head_tile(1, u), start=True, stop=True)
            last.then_inc(kk_psum, 1)
            for u in range(U):
                last = mm(quad(qkb[u // 4], u % 4), head_tile(0, u), head_tile(1, u), start=True, stop=True)
            last.then_inc(kk_psum, 1)
            scores(0)
            project(6, 0)
            pe.wait_ge(lq_sb, 1)
            for u in range(U):
                last = tr(quad(kkb[u // 4], u % 4), L[:, u, :], ident)
            last.then_inc(lt_psum, 1)
            pe.wait_ge(lq_sb, 2)
            for u in range(U):
                last = tr(quad(qkb[u // 4], u % 4), QKT[:, u, :], ident)
            last.then_inc(lt_psum, 1)
            project(6, 1, ks=range(4))
            key_sums(0)
            project(6, 1, ks=range(4, KD))
            pe.wait_ge(lt_sb, 1)
            pe.wait_ge(qkt_sb, 1)
            for u in range(U):
                last = tr(quad(bank[5 + 2 * (u // H)], u % H), head_tile(2, u), ident)
            for h in range(H):
                last = tr(quad(bank[4], h), head_tile(1, h), ident)
            last.then_inc(vk_psum, 1)
            values(0)
            scores(1)
            project(7, 0)
            level_y(1)
            project(7, 1, 0)
            key_sums(1)
            level_p(1)
            project(7, 1, 1)
            values(1)
            level_y(2)
            scores(2)
            project(8, 0, 0)
            level_p(2)
            project(8, 0, 1)
            level_y(3)
            project(8, 1, 0)
            level_p(3)
            key_sums(2)
            project(8, 1, 1)
            values(2)
            level_y(4)
            scores(3)
            project(9, 0, 0)
            level_p(4)
            project(9, 0, 1)
            level_y(5)
            project(9, 1, 0)
            level_p(5)
            key_sums(3)
            project(9, 1, 1)
            values(3)
            level_t(5)
            level_y(6)
            project(10, 0, 0)
            level_p(6)
            project(10, 0, 1)

            def project_branch(n0, bh, bl, first_bank, pair, psum_sem, subs=range(2), js=range(4)):
                for sub in subs:
                    a = (2 * pair + sub) * P
                    for j in js:
                        n = n0 + j // 2
                        if pair == 0 and sub == 0 and j % 2 == 0:
                            wait_split(pe, n)
                        last = mm3(bank[first_bank + pair][:, sub * S:(sub + 1) * S],
                                   s2(whi, n)[:, j % 2, a:a + P], s2(wlo, n)[:, j % 2, a:a + P],
                                   bh[:, j, :], bl[:, j, :], start=(j == 0), stop=(j == 3))
                        if pair == 3 and sub == 1 and j % 2 == 1:
                            last.then_inc(halves_used, 1)
                if pair < 3 and sub == 1:
                    last.then_inc(psum_sem, 1)

            def branch_b(pair, **part):
                project_branch(PB0, obh, obl, 0, pair, pb_psum, **part)

            def branch_a(pair, **part):
                project_branch(PA0, oah, oal, 4, pair, pa_psum, **part)

            pe.wait_ge(lev_u, 13)
            for h in range(H):
                last = mm(quad(bank[6], h), UT[:, h, :], VB[:, h, :], start=True, stop=True)
            last.then_inc(u0_psum, 1)
            project(10, 1, 0)
            pe.wait_ge(u0_sb, 1)
            for h in range(H):
                last = mm(quad(bank[4], h), KDEC[:, h, :], U0[:, h, :], start=True, stop=True)
            last.then_inc(s1_psum, 1)
            for h in range(H):
                last = mm(quad(bank[5], h), QKT[:, h, :], U0[:, h, :], start=True, stop=True)
            last.then_inc(o_psum, 1)
            project(10, 1, 1)
            pe.wait_ge(s1_sb, 1)
            pe.wait_ge(lev_u, 14)
            for h in range(H):
                last = mm(quad(bank[6], h), head_tile(1, H + h), S1[:, h, :], start=True, stop=True)
            last.then_inc(ks_psum, 1)
            for h in range(H):
                last = mm(quad(bank[7], h), head_tile(0, H + h), S1[:, h, :], start=True, stop=True)
            last.then_inc(ks_psum, 1)
            pe.wait_ge(obl_sb, 4)
            pe.wait_ge(proj_sb, 2 * NB)
            branch_b(0)
            pe.wait_ge(r1_sb, 1)
            for h in range(H):
                last = mm(quad(bank[4], h), UT[:, H + h, :], R1[:, h, :], start=True, stop=True)
            last.then_inc(vn_psum, 1)
            branch_b(1)
            pe.wait_ge(vn_sb, 1)
            for h in range(H):
                last = mm(quad(bank[6], h), QKT[:, H + h, :], VN[:, h, :], start=True, stop=True)
            last.then_inc(o_psum, 1)
            branch_b(2)

            def branch_a_t(t):
                pe.wait_ge(on_sb, t + 1)
                for h in range(H):
                    last = tr(quad(bank[5 + 2 * t], h), ON[:, t * H + h, :], ident)
                last.then_inc(oat_psum, 1)

            branch_a_t(0)
            branch_b(3, subs=(0,))
            branch_a_t(1)
            branch_b(3, subs=(1,))
            pe.wait_ge(oal_sb, 2)
            for js in (range(2), range(2, 4)):
                for pair in range(2):
                    branch_a(pair, subs=(0,), js=js)
            for pair in range(2):
                branch_a(pair, subs=(1,))
            branch_a(2)
            branch_a(3)
            def mix(t, hs, half):
                for kk in range(2):
                    k = 2 * hs + kk
                    ts, cs_ = slice(t * P, (t + 1) * P), slice(half * 512, (half + 1) * 512)
                    last = mm3(bank[2 * t + half], mh[:, k, ts], ml[:, k, ts], s2(whi, WO0 + hs)[:, kk, cs_],
                               s2(wlo, WO0 + hs)[:, kk, cs_], start=(k == 0), stop=(k == KD - 1))
                return last

            for hs in range(4):
                wait_split(pe, WO0 + hs)
                pe.wait_ge(ml_sb, hs + 1)
                for half in range(2):
                    last = mix(0, hs, half)
            last.then_inc(mix_psum, 1)
            for hs in range(4):
                last = mix(1, hs, 0)
            last.then_inc(mix_psum, 1)

            def x1k(t):
                return xres[:, t, :].rearrange("s (p k) -> s k p", k=KD)

            def x1_transposed(t):
                for half in range(2):
                    pe.wait_ge(x1_sb, 2 * t + half + 1)
                    for k in range(4):
                        last = tr(quad(bank[2 * t + half], k), quad(xres[:, t, :], 4 * half + k), ident)
                    last.then_inc(x1t_psum, 1)

            def logits(t):
                for k in range(KD):
                    if k % 4 == 0:
                        pe.wait_ge(x1t_sb, 2 * t + k // 4 + 1)
                    last = mm(bank[4 + t][0:NE, 0:P], wr[:, k, :], x1T[:, k, t * P:(t + 1) * P],
                              start=(k == 0), stop=(k == KD - 1))
                last.then_inc(lgt_psum, 1)

            mix(1, 0, 1).then_inc(halves_used, 1)
            x1_transposed(0)
            for hs in range(1, 4):
                mix(1, hs, 1).then_inc(halves_used, 1)
            logits(0)
            clock = dict(weights=mh[:, 6, 0:P], moving=mh[:, 6:8, :].rearrange("p k s -> p (k s)"), b=bank[7])
            keep_clock(6, **clock)
            x1_transposed(1)
            keep_clock(2, **clock)
            logits(1)
            for t in range(TT):
                pe.wait_ge(lgt_sb, t + 1)
                last = tr(bank[6][:, t * NE:(t + 1) * NE], lgt[0:NE, t * P:(t + 1) * P], cst[0:NE, C_IDENT:C_IDENT + NE])
            last.then_inc(lg_psum, 1)
            keep_clock(14, **clock)
            pe.wait_ge(gsel_sb, 1)
            mm(bank[5][:, 0:4], sup, gsel[:, 0:4], start=True, stop=True)
            mm(bank[5][:, 4:8], ones, gsel[:, 0:4], start=True, stop=False)
            mm(bank[5][:, 4:8], sup, gsel[:, 4:8], start=False, stop=True)
            mm(bank[5][:, 8:12], ones, gsel[:, 0:4], start=True, stop=False)
            mm(bank[5][:, 8:12], ones, gsel[:, 4:8], start=False, stop=True).then_inc(rank_psum, 1)

            def gather(i):
                for half in range(2):
                    for k in range(4):
                        for t in range(TT):
                            last = mm(quad(bank[7 - 7 * half], k), x1k(t)[:, 4 * half + k, :],
                                      SEL[:, bass.ds(i, 1), t, :].rearrange("p n s -> p (n s)"),
                                      start=(t == 0), stop=(t == TT - 1))
                    last.then_inc(xg_psum, 1)

            keep_clock(3, **clock)
            pe.wait_ge(sel_sb, 1)
            gather(0)
            pe.wait_ge(sel_sb, 2)
            for n in range(5):
                for t in range(TT):
                    last = tr(bank[1 + n // 2][:, (n % 2) * S + t * P:(n % 2) * S + (t + 1) * P], SEL[:, n, t, :], ident)
            last.then_inc(selt_psum, 1)
            for n in range(5):
                for t in range(TT):
                    last = mm(bank[6][:, n * EPG:(n + 1) * EPG], SEL[:, n, t, :],
                              comb5[:, (t * 5 + n) * EPG:(t * 5 + n + 1) * EPG], start=(t == 0), stop=(t == TT - 1))
            last.then_inc(selt_psum, 1)
            pe.wait_ge(npass_sb, 1)
            before_last = pe.value_load(small_i[0:1, 1:2], min_val=NG - 1, max_val=NPASS_MAX - 1)

            def expert_pass(i, last_pass):
                def half_ready(n):
                    wait_split(pe, n, i)

                def gate_or_up(m):
                    j, w = PASS_ORDER[m]
                    for h in range(2):
                        n = PRE + 2 * m + h
                        half_ready(n)
                        for k in range(4):
                            kt = 4 * h + k
                            last = mm3(bank[2 * (j % 2) + w], xgh[:, kt, :], xgl[:, kt, :], s4(whi, n)[:, k, :],
                                       s4(wlo, n)[:, k, :], start=(kt == 0), stop=(kt == KD - 1))
                        last.then_inc(halves_used, 1)

                def transposes(j):
                    pe.wait_ge(hid_sb, i * 4 + (j + 1))
                    hk = hid[:, :].rearrange("s (p k) -> s k p", k=KF)
                    for k in range(KF):
                        last = tr(quad(bank[4], k), hk[:, k, :], ident)
                    last.then_inc(ht_psum, 1)

                def down(m, between=None):
                    j = PASS_ORDER[m][0]
                    pe.wait_ge(htl_sb, i * 4 + (j + 1))
                    for h in range(2):
                        n = PRE + 2 * m + h
                        half_ready(n)
                        for o in range(2):
                            for kk in range(2):
                                k = 2 * h + kk
                                last = mm3(bank[5 + o], hth[j % 2][:, k, :], htl[j % 2][:, k, :],
                                           s2(whi, n)[:, kk, o * 512:(o + 1) * 512],
                                           s2(wlo, n)[:, kk, o * 512:(o + 1) * 512], start=(j == 0 and k == 0), stop=False)
                        last.then_inc(halves_used, 1)
                        if h == 0 and between is not None:
                            transposes(between)

                def last_down(m):
                    j = PASS_ORDER[m][0]
                    pe.wait_ge(htl_sb, i * 4 + (j + 1))
                    for h in range(2):
                        n = PRE + 2 * m + h
                        half_ready(n)
                        for o in range(2):
                            for kk in range(2):
                                k = 2 * h + kk
                                last = mm3(bank[5 + o], hth[j % 2][:, k, :], htl[j % 2][:, k, :],
                                           s2(whi, n)[:, kk, o * 512:(o + 1) * 512],
                                           s2(wlo, n)[:, kk, o * 512:(o + 1) * 512], start=False, stop=(k == KF - 1))
                            if h == 1 and o == 0:
                                last.then_inc(y_psum, 1)
                        last.then_inc(halves_used, 1)

                pe.wait_ge(xgl_sb, i * 2 + 2)
                gate_or_up(0)
                pe.wait_ge(selt_sb, 1)
                gate_or_up(1)
                gate_or_up(2)
                transposes(0)
                gate_or_up(3)
                down(4)
                gate_or_up(5)
                transposes(1)
                gate_or_up(6)
                down(7)
                gate_or_up(8)
                transposes(2)
                gate_or_up(9)
                down(10, between=3)
                if not last_pass:
                    gather(i + 1)
                last_down(11)
                pe.wait_ge(cur_sb, i + 1)
                if last_pass:
                    for o in range(2):
                        os_ = slice(o * 512, (o + 1) * 512)
                        pe.wait_ge(yh_sb, i * 2 + (o + 1))
                        for t in range(TT):
                            mm(bank[2 * o + t], selt_cur[:, t * P:(t + 1) * P].bitcast(F32), y_last[:, os_],
                               start=True, stop=True).then_inc(sc_psum, 1)
                    return
                pe.wait_ge(xgl_sb, i * 2 + 4)
                for o in range(2):
                    os_ = slice(o * 512, (o + 1) * 512)
                    places = [(bank[[7, 4, 5, 6][2 * o + t]], slice(t * P, (t + 1) * P)) for t in range(TT)]
                    pe.wait_ge(yh_sb, i * 2 + (o + 1))
                    if o == 1:
                        pe.wait_ge(yl_sb, i * 2 + 2)
                    for b, ts in places:
                        mm(b, selt_cur[:, ts], yh[:, os_], start=True, stop=False)
                    pe.wait_ge(yl_sb, i * 2 + (o + 1))
                    for b, ts in places:
                        mm(b, selt_cur[:, ts], yl[:, os_], start=False, stop=True).then_inc(sc_psum, 1)

            with pe.Fori(0, before_last) as i:
                expert_pass(i, False)
            expert_pass(before_last, True)

        @block.scalar
        def _(act):
            steps = Steps(act, act_steps)
            a_ = nc.scalar.activation
            act.dma_start(cst[:, 0:P], consts[:, 0:P]).then_inc(ident_in, 16)
            act.wait_ge(pads, 1)
            nc.scalar.copy(normw, raw[:, 0, 0, 0:1]).then_inc(table_in, 1)
            act.dma_start(cwrow[0:CONV_K * 3 * H, :], conv_w.rearrange("l k (j c) -> (l k j) c", c=P)).then_inc(small_in, 16)
            act.dma_start(wba, win_d[:, :, BA_COL:BA_COL + 8]).then_inc(small_in, 16)
            act.dma_start(alog, row(dn_a_log)).then_inc(small_in, 16)
            act.dma_start(dtb, row(dn_dt_bias)).then_inc(small_in, 16)
            act.wait_ge(table_in, 1)
            act.dma_start(normw, dn_norm_w.rearrange("l (p o) -> (l p) o", o=1)).then_inc(small_in, 16)
            for t in range(TT):
                for half in range(2):
                    act.wait_ge(xt_psum, 2 * t + half + 1)
                    nc.scalar.copy(xh[:, 4 * half:4 * half + 4, t * P:(t + 1) * P],
                                   quads(bank[2 * t + half])).then_inc(xh_sb, 1)

            def to_hi(n, i=None):
                if n < PRE:
                    act.wait_ge(raw_in[n % NSLOT], 16 * (n // NSLOT + 1))
                else:
                    m = n - PRE
                    turns = 0 if i is None else (PASS // NRAW * 16) * i
                    act.wait_ge(expert_in[m % NRAW], turns + 16 * (m // NRAW + 1))
                if n >= NSLOT:
                    act.wait_ge(halves_used, (n - NSLOT + 1) + (0 if i is None else PASS * i))
                nc.scalar.copy(whi[:, n % NSLOT, :], raw_half(n)).then_inc(hi_done, 1)

            def block_hi(b):
                to_hi(2 * b)
                to_hi(2 * b + 1)

            def evacuate(b, part):
                kind = BLOCKS[b][1]
                u = 2 * b + part
                o = bank[unit_bank(u)]
                o2 = o.rearrange("p (a s) -> p a s", a=2)
                if part == 0:
                    act.wait_ge(proj_a, b + 1)
                else:
                    act.wait_ge(halves_used, 2 * b + 2)
                a = slice(2 * part, 2 * part + 2)
                if kind == "qkv":
                    if u == 0:
                        act.wait_ge(pads, 1)
                    if b == 2:
                        act.wait_ge(conv_done, 1)
                    if b == 0:
                        for sub in range(2):
                            ins = nc.scalar.copy(raw[:, 0, 2 * part + sub, 3:3 + S], bank[2 * sub + part][:, 0:S])
                    else:
                        ins = nc.scalar.copy(raw[:, b % 2, a, 3:3 + S], o2)
                elif kind == "sq":
                    ins = nc.scalar.mul(sqT[:, a, :], o2, DH ** -0.5)
                elif kind == "sk":
                    ins = nc.scalar.copy(skT[:, a, :], o2)
                elif kind == "sv":
                    ins = nc.scalar.copy(sv[:, part, :], o)
                elif kind == "z":
                    ins = nc.scalar.copy(zg[:, part * 512:(part + 1) * 512], o)
                else:
                    g = 4 * (b - 7) + 2 * part
                    ins = nc.scalar.copy(gates[:, g:g + 2, :], o2)
                ins.then_inc(proj_sb, 1)

            def silu_block(blk):
                act.wait_ge(conv_done, blk + 1)
                v = qkvT[:, 4 * blk:4 * blk + 4, :]
                a_(v, v, ACT.Silu).then_inc(silu_done, 1)
                if blk < 2:
                    act.wait_ge(silu_done, blk + 1)
                    if blk == 0:
                        act.wait_ge(cw_psum, 1)
                    dst = sqq[:, blk * D:(blk + 1) * D].rearrange("p (a s) -> p a s", a=4)
                    a_(dst, v, ACT.Square).then_inc(sq_done, 1)

            act.wait_ge(raw_in[0], 16)
            for part, done in ((slice(0, HALF // 2), hi_first), (slice(HALF // 2, HALF), hi_done)):
                nc.scalar.copy(whi[:, 0, part], raw_half(0)[:, part]).then_inc(done, 1)
            to_hi(1)
            block_hi(1)
            act.dma_start(cst[:, P:], consts[:, P:NCONST]).then_inc(cst_in, 16)
            act.wait_ge(small_in, 16 * 5)
            nc.scalar.copy(wbah[:, :, :], wba).then_inc(wbah_sb, 1)
            evacuate(0, 0)
            evacuate(0, 1)
            block_hi(2)
            evacuate(1, 0)
            evacuate(1, 1)
            block_hi(3)
            act.wait_ge(ba_psum, 1)
            nc.scalar.copy(baT[0:8, :], bank[4][0:8, 0:S]).then_inc(ba_sb, 1)
            silu_block(0)
            act.wait_ge(ba_psum, 2)
            nc.scalar.copy(ba, bank[4][:, S:S + 16]).then_inc(ba_sb, 1)
            evacuate(2, 0)
            evacuate(2, 1)
            block_hi(4)
            silu_block(1)
            evacuate(3, 0)
            silu_block(2)
            evacuate(3, 1)
            block_hi(5)
            act.wait_ge(gb_pre, 1)
            a_(gb2, gb2, ACT.Exp)
            a_(nalog, alog, ACT.Exp)
            steps.then(a_(gb1, gg, ACT.Abs))
            steps.then(a_(gb1, gb1, ACT.Exp, scale=-1.0))
            a_(gb1, gb1, ACT.Ln, bias=1.0).then_inc(gb_exp, 1)
            act.wait_ge(cst_in, 16)
            act.wait_ge(ss_psum, 4)
            a_(rn[:, :].rearrange("p (b s) -> p b s", b=4), psum[:, 4:8, :], ACT.Ln,
               bias=cst[:, C_SMALL:C_SMALL + 1]).then_inc(rn_ln, 1)
            act.wait_ge(rn_ln, 1)
            a_(rn[:, :], rn[:, :], ACT.Exp, scale=-0.5).then_inc(rn_done, 1)
            evacuate(4, 0)
            evacuate(4, 1)
            block_hi(6)
            act.wait_ge(dif_sb, 1)
            a_(DEC[:, :, :], DEC[:, :, :], ACT.Exp, scale=-1.0).then_inc(dec_exp, 1)
            a_(expg, gcum, ACT.Exp)
            a_(kdc, kdc, ACT.Exp).then_inc(eg_done, 1)
            def y_sb(n):
                for half in range(2):
                    act.wait_ge(lev_y, 2 * (n - 1) + half + 1)
                    nc.scalar.copy(Y[:, 4 * half:4 * half + 4, :], quads(bank[4 + 2 * half])).then_inc(lev_ysb, 1)

            def t_sb():
                for half in range(2):
                    act.wait_ge(lev_tt, half + 1)
                    nc.scalar.copy(T[:, 4 * half:4 * half + 4, :], quads(bank[4 + 2 * half])).then_inc(lev_t, 1)

            def scores_sb(g):
                act.wait_ge(z_psum, g + 1)
                if g >= 1:
                    act.wait_ge(s_t, g)
                nc.scalar.copy(stick[:, 0, :, :], psum[:, 2:4, 0:384]).then_inc(z_sb, 1)

            def softplus(g):
                act.wait_ge(z_masked, g + 1)
                e_buf = stick[:, 1, :, :]
                steps.then(a_(e_buf, stick[:, 0, :, :], ACT.Abs))
                steps.then(a_(e_buf, e_buf, ACT.Exp, scale=-1.0))
                a_(e_buf, e_buf, ACT.Ln, bias=1.0).then_inc(s_ln, 1)

            def attention(g):
                act.wait_ge(s_t, g + 1)
                a_(stick[:, 2, :, :], stick[:, 2, :, :], ACT.Exp).then_inc(s_att, 1)

            def branch_b(g):
                act.wait_ge(av_psum, g + 1)
                nc.scalar.copy(obh[:, g, :], bank[2][:, 0:S]).then_inc(obh_sb, 1)

            evacuate(5, 0)
            evacuate(5, 1)
            scores_sb(0)
            to_hi(14)
            softplus(0)
            to_hi(15)
            evacuate(6, 0)
            act.wait_ge(lt_psum, 1)
            nc.scalar.copy(LT[:, 0:4, :], quads(bank[7]))
            nc.scalar.copy(LT[:, 4:8, :], quads(bank[4])).then_inc(lt_sb, 1)
            act.wait_ge(lt_psum, 2)
            nc.scalar.copy(QKT[:, :, :].rearrange("p (b j) c -> p b (j c)", b=2), psum[:, 5:7, :]).then_inc(qkt_sb, 1)
            attention(0)
            evacuate(6, 1)
            branch_b(0)
            to_hi(16)
            scores_sb(1)
            to_hi(17)
            softplus(1)
            evacuate(7, 0)
            y_sb(1)
            attention(1)
            evacuate(7, 1)
            branch_b(1)
            y_sb(2)
            scores_sb(2)
            to_hi(18)
            softplus(2)
            evacuate(8, 0)
            y_sb(3)
            to_hi(19)
            attention(2)
            evacuate(8, 1)
            branch_b(2)
            y_sb(4)
            scores_sb(3)
            to_hi(20)
            softplus(3)
            evacuate(9, 0)
            y_sb(5)
            to_hi(21)
            attention(3)
            evacuate(9, 1)
            branch_b(3)
            t_sb()
            y_sb(6)
            to_hi(PB0)
            evacuate(10, 0)
            to_hi(PB0 + 1)
            act.wait_ge(u0_psum, 1)
            nc.scalar.copy(U0[:, :, :], quads(bank[6])).then_inc(u0_sb, 1)
            act.wait_ge(proj_sb, 14)
            a_(zg[:, :], zg[:, :], ACT.Silu).then_inc(zg_silu, 1)
            act.wait_ge(s1_psum, 1)
            nc.scalar.copy(S1[:, :, :], quads(bank[4])).then_inc(s1_sb, 1)
            evacuate(10, 1)

            def output_squares(t):
                act.wait_ge(o_sb, t + 1)
                a_(OSQ[:, t * H:(t + 1) * H, :], O[:, t * H:(t + 1) * H, :], ACT.Square).then_inc(osq_sb, 1)

            output_squares(0)
            act.wait_ge(ks_psum, 2)
            for h in range(H):
                ins = nc.scalar.mul(QS[:, h, :], quad(bank[7], h), expg[:, H + h:H + h + 1])
            ins.then_inc(qs_sb, 1)
            to_hi(PA0)
            act.wait_ge(vn_psum, 1)
            nc.scalar.copy(VN[:, :, :], quads(bank[4])).then_inc(vn_sb, 1)
            act.wait_ge(proj_sb, 2 * NB)
            a_(gates[:, KD:2 * KD, :], gates[:, KD:2 * KD, :], ACT.Sigmoid).then_inc(gates_sb, 1)
            output_squares(1)
            to_hi(PA0 + 1)

            def branch_a_hi(t):
                act.wait_ge(oat_psum, t + 1)
                nc.scalar.mul(oah[:, :, t * P:(t + 1) * P], quads(bank[5 + 2 * t]), normw).then_inc(oah_sb, 1)

            branch_a_hi(0)
            branch_a_hi(1)
            a_(gates[:, 0:KD, :], gates[:, 0:KD, :], ACT.Sigmoid).then_inc(gates_sb, 1)
            act.dma_start(lnp[:, 0, :], row(ln1_g)).then_inc(ln1_in, 16)
            act.dma_start(lnp[:, 1, :], row(ln1_b)).then_inc(ln1_in, 16)
            act.dma_start(rbias, router_bias.partition_broadcast(P)).then_inc(late_in, 16)
            act.dma_start(late[:, :], consts[:, NCONST:NTABLE]).then_inc(late_in, 16)
            act.dma_start(wr[:, :, :], w_router.rearrange("(k p) e -> p k e", p=P)).then_inc(wr_in, 16)
            to_hi(WO0)
            to_hi(WO0 + 1)
            for pair in range(4):
                if pair == 3:
                    to_hi(WO0 + 2)
                act.wait_ge(msum_sb, pair + 1)
                nc.scalar.copy(mh[:, 2 * pair:2 * pair + 2, :],
                               msum[:, pair % 2, :].rearrange("p (a s) -> p a s", a=2)).then_inc(mh_sb, 1)
            to_hi(WO0 + 3)
            act.wait_ge(wr_in, 16)
            for t in range(TT):
                for half in range(2):
                    act.wait_ge(x1t_psum, 2 * t + half + 1)
                    nc.scalar.copy(x1T[:, 4 * half:4 * half + 4, t * P:(t + 1) * P],
                                   quads(bank[2 * t + half])).then_inc(x1t_sb, 1)
                if t == 0:
                    for h in range(4):
                        to_hi(PRE + h)
                act.wait_ge(lgt_psum, t + 1)
                a_(lgt[0:NE, t * P:(t + 1) * P], bank[4 + t][0:NE, 0:P], ACT.Sigmoid).then_inc(lgt_sb, 1)
            act.wait_ge(x1_sb, 4)
            act.dma_start(lnp[:, 0, :], row(ln2_g)).then_inc(ln2_in, 16)
            act.dma_start(lnp[:, 1, :], row(ln2_b)).then_inc(ln2_in, 16)
            nc.scalar.mul(r2[:, :, :], xres[:, :, :], ALPHA).then_inc(r2_init, 1)

            def xg_hi(i):
                for half in range(2):
                    act.wait_ge(xg_psum, i * 2 + (half + 1))
                    nc.scalar.copy(xgh[:, 4 * half:4 * half + 4, :], quads(bank[7 - 7 * half])).then_inc(xgh_sb, 1)

            xg_hi(0)
            act.wait_ge(selt_psum, 1)
            for n in range(0, 5, 2):
                m = min(2, 5 - n)
                nc.scalar.copy(SELT[:, n:n + m, :], bank[1 + n // 2][:, 0:m * S].rearrange("p (n s) -> p n s", s=S))
            act.wait_ge(selt_psum, 2)
            nc.scalar.copy(cg, bank[6][:, 0:5 * EPG]).then_inc(selt_sb, 1)
            act.wait_ge(npass_sb, 1)
            before_last = act.value_load(small_i[0:1, 1:2], min_val=NG - 1, max_val=NPASS_MAX - 1)

            def expert_pass(i, last_pass):
                def matrix_hi(m):
                    for h in range(2):
                        to_hi(PRE + 2 * m + h, i)

                def silu(j):
                    m = PASS_ORDER.index((j, 0))
                    act.wait_ge(halves_used, PASS * i + (PRE + 2 * (m + 1)))
                    if j >= 1:
                        act.wait_ge(hid_sb, i * 4 + j)
                    a_(silu_g[:, :], bank[2 * (j % 2)], ACT.Silu).then_inc(silu_sb, 1)

                def hid_t(j):
                    act.wait_ge(ht_psum, i * 4 + (j + 1))
                    nc.scalar.copy(hth[j % 2][:, :, :], quads(bank[4])).then_inc(hth_sb, 1)

                matrix_hi(2)
                silu(0)
                matrix_hi(3)
                hid_t(0)
                matrix_hi(4)
                silu(1)
                matrix_hi(5)
                matrix_hi(6)
                hid_t(1)
                matrix_hi(7)
                silu(2)
                matrix_hi(8)
                matrix_hi(9)
                hid_t(2)
                matrix_hi(10)
                silu(3)
                matrix_hi(11)
                hid_t(3)
                if not last_pass:
                    xg_hi(i + 1)
                    to_hi(PRE + PASS, i)
                for o in range(2):
                    if o == 0:
                        act.wait_ge(y_psum, i + 1)
                    else:
                        act.wait_ge(halves_used, PASS * i + (PRE + PASS))
                    nc.scalar.copy((y_last if last_pass else yh)[:, o * 512:(o + 1) * 512], bank[5 + o]).then_inc(yh_sb, 1)
                if not last_pass:
                    to_hi(PRE + PASS + 1, i)
                    matrix_hi(13)

            with act.Fori(0, before_last) as i:
                expert_pass(i, False)
            expert_pass(before_last, True)

        @block.gpsimd
        def _(pool):
            nc.gpsimd.memset(raw[:, :, :, 0:3], 0.0).then_inc(pads, 1)
            steps = Steps(pool, pool_steps)

            def to_lo(n, i=None):
                pool.wait_ge(hi_done, (n + 1) + (0 if i is None else PASS * i))
                s = n % NSLOT
                nc.gpsimd.tensor_tensor(wlo[:, s, LO_CUT:], raw_half(n)[:, LO_CUT:], whi[:, s, LO_CUT:].bitcast(F32),
                                        ALU.subtract).then_inc(lo_pool, 1)

            def level_mask(n):
                if n > 1:
                    pool.wait_ge(lev_y, 2 * (n - 1))
                m = c(C_LEV + n * P).unsqueeze(1).to_broadcast([P, U, P])
                nc.gpsimd.tensor_tensor(CM[:, :, :], LT[:, :, :], m, ALU.mult).then_inc(lev_mask, 1)

            for n in range(14):
                to_lo(n)
            pool.wait_ge(lq_sb, 1)
            steps.then(nc.gpsimd.tensor_tensor(T[:, :, :], L[:, :, :], c(C_LEV1).unsqueeze(1).to_broadcast([P, U, P]),
                                               ALU.mult))
            nc.gpsimd.tensor_tensor(T[:, :, :], T[:, :, :], ident.unsqueeze(1).to_broadcast([P, U, P]),
                                    ALU.add).then_inc(lev_t, 2)
            to_lo(14)
            pool.wait_ge(cst_in, 16)
            pool.wait_ge(lt_sb, 1)
            level_mask(1)
            for n in (15, 16, 17):
                to_lo(n)
            level_mask(2)
            level_mask(3)
            to_lo(18)
            level_mask(4)
            to_lo(19)
            to_lo(20)
            level_mask(5)
            to_lo(21)
            level_mask(6)
            to_lo(PB0)
            to_lo(PB0 + 1)
            for t in range(TT):
                pool.wait_ge(rms_in, t + 1)
                hs_ = slice(t * H, (t + 1) * H)
                nc.gpsimd.tensor_tensor(rms[:, hs_], ssq[:, hs_], c(C_SMALL + 1, H), ALU.pow).then_inc(rms_done, 1)
                to_lo(PA0 + t)
            for n in range(WO0, WO0 + 4):
                to_lo(n)

            def power(t, var, ready):
                pool.wait_ge(var, t + 1)
                nc.gpsimd.tensor_tensor(rstd[:, t:t + 1], rstd[:, t:t + 1], c(C_SMALL + 1, 1), ALU.pow).then_inc(ready, 1)

            power(0, var1, rstd1)
            to_lo(PRE)
            power(1, var1, rstd1)
            for h in range(1, 4):
                to_lo(PRE + h)
            pool.wait_ge(npass_sb, 1)
            before_last = pool.value_load(small_i[0:1, 1:2], min_val=NG - 1, max_val=NPASS_MAX - 1)
            pool.wait_ge(selt_sb, 1)

            def expert_pass(i, last_pass):
                pool.wait_ge(halves_used, PASS * i + (PRE + 1))
                nc.gpsimd.tensor_copy(selt_cur[:, :], SELT[:, bass.ds(i, 1), :]
                                      .rearrange("p n s -> p (n s)")).then_inc(cur_sb, 1)
                for n in range(PRE + NSLOT, PRE + PASS + (0 if last_pass else NSLOT)):
                    to_lo(n, i)

            with pool.Fori(0, before_last) as i:
                expert_pass(i, False)
            expert_pass(before_last, True)
            for t in range(TT):
                power(t, var2, rstd2)

        @block.vector
        def _(dve):
            v = nc.vector
            steps = Steps(dve, dve_steps)

            def to_lo(n, i=None):
                dve.wait_ge(hi_done, (n + 1) + (0 if i is None else PASS * i))
                s = n % NSLOT
                v.tensor_tensor(wlo[:, s, 0:LO_CUT], raw_half(n)[:, 0:LO_CUT], whi[:, s, 0:LO_CUT].bitcast(F32),
                                ALU.subtract).then_inc(lo_vector, 1)

            def block_lo(b):
                to_lo(2 * b)
                to_lo(2 * b + 1)

            def u_update(n):
                for half in range(2):
                    dve.wait_ge(lev_p, 2 * (n - 1) + half + 1)
                    us = UT[:, 4 * half:4 * half + 4, :]
                    v.tensor_tensor(us, us, quads(bank[5 + 2 * half]), ALU.subtract).then_inc(lev_u, 1)
                    if n <= 4:
                        dve.wait_ge(lev_u, 2 * n + half + 1)
                        hs_ = slice(4 * half, 4 * half + 4)
                        v.transpose(T[:, hs_, :].rearrange("p u c -> p (u c)"),
                                    UT[:, hs_, :].rearrange("p u c -> p (u c)")).then_inc(lev_t, 1)

            def mask_scores(g):
                dve.wait_ge(z_sb, g + 1)
                diag = stick[:, 0, :, :].rearrange("p e (b s) -> p e b s", s=P)[:, :, 0:3:2, :]
                v.tensor_tensor(diag, diag, neg.unsqueeze(1).unsqueeze(1).to_broadcast([P, 2, 2, P]),
                                ALU.add).then_inc(z_masked, 1)

            def softplus(g):
                dve.wait_ge(z_masked, g + 1)
                dve.wait_ge(s_ln, g + 1)
                if g >= 1:
                    dve.wait_ge(av_psum, g)
                steps.then(v.scalar_tensor_tensor(stick[:, 1, :, :], stick[:, 0, :, :], 0.0, stick[:, 1, :, :],
                                                  ALU.max, ALU.add))
                steps.then(v.tensor_copy(sph[:, :, :], stick[:, 1, :, :]))
                v.tensor_tensor(spl[:, :, :], stick[:, 1, :, :], sph[:, :, :].bitcast(F32), ALU.subtract).then_inc(s_sp, 1)

            def exponents(g):
                dve.wait_ge(cs_psum, g + 1)
                v.tensor_tensor(stick[:, 2, :, 0:S], stick[:, 0, :, 0:S], bank[2].rearrange("p (e s) -> p e s", e=2),
                                ALU.subtract)
                v.tensor_tensor(stick[:, 2, :, S:S + P], stick[:, 0, :, S:S + P],
                                bank[3][:, 0:2 * P].rearrange("p (e s) -> p e s", e=2), ALU.subtract).then_inc(s_t, 1)

            def branch_b(g):
                dve.wait_ge(obh_sb, g + 1)
                v.tensor_tensor(obl[:, g, :], bank[2][:, 0:S], obh[:, g, :].bitcast(F32), ALU.subtract).then_inc(obl_sb, 1)

            v.memset(idle[:, :], 0.0).then_inc(idle_set, 1)
            for t in range(TT):
                for half in range(2):
                    dve.wait_ge(xh_sb, 2 * t + half + 1)
                    ks, ts = slice(4 * half, 4 * half + 4), slice(t * P, (t + 1) * P)
                    v.tensor_tensor(xl[:, ks, ts], quads(bank[2 * t + half]), xh[:, ks, ts].bitcast(F32),
                                    ALU.subtract).then_inc(xl_sb, 1)
            for part, ready, done in ((slice(0, HALF // 2), hi_first, lo_first),
                                      (slice(HALF // 2, LO_CUT), hi_done, lo_vector)):
                dve.wait_ge(ready, 1)
                v.tensor_tensor(wlo[:, 0, part], raw_half(0)[:, part], whi[:, 0, part].bitcast(F32),
                                ALU.subtract).then_inc(done, 1)
            to_lo(1)
            block_lo(1)
            dve.wait_ge(small_in, 16 * 5)
            dve.wait_ge(wbah_sb, 1)
            v.tensor_tensor(wbal[:, :, :], wba, wbah[:, :, :].bitcast(F32), ALU.subtract).then_inc(wbal_sb, 1)
            dve.wait_ge(cw_psum, 1)
            v.tensor_copy(convw, bank[4][:, 0:CONV_K * 3 * H]).then_inc(cw_sb, 1)
            dve.wait_ge(cw_sb, 1)
            dve.wait_ge(pads, 1)

            def conv(blk):
                dve.wait_ge(proj_sb, 2 * blk + 2)
                for k in range(CONV_K):
                    for h in range(H):
                        j = 4 * blk + h
                        src, dst = raw[:, blk % 2, h, k:k + S], qkvT[:, j, :]
                        w = convw[:, k * 3 * H + j:k * 3 * H + j + 1]
                        if k == 0:
                            ins = v.tensor_scalar(dst, src, w, None, ALU.mult)
                        else:
                            ins = v.scalar_tensor_tensor(dst, src, w, dst, ALU.mult, ALU.add)
                    if k < CONV_K - 1:
                        steps.then(ins)
                ins.then_inc(conv_done, 1)

            block_lo(2)
            conv(0)
            block_lo(3)
            conv(1)
            dve.wait_ge(ba_sb, 2)
            dve.wait_ge(small_in, 16 * 5)
            ba3 = ba.rearrange("p (t n) -> p t n", t=TT)
            g3, b3 = (z_.rearrange("p (t n) -> p t n", t=TT) for z_ in (gg, gb2))
            steps.then(v.tensor_tensor(g3, ba3[:, :, H:2 * H], dtb.unsqueeze(1).to_broadcast([P, TT, H]), ALU.add))
            v.tensor_scalar(b3, ba3[:, :, 0:H], -1.0, None, ALU.mult).then_inc(gb_pre, 1)
            block_lo(4)
            conv(2)
            block_lo(5)
            dve.wait_ge(gb_exp, 1)
            v.tensor_scalar_add(gb2, gb2, 1.0)
            steps.then(v.scalar_tensor_tensor(gg, gg, 0.0, gb1, ALU.max, ALU.add))
            v.reciprocal(beta, gb2)
            steps.then(v.scalar_tensor_tensor(g3, g3, -1.0, nalog.unsqueeze(1).to_broadcast([P, TT, H]), ALU.mult, ALU.mult))
            v.tensor_copy(GB[:, :, :], gg.unsqueeze(2).to_broadcast([P, U, P])).then_inc(g_sb, 1)
            dve.wait_ge(rn_done, 1)
            qv, kv = (qkvT[:, 4 * i:4 * i + 4, :].rearrange("p a s -> p (a s)") for i in range(2))
            v.scalar_tensor_tensor(qv, qv, P ** -0.5, rn[:, 0:D], ALU.mult, ALU.mult)
            v.tensor_tensor(kv, kv, rn[:, D:2 * D], ALU.mult).then_inc(qk_norm, 1)
            block_lo(6)
            dve.wait_ge(gc_psum, 1)
            v.tensor_copy(gcum, bank[4][:, 0:U])
            v.tensor_copy(glast, bank[4][:, U:2 * U]).then_inc(gc_sb, 1)
            dve.wait_ge(gc_sb, 1)
            dve.wait_ge(gc_psum, 2)
            v.tensor_tensor(kdc, glast, gcum, ALU.subtract)
            for u in range(U):
                ins = v.tensor_scalar(DEC[:, u, :], quad(bank[5 + u // 4], u % 4),
                                      gcum[:, u:u + 1], 0.0, ALU.subtract, ALU.max)
            ins.then_inc(dif_sb, 1)
            dve.wait_ge(dec_exp, 1)
            dve.wait_ge(eg_done, 1)
            v.scalar_tensor_tensor(nbg, beta, -1.0, expg, ALU.mult, ALU.mult)
            dve.wait_ge(cst_in, 16)
            v.tensor_copy(tril_r[:, :], tril)
            v.tensor_copy(ones_r[:, :], ones)
            steps.then(v.tensor_tensor(DEC[:, :, :], DEC[:, :, :], tril.unsqueeze(1).to_broadcast([P, U, P]), ALU.mult))
            dve.wait_ge(kk_psum, 1)
            for u in range(U):
                ins = v.scalar_tensor_tensor(L[:, u, :], quad(kkb[u // 4], u % 4),
                                             beta[:, u:u + 1], DEC[:, u, :], ALU.mult, ALU.mult)
            ins.then_inc(lq_sb, 1)
            dve.wait_ge(kk_psum, 2)
            for t in range(TT):
                ins = v.tensor_tensor(QKT[:, 4 * t:4 * t + 4, :], quads(qkb[t]), DEC[:, 4 * t:4 * t + 4, :], ALU.mult)
            ins.then_inc(lq_sb, 1)
            mask_scores(0)
            to_lo(14)
            softplus(0)
            to_lo(15)
            ident_b = ident.unsqueeze(1).to_broadcast([P, U, P])
            exponents(0)
            dve.wait_ge(lt_sb, 1)
            steps.then(v.tensor_tensor(UT[:, :, :], LT[:, :, :], c(C_LEV).unsqueeze(1).to_broadcast([P, U, P]), ALU.mult))
            steps.then(v.tensor_tensor(UT[:, :, :], UT[:, :, :], ident_b, ALU.add))
            v.sem_inc(lev_u, 2)
            branch_b(0)
            dve.wait_ge(vk_psum, 1)
            dve.wait_ge(lev_t, 2)
            for u in range(U):
                v.tensor_scalar(VB[:, u, :], quad(bank[5 + 2 * (u // H)], u % H), beta[:, u:u + 1], None, ALU.mult)
            for h in range(H):
                ins = v.tensor_scalar(KDEC[:, h, :], quad(bank[4], h), kdc[:, h:h + 1], None, ALU.mult)
            ins.then_inc(vb_sb, 1)

            mask_scores(1)
            to_lo(16)
            to_lo(17)
            softplus(1)
            exponents(1)
            u_update(1)
            branch_b(1)
            mask_scores(2)
            u_update(2)
            to_lo(18)
            softplus(2)
            u_update(3)
            exponents(2)
            to_lo(19)
            branch_b(2)
            mask_scores(3)
            u_update(4)
            to_lo(20)
            softplus(3)
            u_update(5)
            exponents(3)
            to_lo(21)
            branch_b(3)
            to_lo(PB0)
            u_update(6)
            to_lo(PB0 + 1)

            def output_norm(t):
                hs_ = slice(t * H, (t + 1) * H)
                dve.wait_ge(osq_sb, t + 1)
                steps.then(v.tensor_reduce(ssq[:, hs_], OSQ[:, hs_, :], AX_X, ALU.add))
                v.tensor_scalar(ssq[:, hs_], ssq[:, hs_], 1.0 / P, RMS_EPS, ALU.mult, ALU.add).then_inc(rms_in, 1)

            def norm_gate(t):
                dve.wait_ge(rms_done, t + 1)
                dve.wait_ge(zg_silu, 1)
                dve.wait_ge(o_sb, t + 1)
                for u in range(t * H, (t + 1) * H):
                    ins = v.scalar_tensor_tensor(ON[:, u, :], O[:, u, :], rms[:, u:u + 1],
                                                 zg[:, u * P:(u + 1) * P], ALU.mult, ALU.mult)
                ins.then_inc(on_sb, 1)

            dve.wait_ge(o_psum, 1)
            v.tensor_copy(O[:, 0:H, :], quads(bank[5])).then_inc(o_sb, 1)
            output_norm(0)
            dve.wait_ge(vb_sb, 1)
            dve.wait_ge(ks_psum, 1)
            for h in range(H):
                ins = v.scalar_tensor_tensor(R1[:, h, :], quad(bank[6], h), nbg[:, H + h:H + h + 1],
                                             VB[:, H + h, :], ALU.mult, ALU.add)
            ins.then_inc(r1_sb, 1)
            norm_gate(0)
            to_lo(PA0)
            dve.wait_ge(o_psum, 2)
            dve.wait_ge(qs_sb, 1)
            v.tensor_tensor(O[:, H:U, :], QS[:, :, :], quads(bank[6]), ALU.add).then_inc(o_sb, 1)
            output_norm(1)

            def branch_a_lo(t):
                dve.wait_ge(oah_sb, t + 1)
                ts = slice(t * P, (t + 1) * P)
                v.scalar_tensor_tensor(oal[:, :, ts], quads(bank[5 + 2 * t]), normw, oah[:, :, ts].bitcast(F32),
                                       ALU.mult, ALU.subtract).then_inc(oal_sb, 1)

            norm_gate(1)
            branch_a_lo(0)
            branch_a_lo(1)
            to_lo(PA0 + 1)
            gp = [gates[:, 2 * q:2 * q + 2, :] for q in range(8)]

            def bank2(b):
                return bank[b].rearrange("p (a s) -> p a s", a=2)

            dve.wait_ge(gates_sb, 1)
            for pair in range(4):
                if pair < 3:
                    dve.wait_ge(pb_psum, pair + 1)
                else:
                    dve.wait_ge(halves_used, PB0 + 2)
                ins = v.tensor_tensor(gp[4 + pair], gp[4 + pair], bank2(pair), ALU.mult)
            steps.then(ins)
            dve.wait_ge(gates_sb, 2)
            to_lo(WO0)
            to_lo(WO0 + 1)
            def merged(pair):
                return msum[:, pair % 2, :].rearrange("p (a s) -> p a s", a=2)

            def merge(pair):
                if pair < 3:
                    dve.wait_ge(pa_psum, pair + 1)
                else:
                    dve.wait_ge(halves_used, PA0 + 2)
                steps.then(v.tensor_tensor(gp[pair], gp[pair], bank2(4 + pair), ALU.mult))
                v.tensor_tensor(merged(pair), gp[pair], gp[4 + pair], ALU.add).then_inc(msum_sb, 1)

            def merged_lo(pair):
                dve.wait_ge(mh_sb, pair + 1)
                ps = slice(2 * pair, 2 * pair + 2)
                v.tensor_tensor(ml[:, ps, :], merged(pair), mh[:, ps, :].bitcast(F32), ALU.subtract).then_inc(ml_sb, 1)

            merge(0)
            for pair in range(1, 4):
                merge(pair)
                merged_lo(pair - 1)
            to_lo(WO0 + 2)
            merged_lo(3)
            to_lo(WO0 + 3)

            st = stats.rearrange("p (t h s) -> p t h s", t=TT, h=2)

            def half_stats(src, t, half):
                v.bn_stats(st[:, t, half, :], src[:, half * 512:(half + 1) * 512]).then_inc(bn_sem, 1)

            def norm_stats(t, count, done):
                dve.wait_ge(bn_sem, count)
                steps.then(v.bn_aggr(mv[:, 2 * t:2 * t + 2], st[:, t, :, :].rearrange("p h s -> p (h s)")))
                v.tensor_scalar_add(rstd[:, t:t + 1], mv[:, 2 * t + 1:2 * t + 2], LN_EPS).then_inc(done, 1)

            def normalise(dst, t, ready, done):
                steps.then(v.scalar_tensor_tensor(dst, dst, mv[:, 2 * t:2 * t + 1], lnp[:, 0, :], ALU.subtract, ALU.mult))
                dve.wait_ge(ready, t + 1)
                for half in range(2):
                    hs_ = slice(half * 512, (half + 1) * 512)
                    v.scalar_tensor_tensor(dst[:, hs_], dst[:, hs_], rstd[:, t:t + 1], lnp[:, 1, hs_],
                                           ALU.mult, ALU.add).then_inc(done, 1)

            dve.wait_ge(xres_in, 16 * TT)
            dve.wait_ge(ln1_in, 32)

            def mix_norm(t):
                for half in range(2):
                    if t == 1 and half == 1:
                        to_lo(PRE)
                    if half == 0:
                        dve.wait_ge(mix_psum, t + 1)
                    elif t == 1:
                        dve.wait_ge(halves_used, PRE)
                    xs = xres[:, t, half * 512:(half + 1) * 512]
                    steps.then(v.scalar_tensor_tensor(xs, xs, ALPHA, bank[2 * t + half], ALU.mult, ALU.add))
                    half_stats(xres[:, t, :], t, half)
                norm_stats(t, 2 * t + 2, var1)
                normalise(xres[:, t, :], t, rstd1, x1_sb)

            mix_norm(0)
            mix_norm(1)
            for h in range(1, 3):
                to_lo(PRE + h)

            dve.wait_ge(lg_psum, 1)
            dve.wait_ge(late_in, 32)
            v.tensor_copy(aff, bank[6][:, 0:TT * NE])
            sel3 = selv.rearrange("p (t e) -> p t e", t=TT)
            steps.then(v.tensor_tensor(sel3, bank[6][:, 0:TT * NE].rearrange("p (t e) -> p t e", t=TT),
                                       rbias.unsqueeze(1).to_broadcast([P, TT, NE]), ALU.add))

            def rank_of_four(dst, src, n):
                s4_ = src.rearrange("p (m i) -> p m i", i=4)
                other = s4_.unsqueeze(2).to_broadcast([P, n, 4, 4])
                own = s4_.unsqueeze(3).to_broadcast([P, n, 4, 4])
                cmp = spare[:, 0:32 * n].rearrange("p (m i c j) -> p m i c j", i=4, c=2, j=4)
                v.tensor_tensor(cmp[:, :, :, 0, :], other, own, ALU.is_gt)
                steps.then(v.tensor_tensor(cmp[:, :, :, 1, :], other, own, ALU.is_equal))
                eq = cmp[:, :, :, 1, :]
                steps.then(v.tensor_tensor(eq, eq, jlt.rearrange("p (i j) -> p i j", i=4).unsqueeze(1)
                                           .to_broadcast([P, n, 4, 4]), ALU.mult))
                steps.then(v.tensor_reduce(dst, spare[:, 0:32 * n].rearrange("p (q j) -> p q j", j=8), AX_X, ALU.add))

            rank_of_four(top2, selv, 2 * NG)
            steps.then(v.scalar_tensor_tensor(selv, top2, 2.0, selv, ALU.is_lt, ALU.mult))
            steps.then(v.tensor_reduce(gscore, selv.rearrange("p (g i) -> p g i", i=EPG), AX_X, ALU.add))
            rank_of_four(gsel, gscore, TT)
            v.tensor_single_scalar(gsel, gsel, 1.0, ALU.is_lt).then_inc(gsel_sb, 1)
            dve.wait_ge(gsel_sb, 1)
            steps.then(v.tensor_single_scalar(top2, top2, 2.0, ALU.is_lt))
            t3 = top2.rearrange("p (g i) -> p g i", i=EPG)
            s5 = sel5.rearrange("p (t n) -> p t n", t=TT)
            r5 = rank5.rearrange("p (t n) -> p t n", t=TT)
            c5 = comb5.rearrange("p (t n j) -> p t n j", t=TT, n=5)
            v.tensor_copy(s5[:, :, 0:NG], gsel.rearrange("p (t g) -> p t g", t=TT))
            v.memset(s5[:, :, NG:NG + 1], 1.0)
            steps.then(v.tensor_tensor(t3, t3, gsel.unsqueeze(2).to_broadcast([P, 2 * NG, EPG]), ALU.mult))
            dve.wait_ge(rank_psum, 1)
            rk3 = rank.rearrange("p (t g) -> p t g", t=TT)
            steps.then(v.tensor_copy(r5[:, :, 0:NG], bank[5][:, 0:8].rearrange("p (t g) -> p t g", t=TT)))

            def selection(n):
                for t in range(TT):
                    ins = v.tensor_scalar(SEL[:, n, t, :], iota, rank5[:, t * 5 + n:t * 5 + n + 1],
                                          sel5[:, t * 5 + n:t * 5 + n + 1], ALU.is_equal, ALU.mult)
                return ins

            selection(0).then_inc(sel_sb, 1)
            v.tensor_copy(cnt, bank[5][:, 8:12])
            steps.then(v.tensor_tensor(rank, gsel, bank[5][:, 0:8], ALU.mult))
            v.tensor_tensor(comb, aff, top2, ALU.mult)
            steps.then(v.tensor_reduce(wsum, rk3, AX_X, ALU.add))
            steps.then(v.tensor_scalar_add(r5[:, :, NG], wsum, -128.0))
            for n in range(1, 5):
                selection(n)
            steps.then(v.tensor_reduce(wsum, comb.rearrange("p (t e) -> p t e", t=TT), AX_X, ALU.add))
            steps.then(v.reciprocal(wsum, wsum))
            for t in range(TT):
                ins = v.tensor_scalar(comb[:, t * NE:(t + 1) * NE], comb[:, t * NE:(t + 1) * NE],
                                      wsum[:, t:t + 1], None, ALU.mult)
            steps.then(ins)
            for t in range(TT):
                v.tensor_copy(c5[:, t, 0:NG, :], comb[:, t * NE:(t + 1) * NE].rearrange("p (g j) -> p g j", j=EPG))
                ins = v.tensor_reduce(c5[:, t, NG, :], comb[:, t * NE:(t + 1) * NE].rearrange("p (g j) -> p j g", j=EPG),
                                      AX_X, ALU.add)
            ins.then_inc(sel_sb, 1)

            def xg_lo(i):
                for half in range(2):
                    dve.wait_ge(xgh_sb, i * 2 + (half + 1))
                    ks = slice(4 * half, 4 * half + 4)
                    v.tensor_tensor(xgl[:, ks, :], quads(bank[7 - 7 * half]), xgh[:, ks, :].bitcast(F32),
                                    ALU.subtract).then_inc(xgl_sb, 1)

            xg_lo(0)
            steps.then(v.tensor_single_scalar(ovf, cnt, 128.0, ALU.is_gt))
            steps.then(v.tensor_reduce(cnt[:, 0:1], ovf, AX_X, ALU.add))
            v.tensor_tensor(cnt[:, 1:4], ovf[:, 1:4], iota[:, 1:4], ALU.mult)
            steps.then(v.tensor_scalar_add(small_i[:, 0:1], cnt[:, 0:1], float(NG)))
            v.tensor_scalar_add(small_i[:, 1:2], cnt[:, 0:1], float(NG - 1))
            v.memset(small_i[:, 3:4], NG - 1)
            steps.then(v.tensor_reduce(ovf[:, 0:1], cnt[:, 1:4], AX_X, ALU.add))
            v.tensor_copy(small_i[:, 4:5], ovf[:, 0:1]).then_inc(npass_sb, 1)

            to_lo(PRE + 3)
            dve.wait_ge(npass_sb, 1)
            before_last = dve.value_load(small_i[0:1, 1:2], min_val=NG - 1, max_val=NPASS_MAX - 1)
            dve.wait_ge(selt_sb, 1)
            dve.wait_ge(r2_init, 1)

            def expert_pass(i, last_pass):
                def matrix_lo(m):
                    for h in range(2):
                        to_lo(PRE + 2 * m + h, i)

                def hidden(j):
                    m = PASS_ORDER.index((j, 1))
                    dve.wait_ge(halves_used, PASS * i + (PRE + 2 * (m + 1)))
                    dve.wait_ge(silu_sb, i * 4 + (j + 1))
                    if j >= 1:
                        dve.wait_ge(ht_psum, i * 4 + j)
                    v.scalar_tensor_tensor(hid[:, :], silu_g[:, :], cgcur[:, j:j + 1],
                                           bank[2 * (j % 2) + 1], ALU.mult, ALU.mult).then_inc(hid_sb, 1)

                def hid_t(j):
                    dve.wait_ge(hth_sb, i * 4 + (j + 1))
                    v.tensor_tensor(htl[j % 2][:, :, :], quads(bank[4]), hth[j % 2][:, :, :].bitcast(F32),
                                    ALU.subtract).then_inc(htl_sb, 1)

                v.tensor_copy(cgcur, cg.rearrange("p (n j) -> p n j", j=EPG)[:, bass.ds(i, 1), :]
                              .rearrange("p n j -> p (n j)")).then_inc(cg_sb, 1)
                matrix_lo(2)
                dve.wait_ge(cg_sb, i + 1)
                hidden(0)
                matrix_lo(3)
                hid_t(0)
                matrix_lo(4)
                hidden(1)
                matrix_lo(5)
                matrix_lo(6)
                hid_t(1)
                matrix_lo(7)
                hidden(2)
                matrix_lo(8)
                matrix_lo(9)
                hid_t(2)
                matrix_lo(10)
                hidden(3)
                matrix_lo(11)
                hid_t(3)
                if not last_pass:
                    xg_lo(i + 1)
                    to_lo(PRE + PASS, i)
                for o in () if last_pass else range(2):
                    dve.wait_ge(yh_sb, i * 2 + (o + 1))
                    os_ = slice(o * 512, (o + 1) * 512)
                    v.tensor_tensor(yl[:, os_], bank[5 + o], yh[:, os_].bitcast(F32), ALU.subtract).then_inc(yl_sb, 1)
                if not last_pass:
                    to_lo(PRE + PASS + 1, i)
                    matrix_lo(13)
                for o in range(2):
                    for t in range(TT):
                        m = 2 * o + t
                        dve.wait_ge(sc_psum, i * 4 + (m + 1))
                        rs = r2[:, t, o * 512:(o + 1) * 512]
                        v.tensor_tensor(rs, rs, bank[m if last_pass else [7, 4, 5, 6][m]], ALU.add).then_inc(sc_done, 1)
                        if last_pass:
                            dve.wait_ge(sc_done, i * 4 + (m + 1))
                            half_stats(r2[:, t, :], t, o)
                            if o == 1 and t == 0:
                                norm_stats(0, 4 + 3, var2)

            with dve.Fori(0, before_last) as i:
                expert_pass(i, False)
            expert_pass(before_last, True)
            dve.wait_ge(ln2_in, 32)
            norm_stats(1, 4 + 4, var2)
            for t in range(TT):
                normalise(r2[:, t, :], t, rstd2, out_sb)


_INS = ['x', 'w_in', 'conv_w', 'dn_a_log', 'dn_dt_bias', 'dn_norm_w', 'p_a', 'p_b', 'w_out', 'ln1_g', 'ln1_b',
        'w_router', 'router_bias', 'w_gate', 'w_up', 'w_down', 'ln2_g', 'ln2_b']


def kernel(**inputs):
    import numpy as _np
    import concourse.bacc as _bacc
    from concourse.bass_utils import run_bass_kernel_spmd as _run

    nc = _bacc.Bacc("TRN2", target_bir_lowering=False, num_devices=1)
    table = constant_table()
    arrays = {"consts_dram": table}
    args = [nc.dram_tensor("consts_dram", table.shape, F32, kind="ExternalInput").ap()]
    for name in _INS:
        a = _np.ascontiguousarray(inputs[name])
        arrays[f"in_{name}_dram"] = a
        args.append(nc.dram_tensor(f"in_{name}_dram", a.shape, mybir.dt.from_np(a.dtype), kind="ExternalInput").ap())
    args.append(nc.dram_tensor("out_dram", (1, S, D), F32, kind="ExternalOutput").ap())
    hybrid_moe_block(nc, *args)
    r = _run(nc, [arrays], core_ids=[0])
    return r.results[0]["out_dram"]
```
